# Optimizing a Trainium2 kernel written in Bass

```python
import jax, jax.numpy as jnp
from jax import lax
import numpy as np

D_MODEL = 1024
BATCH = 1
SEQ = 1024
DEPTH = 1
DEC_BATCH = 8
DEC_SEQ = 1
PAST_LEN = 8192
PAGE_SIZE = 128

MIX_WIDTH = D_MODEL
A_WIDTH = 3 * MIX_WIDTH // 8
A_HEADS = 4
A_HEAD_DIM = A_WIDTH // A_HEADS
CHUNK = 128
B_WIDTH = 3 * MIX_WIDTH // 8
B_BLOCKS = 8
B_BLOCK_DIM = B_WIDTH // B_BLOCKS
CONV_WIDTH = 4
LRU_C = 8.0
C_WIDTH = MIX_WIDTH - A_WIDTH - B_WIDTH
C_HEADS = 4
C_HEAD_DIM = C_WIDTH // C_HEADS
N_MEM = 256
IN_WIDTH = 3 * A_WIDTH + 2 * B_WIDTH + 2 * C_WIDTH
EPS = 1e-6

kernel_name = "hymba_gmlp_rglru_memxattn_step"

def rmsnorm(x, g):
    xf = x.astype(jnp.float32)
    y = xf * lax.rsqrt(jnp.mean(xf * xf, axis=-1, keepdims=True) + EPS)
    return (y * g.astype(jnp.float32)).astype(x.dtype)

def chunk_spatial_gate(u, v, w_s, b_s):
    n, t, h, dh = v.shape
    t_pad = -(-t // CHUNK) * CHUNK
    if t_pad != t:
        v = jnp.pad(v, ((0, 0), (0, t_pad - t), (0, 0), (0, 0)))
    vc = v.reshape(n, t_pad // CHUNK, CHUNK, h, dh)
    mask = jnp.tril(jnp.ones((CHUNK, CHUNK), dtype=bool))
    ws = jnp.where(mask[None], w_s, jnp.zeros_like(w_s))
    mixed = jnp.einsum('hij,ncjhd->ncihd', ws, vc) + b_s.T[:, :, None]
    mixed = mixed.reshape(n, t_pad, h, dh)[:, :t]
    return u * mixed

def causal_conv(xb, buf, w, b):
    t = xb.shape[1]
    xp = jnp.concatenate([buf.astype(xb.dtype), xb], axis=1)
    out = b
    for k in range(CONV_WIDTH):
        out = out + xp[:, k:k + t] * w[k]
    return out, xp[:, -(CONV_WIDTH - 1):]

def rg_lru(xc, h0, w_a, b_a, w_x, b_x, lam):
    n, t, _ = xc.shape
    xf = xc.astype(jnp.float32)
    xblk = xf.reshape(n, t, B_BLOCKS, B_BLOCK_DIM)
    r = jax.nn.sigmoid(jnp.einsum('ntki,kij->ntkj', xblk, w_a.astype(jnp.float32)).reshape(n, t, B_WIDTH) + b_a.astype(jnp.float32))
    i = jax.nn.sigmoid(jnp.einsum('ntki,kij->ntkj', xblk, w_x.astype(jnp.float32)).reshape(n, t, B_WIDTH) + b_x.astype(jnp.float32))
    log_a = -LRU_C * r * jax.nn.softplus(-lam.astype(jnp.float32))
    a = jnp.exp(log_a)
    inp = jnp.sqrt(-jnp.expm1(2.0 * log_a)) * (i * xf)

    def step(h, elems):
        a_t, x_t = elems
        h = a_t * h + x_t
        return h, h

    h_last, hs = lax.scan(step, h0.astype(jnp.float32), (a.transpose(1, 0, 2), inp.transpose(1, 0, 2)))
    return hs.transpose(1, 0, 2).astype(xc.dtype), h_last.astype(h0.dtype)

def mem_kv(mem, g_mem, w_mk, w_mv):
    n = mem.shape[0]
    m = rmsnorm(mem, g_mem)
    k = (m @ w_mk).reshape(n, N_MEM, C_HEADS, C_HEAD_DIM)
    v = (m @ w_mv).reshape(n, N_MEM, C_HEADS, C_HEAD_DIM)
    return k, v

def cross_attend(q, k, v):
    n, t, _ = q.shape
    q = q.reshape(n, t, C_HEADS, C_HEAD_DIM)
    s = jnp.einsum('nthd,nshd->nhts', q, k.astype(q.dtype)).astype(jnp.float32) * (C_HEAD_DIM ** -0.5)
    p = jax.nn.softmax(s, axis=-1).astype(q.dtype)
    o = jnp.einsum('nhts,nshd->nthd', p, v.astype(q.dtype))
    return o.reshape(n, t, C_WIDTH)

def mixer_layer(x, mk, mv, conv_buf, h0, g_pre, g_post, w_in, w_out, g_v, w_s, b_s,
                w_conv, b_conv, w_a, b_a, w_x, b_x, lam):
    n, t, _ = x.shape
    h = rmsnorm(x, g_pre)
    z = h @ w_in
    cuts = [A_WIDTH, 2 * A_WIDTH, 3 * A_WIDTH, 3 * A_WIDTH + B_WIDTH,
            3 * A_WIDTH + 2 * B_WIDTH, 3 * A_WIDTH + 2 * B_WIDTH + C_WIDTH]
    u, v, ga, xb, gb, q, gc = jnp.split(z, cuts, axis=-1)
    vn = rmsnorm(v.reshape(n, t, A_HEADS, A_HEAD_DIM), g_v.reshape(A_HEADS, A_HEAD_DIM))
    out_a = chunk_spatial_gate(u.reshape(n, t, A_HEADS, A_HEAD_DIM), vn, w_s, b_s).reshape(n, t, A_WIDTH)
    out_a = out_a * jax.nn.silu(ga)
    xc, new_buf = causal_conv(xb, conv_buf, w_conv, b_conv)
    hs, h_last = rg_lru(xc, h0, w_a, b_a, w_x, b_x, lam)
    out_b = hs * jax.nn.silu(gb)
    out_c = cross_attend(q, mk, mv) * jax.nn.silu(gc)
    o = jnp.concatenate([out_a, out_b, out_c], axis=-1) @ w_out
    y = x + rmsnorm(o, g_post)
    return y, vn.reshape(n, t, A_WIDTH), new_buf, h_last

def setup_inputs(seed: int = 0) -> dict:
    key = jax.random.key(seed)
    ks = jax.random.split(key, 32)
    f32 = jnp.float32
    nrm = lambda k, s, sc: jax.random.normal(k, s, f32) * sc
    a_init = jax.random.uniform(ks[20], (DEPTH, B_WIDTH), f32, 0.9, 0.999)
    return {
        "x_prompt": nrm(ks[0], (BATCH, SEQ, D_MODEL), 1.0),
        "x_sample": nrm(ks[1], (DEC_BATCH, DEC_SEQ, D_MODEL), 1.0),
        "mem_prompt": nrm(ks[2], (BATCH, N_MEM, D_MODEL), 1.0),
        "cache_mem_k": nrm(ks[3], (DEPTH, DEC_BATCH, N_MEM, C_HEADS, C_HEAD_DIM), 1.0),
        "cache_mem_v": nrm(ks[4], (DEPTH, DEC_BATCH, N_MEM, C_HEADS, C_HEAD_DIM), 1.0),
        "state_conv": nrm(ks[5], (DEPTH, DEC_BATCH, CONV_WIDTH - 1, B_WIDTH), 1.0),
        "state_h": nrm(ks[6], (DEPTH, DEC_BATCH, B_WIDTH), 0.5),
        "g_pre": 1.0 + nrm(ks[7], (DEPTH, D_MODEL), 0.02),
        "g_post": 1.0 + nrm(ks[8], (DEPTH, D_MODEL), 0.02),
        "w_in": nrm(ks[9], (DEPTH, D_MODEL, IN_WIDTH), D_MODEL ** -0.5),
        "w_out": nrm(ks[10], (DEPTH, MIX_WIDTH, D_MODEL), MIX_WIDTH ** -0.5),
        "g_v": 1.0 + nrm(ks[11], (DEPTH, A_WIDTH), 0.02),
        "w_s": nrm(ks[12], (DEPTH, A_HEADS, CHUNK, CHUNK), CHUNK ** -0.5),
        "b_s": 1.0 + nrm(ks[13], (DEPTH, A_HEADS, CHUNK), 0.02),
        "w_conv": nrm(ks[14], (DEPTH, CONV_WIDTH, B_WIDTH), CONV_WIDTH ** -0.5),
        "b_conv": nrm(ks[15], (DEPTH, B_WIDTH), 0.01),
        "w_a": nrm(ks[16], (DEPTH, B_BLOCKS, B_BLOCK_DIM, B_BLOCK_DIM), B_BLOCK_DIM ** -0.5),
        "b_a": nrm(ks[17], (DEPTH, B_WIDTH), 0.01),
        "w_x": nrm(ks[18], (DEPTH, B_BLOCKS, B_BLOCK_DIM, B_BLOCK_DIM), B_BLOCK_DIM ** -0.5),
        "b_x": nrm(ks[19], (DEPTH, B_WIDTH), 0.01),
        "lru_lambda": jnp.log(a_init) - jnp.log1p(-a_init),
        "g_mem": 1.0 + nrm(ks[21], (DEPTH, D_MODEL), 0.02),
        "w_mk": nrm(ks[22], (DEPTH, D_MODEL, C_WIDTH), D_MODEL ** -0.5),
        "w_mv": nrm(ks[23], (DEPTH, D_MODEL, C_WIDTH), D_MODEL ** -0.5),
    }

def reference(x_prompt, x_sample, mem_prompt, cache_mem_k, cache_mem_v, state_conv, state_h,
              g_pre, g_post, w_in, w_out, g_v, w_s, b_s, w_conv, b_conv, w_a, b_a, w_x, b_x,
              lru_lambda, g_mem, w_mk, w_mv):
    xp, xs = x_prompt, x_sample
    zero_buf = jnp.zeros((x_prompt.shape[0], CONV_WIDTH - 1, B_WIDTH), x_prompt.dtype)
    zero_h = jnp.zeros((x_prompt.shape[0], B_WIDTH), x_prompt.dtype)
    mk_p_all, mv_p_all, conv_p_all, h_p_all = [], [], [], []
    conv_s_all, h_s_all, v_s_all = [], [], []
    for l in range(DEPTH):
        lp = (g_pre[l], g_post[l], w_in[l], w_out[l], g_v[l], w_s[l], b_s[l], w_conv[l], b_conv[l],
              w_a[l], b_a[l], w_x[l], b_x[l], lru_lambda[l])
        mk_p, mv_p = mem_kv(mem_prompt, g_mem[l], w_mk[l], w_mv[l])
        xp, _, conv_p, h_p = mixer_layer(xp, mk_p, mv_p, zero_buf, zero_h, *lp)
        xs, v_s, conv_s, h_s = mixer_layer(xs, cache_mem_k[l], cache_mem_v[l], state_conv[l], state_h[l], *lp)
        mk_p_all.append(mk_p); mv_p_all.append(mv_p); conv_p_all.append(conv_p); h_p_all.append(h_p)
        conv_s_all.append(conv_s); h_s_all.append(h_s); v_s_all.append(v_s)
    return (xp, xs, jnp.stack(mk_p_all), jnp.stack(mv_p_all), jnp.stack(conv_p_all), jnp.stack(h_p_all),
            jnp.stack(conv_s_all), jnp.stack(h_s_all), jnp.stack(v_s_all))


_drawn_inputs = setup_inputs


def setup_inputs(seed=0):
    import zlib

    import numpy as np

    out = dict(_drawn_inputs(seed))
    spreads = {}
    factors = {'g_post': 38.735,
     'g_v': 25.641,
     'b_s': 45.084,
     'b_a': 22.797,
     'b_x': 8.0,
     'g_mem': 20.508,
     'cache_mem_k': 3.904,
     'cache_mem_v': 3.118}
    for name, (base, spread) in spreads.items():
        noise = np.random.default_rng([zlib.crc32(name.encode()), seed]).standard_normal(out[name].shape)
        drawn = base * np.exp(spread * noise) if base else spread * noise
        out[name] = __import__('jax').numpy.asarray(drawn.astype(out[name].dtype))
    for name, factor in factors.items():
        out[name] = (out[name] * factor).astype(out[name].dtype)
    return out
```

```python
from contextlib import ExitStack

import numpy as np
import concourse.bass as bass
from concourse import mybir

F = mybir.dt.float32
R = mybir.dt.float32r
ALU = mybir.AluOpType
ACT = mybir.ActivationFunctionType
AX = mybir.AxisListType

P = 128
DM = 1024
NT, NS = 1024, 8
TT = NT + NS
KT = DM // P
NG = 3
GN = TT // NG
NCH = NT // P
LASTC = TT - P
EPS = 1e-6
NM, MT = 256, 2
NH, HD = 4, 64
AH, AD = 4, 96
AW = AH * AD
LRU_C = 8.0
T_Q, T_GC, T_XB, T_V, T_GA, T_GB, T_U, N_TILES = 0, 2, 4, 7, 10, 13, 16, 19
ATT0 = 4
PAR = {}
_at = 0
for _name, _n in (("g_pre", 8), ("g_mem", 8), ("w_conv", 12), ("b_conv", 3), ("b_a", 3), ("b_x", 3),
                  ("lam", 3), ("st_conv", 72), ("st_h", 24), ("b_s", 4)):
    PAR[_name] = _at
    _at += _n
N_PAR = _at
GATE_PAIRS = [(0, 0), (1, 0), (0, 1), (1, 1), (2, 1), (1, 2), (2, 2)]


class Tally:

    def __init__(self, eng, sem):
        self.eng, self.sem, self.base, self.k = eng, sem, 0, 0

    def mark(self, ins):
        ins.then_inc(self.sem, 1)
        self.k += 1

    def wait(self):
        self.eng.wait_ge(self.sem, self.base + self.k)

    def link(self, ins):
        self.mark(ins)
        self.wait()


def build(nc, d):
    with ExitStack() as ctx:
        def sb(name, shape, dt=F):
            return ctx.enter_context(nc.sbuf_tensor(name, shape, dt))

        def sem(name):
            return ctx.enter_context(nc.semaphore(name))

        x_hi, x_lo = sb("x_hi", [P, KT, TT], R), sb("x_lo", [P, KT, TT], R)
        w_stage = sb("w_stage", [P, 2, DM])
        w_hi, w_lo = sb("w_hi", [P, 2, DM], R), sb("w_lo", [P, 2, DM], R)
        mixT = sb("mixT", [P, KT, TT])
        zT = sb("zT", [P, 11, TT])
        rstdB = sb("rstdB", [P, TT])
        probs, probsT = sb("probs", [P, TT]), sb("probsT", [P, TT])
        kv = sb("kv", [P, MT, 512])
        kT = sb("kT", [P, 2, NM])
        x_ring = sb("x_ring", [P, 2, TT])
        rows = sb("rows", [P, AW + 8])
        gate_w = sb("gate_w", [P, 2, len(GATE_PAIRS), P])
        wsT = sb("wsT", [P, AH, P])
        ident, ones = sb("ident", [P, P]), sb("ones", [P, P])
        q_chunk = sb("q_chunk", [P, 2, 2, P])
        attn = sb("attn", [P, NM])
        par = sb("par", [P, N_PAR])
        ssq, rstd = sb("ssq", [P, 11]), sb("rstd", [P, 11])
        ssv, rstdv = sb("ssv", [P, 36]), sb("rstdv", [P, 36])
        mx, negm = sb("mx", [P, 4]), sb("negm", [P, 4])
        sums, rsum = sb("sums", [P, 4]), sb("rsum", [P, 4])
        nba, nsp, lt = sb("nba", [P, 3]), sb("nsp", [P, 3]), sb("lt", [P, 6, 3])
        qb = sb("qb", [P, 2, NS, NH])
        sy, ry = sb("sy", [P, 2]), sb("ry", [P, 2])
        sst = sb("sst", [32, 4])
        h_last = sb("h_last", [P, 3, NS + 1])
        ps = ctx.enter_context(nc.psum_tensor("ps", [P, 8, 512], F))

        zf = zT[:, :, :].rearrange("p a b -> p (a b)")
        memT = zf[:, 2 * TT:2 * TT + KT * NM].rearrange("p (k m) -> p k m", k=KT)
        w_mem = zf[:, 4 * TT:4 * TT + KT * 512].rearrange("p (k m) -> p k m", k=KT)
        mem_nat = zf[:, 8 * TT:8 * TT + MT * DM].rearrange("p (k m) -> p k m", k=MT)
        v_tok = zf[:, TT:TT + 9 * AW].rearrange("p (c n) -> p c n", c=9)
        v_sq = x_ring[:, :, :].rearrange("p a b -> p (a b)")[:, 0:4 * AW].rearrange("p (c n) -> p c n", c=4)
        cache_ring = zf[:, 5 * TT:5 * TT + 6 * 512].rearrange("p (c n) -> p c n", c=6)
        wo_early = zf[:, TT:TT + 4 * DM].rearrange("p (c n) -> p c n", c=4)
        y_out = zf[:, 5 * TT:5 * TT + 2 * DM].rearrange("p (c n) -> p c n", c=2)
        g_post = zf[:, 7 * TT:7 * TT + DM]
        s_r, s_i, s_th = zT[:, 0, :], probs[:, :], probsT[:, :]
        s_a2, s_sig = x_ring[:, 0, :], x_ring[:, 1, :]
        sT_s = kT[:, 0, 0:64]
        p_s = kv[0:32, 0, 0:NM]
        pT_s = kT[:, 1, 0:64].rearrange("p (m n) -> p m n", m=2)
        o_hi, o_lo = w_hi, w_lo
        wo_hi, wo_lo = x_hi, x_lo

        def wo_source(k):
            if k < 2 or k >= 6:
                return w_stage[:, k % 2, :], wo_in[k % 2], 16 if k < 2 else 32
            return wo_early[:, k - 2, :], wo_in[k], 16

        def pc(name, i=0, n=1):
            return par[:, PAR[name] + i:PAR[name] + i + n]

        par_in, rows_in, gatew_in, wsT_in, memT_in, memn_in = map(sem, (
            "par_in", "rows_in", "gatew_in", "wsT_in", "memT_in", "memn_in"))
        wm_in = [sem(f"wm_in{i}") for i in range(4)]
        xT_in = [sem(f"xT_in{k}") for k in range(KT)]
        w_in = [sem(f"w_in{i}") for i in range(2)]
        x_in = [sem(f"x_in{i}") for i in range(2)]
        c_in = [sem(f"cache_in{i}") for i in range(6)]
        wo_in = [sem(f"wo_in{i}") for i in range(6)]
        gpost_in = sem("gpost_in")
        y_stored = [sem(f"y_stored{i}") for i in range(2)]
        kv_stored, conv_stored, h_stored, vs_stored = map(sem, (
            "kv_stored", "conv_stored", "h_stored", "vs_stored"))
        const_set, w_masked, wlo_done, qc_done, xsq_done, whi_done, xhi_done = map(sem, (
            "const_set", "w_masked", "wlo_done", "qc_done", "xsq_done", "whi_done", "xhi_done"))
        xlo_done, memg_done, ms_done, root_done, diag_done, rstdB_done = map(sem, (
            "xlo_done", "memg_done", "ms_done", "root_done", "diag_done", "rstdB_done"))
        kvp_done, kv_done, kTp_done, kT_done = map(sem, ("kvp_done", "kv_done", "kTp_done", "kT_done"))
        z_done, z_used, rstdp_done = map(sem, ("z_done", "z_used", "rstdp_done"))
        gcsig_done, gc_done = map(sem, ("gcsig_done", "gc_done"))
        sc_done, negm_done, p_done, pTp_done, pTa_done, pTb_done = map(sem, (
            "sc_done", "negm_done", "p_done", "pTp_done", "pTa_done", "pTb_done"))
        pv_done, attn_done, attnT_done, c_done = map(sem, ("pv_done", "attn_done", "attnT_done", "c_done"))
        lam_done, elam_done, nsp_done, conv_done = map(sem, ("lam_done", "elam_done", "nsp_done", "conv_done"))
        gate_done, gate_used, vt_done, vt_used = map(sem, ("gate_done", "gate_used", "vt_done", "vt_used"))
        ixc_done, gbm_done = sem("ixc_done"), sem("gbm_done")
        vsq_done, vsum_done, vroot_done, vms_done, vr_done, vn_done = map(sem, (
            "vsq_done", "vsum_done", "vroot_done", "vms_done", "vr_done", "vn_done"))
        gasig_done, ga_done, gar_done = map(sem, ("gasig_done", "ga_done", "gar_done"))
        sp_done, mix_done, mT_done, a_done = map(sem, ("sp_done", "mix_done", "mT_done", "a_done"))
        decay_done, rest_done, root_b_done, scan_done, placed = map(sem, (
            "decay_done", "rest_done", "root_b_done", "scan_done", "placed"))
        gbsig_done, b_done = map(sem, ("gbsig_done", "b_done"))
        qb_done, s1c_done, s2_done, snegm_done, sp_exp, sp_norm, s3_done, s3c_done, cs_done = map(sem, (
            "qb_done", "s1c_done", "s2_done", "snegm_done", "sp_exp", "sp_norm", "s3_done",
            "s3c_done", "cs_done"))
        kc_read, vc_read = sem("kc_read"), sem("vc_read")
        wohi_done, wo_done, ohi_done, o_done = map(sem, ("wohi_done", "wo_done", "ohi_done", "o_done"))
        y_done, ysq_done, yms_done, yroot_done, y_used, y_ready = map(sem, (
            "y_done", "ysq_done", "yms_done", "yroot_done", "y_used", "y_ready"))
        dve_own, pool_own, act_own = sem("dve_own"), sem("pool_own"), sem("act_own")

        block = ctx.enter_context(nc.Block())

        @block.sync
        def _(sp):
            def load_w(m, slot):
                sp.dma_start(w_stage[:, slot, :], d["w_tiles"][m]).then_inc(w_in[slot], 16)

            def load_cache(src, n, kind):
                u = 3 * kind + n % 3
                if n >= 3:
                    sp.wait_ge((kc_read, vc_read)[kind], n - 2)
                sp.dma_start(cache_ring[:, u, :], src[n]).then_inc(c_in[u], 16)

            sp.dma_start(par[:, :], d["par"]).then_inc(par_in, 16)
            sp.dma_start(memT, d["memT"]).then_inc(memT_in, 16)
            for i in range(4):
                sp.dma_start(w_mem[:, 2 * i:2 * i + 2, :], d["w_mem"][:, 2 * i:2 * i + 2, :]).then_inc(wm_in[i], 16)
            load_w(0, 0)
            for k in range(KT):
                sp.dma_start(mixT[:, k, :], d["xT"][:, k, :]).then_inc(xT_in[k], 16)
            sp.dma_start(mem_nat, d["mem_nat"]).then_inc(memn_in, 16)
            load_w(1, 1)
            for c in range(9):
                if c >= 2:
                    sp.wait_ge(xsq_done, c - 1)
                sp.dma_start(x_ring[:, c % 2, 0:DM],
                             d["x_all"][min(c * P, LASTC):min(c * P, LASTC) + P, :]).then_inc(x_in[c % 2], 16)
            sp.dma_start(rows[:, :], d["rows"].partition_broadcast(P)).then_inc(rows_in, 16)
            sp.dma_start(wsT[:, :, :], d["wsT"]).then_inc(wsT_in, 16)
            sp.dma_start(gate_w[:, :, :, :], d["gate_w"]).then_inc(gatew_in, 16)
            for m in (2, 3):
                sp.wait_ge(wlo_done, m - 1)
                load_w(m, m % 2)
            with sp.Fori(0, 4) as i:
                for u in range(2):
                    sp.wait_ge(wlo_done, i * 2 + (3 + u))
                    load_w(i * 2 + (4 + u), u)
            sp.wait_ge(kv_done, 2)
            sp.dma_start(d["o_kv"], kv[:, :, :]).then_inc(kv_stored, 16)
            for j in range(3):
                sp.wait_ge(z_used, 3 * (T_XB + j + 1))
                sp.dma_start(d["o_conv"][:, j, :], zT[:, 2 + j, NT - 3:TT]).then_inc(conv_stored, 16)
            sp.dma_start(d["o_st"], pc("st_conv", 0, 72)).then_inc(h_stored, 16)
            for m in (12, 13, 14):
                sp.wait_ge(wlo_done, m - 1)
                load_w(m, m % 2)
            sp.wait_ge(vt_done, 9)
            for n in range(3):
                load_cache(d["kcT"], n, 0)
                load_cache(d["vc"], n, 1)
            sp.wait_ge(vn_done, 3)
            sp.dma_start(d["o_vs"], v_tok[P - NS:P, 8, :]).then_inc(vs_stored, 16)
            for m in (15, 16):
                sp.wait_ge(wlo_done, m - 1)
                load_w(m, m % 2)
            for m in (17, 18):
                sp.wait_ge(wlo_done, m - 1)
                load_w(m, m % 2)
            for n in range(3, NS):
                load_cache(d["kcT"], n, 0)
            sp.wait_ge(mT_done, 9)
            sp.wait_ge(a_done, 9)
            for k in range(2, 6):
                sp.dma_start(wo_early[:, k - 2, :], d["w_out"][k]).then_inc(wo_in[k], 16)
            for k in range(2):
                sp.wait_ge(wlo_done, N_TILES - k)
                sp.dma_start(w_stage[:, k, :], d["w_out"][k]).then_inc(wo_in[k], 16)
            for n in range(3, NS):
                load_cache(d["vc"], n, 1)
            sp.wait_ge(placed, 6)
            sp.dma_start(d["o_h"], h_last[:, :, :]).then_inc(h_stored, 16)
            sp.wait_ge(vc_read, NS)
            sp.dma_start(g_post, d["g_post"].partition_broadcast(P)).then_inc(gpost_in, 16)
            for k in range(2):
                sp.wait_ge(wo_done, k + 1)
                sp.dma_start(w_stage[:, k, :], d["w_out"][6 + k]).then_inc(wo_in[k], 16)

            def load_x(c0, slot):
                sp.dma_start(x_ring[:, slot, 0:DM], d["x_all"][bass.ds(c0, P), :]).then_inc(x_in[slot], 16)

            sp.wait_ge(b_done, 3)
            load_x(0, 0)
            load_x(P, 1)
            with sp.Fori(0, 3) as i:
                for u in range(2):
                    sp.wait_ge(y_ready, i * 2 + (u + 1))
                    sp.dma_start(d["o_y"][bass.ds(i * (2 * P) + u * P, P), :], y_out[:, u, :]).then_inc(y_stored[u], 16)
                    load_x(i * (2 * P) + (2 + u) * P, u)
            for c in (6, 7, 8):
                sp.wait_ge(y_ready, c + 1)
                if c < 8:
                    sp.dma_start(d["o_y"][c * P:(c + 1) * P, :], y_out[:, c % 2, :]).then_inc(y_stored[c % 2], 16)
                else:
                    sp.dma_start(d["o_y"][NT:TT, :], y_out[P - NS:P, 0, :]).then_inc(y_stored[0], 16)
                if c == 6:
                    load_x(LASTC, 0)
            sp.wait_ge(y_stored[0], 16 * 5)
            sp.wait_ge(y_stored[1], 16 * 4)
            sp.wait_ge(kv_stored, 16)
            sp.wait_ge(conv_stored, 48)
            sp.wait_ge(h_stored, 32)
            sp.wait_ge(vs_stored, 16)

        @block.tensor
        def _(pe):
            def gemm(m, g, slot, first=False):
                if g == 0:
                    pe.wait_ge(wlo_done, m + 1)
                if not first:
                    pe.wait_ge(z_used, m * 3 + (g - 2))
                cols = slice(g * GN, (g + 1) * GN)
                for k in range(KT):
                    if first and g == 0:
                        pe.wait_ge(xlo_done, k + 1)
                    wk = slice(k * P, (k + 1) * P)
                    for n, (w, x) in enumerate(((w_hi, x_hi), (w_hi, x_lo), (w_lo, x_hi))):
                        last = pe.matmul(ps[:, g, 0:GN], w[:, slot, wk], x[:, k, cols],
                                         start=(k == 0 and n == 0), stop=(k == KT - 1 and n == 2))
                last.then_inc(z_done, 1)

            for k in range(KT):
                pe.wait_ge(memg_done, k // 4 + 1)
                pe.wait_ge(wm_in[k // 2], 16)
                for mt in range(MT):
                    last = pe.matmul(ps[:, 3 + mt, :], memT[:, k, mt * P:(mt + 1) * P], w_mem[:, k, :],
                                     start=(k == 0), stop=(k == KT - 1))
            last.then_inc(kvp_done, 1)
            for g in range(NG):
                gemm(0, g, 0, first=True)
            pe.wait_ge(diag_done, 2)
            pe.wait_ge(const_set, 2)
            for c in range(NCH):
                last = pe.matmul(ps[:, 5 + c // 4, (c % 4) * P:(c % 4 + 1) * P], ones[:, :],
                                 probs[:, c * P:(c + 1) * P], start=True, stop=True)
            last.then_inc(rstdp_done, 1)
            pe.matmul(ps[:, 7, 0:NS], ones[:, :], probs[:, NT:TT], start=True, stop=True).then_inc(rstdp_done, 1)
            gemm(1, 0, 1)
            pe.wait_ge(kv_done, 2)
            pe.wait_ge(rstdB_done, 3)
            for t in range(2):
                for mt in range(MT):
                    last = pe.transpose(ps[:, 5, t * NM + mt * P:t * NM + (mt + 1) * P],
                                        kv[:, mt, t * P:(t + 1) * P], ident[:, :])
            last.then_inc(kTp_done, 1)
            gemm(1, 1, 1)
            gemm(1, 2, 1)
            for m in (2, 3):
                for g in range(NG):
                    gemm(m, g, m % 2)

            pe.wait_ge(kT_done, 1)
            with pe.Fori(0, 4) as i:
                for u in range(2):
                    m, s = i * 2 + (ATT0 + u), i * 2 + u
                    pe.wait_ge(qc_done, s + 1)
                    for t in range(2):
                        for hh in range(2):
                            rows_h = slice(hh * HD, (hh + 1) * HD)
                            last = pe.matmul(ps[:, 3 + hh, t * NM:(t + 1) * NM], q_chunk[rows_h, u, t, :],
                                             kT[rows_h, t, :], start=True, stop=True)
                            if t == 1:
                                last.then_inc(sc_done, 1)
                    gemm(m, 0, u)
                    for b in range(2):
                        pe.wait_ge(p_done, s * 4 + (2 + 2 * b))
                        for n in range(4):
                            last = pe.transpose(ps[:, 5 + b, n * P:(n + 1) * P],
                                                probs[:, (4 * b + n) * P:(4 * b + n + 1) * P], ident[:, :])
                        last.then_inc(pTp_done, 1)
                    gemm(m, 1, u)
                    pe.wait_ge(pTa_done, s + 1)
                    pe.wait_ge(pTb_done, s + 1)
                    for h in range(NH):
                        for mt in range(MT):
                            n = 2 * h + mt
                            last = pe.matmul(ps[:, 7, h * HD:(h + 1) * HD], probsT[:, n * P:(n + 1) * P],
                                             kv[:, mt, 256 + h * HD:256 + (h + 1) * HD],
                                             start=(mt == 0), stop=(mt == 1))
                    last.then_inc(pv_done, 1)
                    gemm(m, 2, u)
                    pe.wait_ge(attn_done, s + 1)
                    for t in range(2):
                        last = pe.transpose(ps[:, 7, 256 + t * P:256 + (t + 1) * P],
                                            attn[:, t * P:(t + 1) * P], ident[:, :])
                    last.then_inc(attnT_done, 1)

            def gates(j, g):
                for gate in range(2):
                    n = (j * 3 + g) * 2 + gate
                    if n >= 3:
                        pe.wait_ge(gate_used, n - 2)
                    pairs = [(x, kin) for x, (kin, out) in enumerate(GATE_PAIRS) if out == j]
                    for x, kin in pairs:
                        last = pe.matmul(ps[:, 3 + n % 3, 0:GN], gate_w[:, gate, x, :],
                                         mixT[:, 3 + kin, g * GN:(g + 1) * GN],
                                         start=(x == pairs[0][0]), stop=(x == pairs[-1][0]))
                    last.then_inc(gate_done, 1)

            def col0(c):
                return min(c * P, LASTC)

            pe.wait_ge(conv_done, 3)
            pe.wait_ge(gatew_in, 16)
            pe.wait_ge(p_done, 32)
            pe.wait_ge(pTa_done, 8)
            pe.wait_ge(pTb_done, 8)
            pe.wait_ge(c_done, 8)
            for g in range(NG):
                gemm(12, g, 0)
                gates(0, g)
                for c in range(3 * g, 3 * g + 3):
                    if c >= 2:
                        pe.wait_ge(vt_used, c - 1)
                    for j in range(3):
                        last = pe.transpose(ps[:, 6 + c % 2, j * P:(j + 1) * P],
                                            zT[:, 5 + j, col0(c):col0(c) + P], ident[:, :])
                    last.then_inc(vt_done, 1)
            for g in range(NG):
                gemm(13, g, 1)
            pe.wait_ge(w_masked, 1)
            for g in range(NG):
                gemm(14, g, 0)
                gates(1, g)
                for c in range(3 * g, 3 * g + 3):
                    if c < NCH:
                        pe.wait_ge(vn_done, c // 4 + 1)
                        pe.wait_ge(vt_used if c < 2 else mix_done, 9 if c < 2 else c - 1)
                        for h in range(AH):
                            last = pe.matmul(ps[:, 6 + c % 2, h * AD:(h + 1) * AD], wsT[:, h, :],
                                             v_tok[:, c, h * AD:(h + 1) * AD], start=True, stop=True)
                        last.then_inc(sp_done, 1)
            for g in range(NG):
                gemm(15, g, 1)
                for c in range(3 * g, 3 * g + 3):
                    pe.wait_ge(mix_done, 9)
                    if c >= 2:
                        pe.wait_ge(a_done, c - 1)
                    for j in range(3):
                        last = pe.transpose(ps[:, 6 + c % 2, j * P:(j + 1) * P],
                                            v_tok[:, c, j * P:(j + 1) * P], ident[:, :])
                    last.then_inc(mT_done, 1)
            for g in range(NG):
                gemm(16, g, 0)
                gates(2, g)
            pe.wait_ge(a_done, 9)
            pe.wait_ge(qb_done, 4)
            for n in range(NS):
                pe.wait_ge(c_in[n % 3], 16 * (n // 3 + 1))
                for mt in range(MT):
                    for t in range(2):
                        last = pe.matmul(ps[:, 6, mt * 32 + n * NH:mt * 32 + (n + 1) * NH],
                                         cache_ring[:, n % 3, t * NM + mt * P:t * NM + (mt + 1) * P],
                                         qb[:, t, n, :], start=(t == 0), stop=(t == 1))
                last.then_inc(kc_read, 1)
            gemm(17, 0, 1)
            pe.wait_ge(s1c_done, 1)
            for mt in range(MT):
                last = pe.matmul(ps[0:32, 7, mt * P:(mt + 1) * P], sT_s[:, mt * 32:(mt + 1) * 32],
                                 ident[:, :], start=True, stop=True)
            last.then_inc(s2_done, 1)
            gemm(17, 1, 1)
            gemm(17, 2, 1)
            gemm(18, 0, 0)
            pe.wait_ge(sp_norm, 1)
            for mt in range(MT):
                last = pe.matmul(ps[:, 6, mt * 32:(mt + 1) * 32], p_s[:, mt * P:(mt + 1) * P],
                                 ident[0:32, 0:32], start=True, stop=True)
            last.then_inc(s3_done, 1)
            gemm(18, 1, 0)
            gemm(18, 2, 0)
            pe.wait_ge(s3c_done, 1)
            for n in range(NS):
                pe.wait_ge(c_in[3 + n % 3], 16 * (n // 3 + 1))
                for t in range(2):
                    at = (t * NS + n) * NH
                    for mt in range(MT):
                        last = pe.matmul(ps[:, 7, at:at + NH],
                                         cache_ring[:, 3 + n % 3, mt * NM + t * P:mt * NM + (t + 1) * P],
                                         pT_s[:, mt, n * NH:(n + 1) * NH], start=(mt == 0), stop=(mt == 1))
                last.then_inc(vc_read, 1)

            def project(c, u, first=False):
                pe.wait_ge(o_done, c + 1)
                for k in range(KT):
                    if first:
                        pe.wait_ge(wo_done, k + 1)
                    ok = slice(k * P, (k + 1) * P)
                    for n in range(2):
                        cols = slice(n * 512, (n + 1) * 512)
                        for part, (o, w) in enumerate(((o_hi, wo_hi), (o_hi, wo_lo), (o_lo, wo_hi))):
                            last = pe.matmul(ps[:, 2 * u + n, :], o[:, u, ok], w[:, k, cols],
                                             start=(k == 0 and part == 0), stop=(k == KT - 1 and part == 2))
                last.then_inc(y_done, 1)

            pe.wait_ge(z_used, 3 * N_TILES)
            pe.wait_ge(gate_used, 18)
            project(0, 0, first=True)
            project(1, 1)
            with pe.Fori(0, 3) as i:
                for u in range(2):
                    pe.wait_ge(y_used, i * 2 + (u + 1))
                    project(i * 2 + (u + 2), u)
            pe.wait_ge(y_used, 7)
            project(8, 0)

        @block.scalar
        def _(act):
            own = Tally(act, act_own)

            def split_w(m, slot, arrived):
                act.wait_ge(w_in[slot], arrived)
                if not isinstance(m, int) or m >= 2:
                    act.wait_ge(z_done, m * 3 + (-3))
                act.activation(w_hi[:, slot, :], w_stage[:, slot, :], ACT.Copy).then_inc(whi_done, 1)

            def split_tile(m):
                split_w(m, m % 2, 16 * (m // 2 + 1))

            split_tile(0)
            act.wait_ge(par_in, 16)
            for k in range(KT):
                act.wait_ge(xT_in[k], 16)
                act.activation(x_hi[:, k, :], mixT[:, k, :], ACT.Copy, scale=pc("g_pre", k)).then_inc(xhi_done, 1)
            split_tile(1)
            act.wait_ge(memn_in, 16)
            for mt in range(MT):
                own.link(act.activation(probsT[:, 0:DM], mem_nat[:, mt, :], ACT.Square, accum_out=ssq[:, 9 + mt:10 + mt]))
            for c in range(9):
                act.wait_ge(x_in[c % 2], 16 * (c // 2 + 1))
                if c:
                    act.wait_ge(xsq_done, c)
                act.activation(probsT[:, 0:DM], x_ring[:, c % 2, 0:DM], ACT.Square,
                               accum_out=ssq[:, c:c + 1]).then_inc(xsq_done, 1)
            act.wait_ge(lam_done, 1)
            act.activation(lt[:, 1, :], lt[:, 0, :], ACT.Exp, scale=-1.0).then_inc(elam_done, 1)
            act.wait_ge(ms_done, 1)
            act.activation(rstd[:, :], ssq[:, :], ACT.Sqrt).then_inc(root_done, 1)
            act.wait_ge(kvp_done, 1)
            act.wait_ge(diag_done, 1)
            for mt in range(MT):
                act.activation(kv[:, mt, :], ps[:, 3 + mt, :], ACT.Copy, scale=rstd[:, 9 + mt:10 + mt]).then_inc(kv_done, 1)
            for b, n in ((0, 512), (1, 512), (2, NS)):
                act.wait_ge(rstdp_done, 1 + b // 2)
                act.activation(rstdB[:, b * 512:b * 512 + n], ps[:, 5 + b, 0:n], ACT.Copy).then_inc(rstdB_done, 1)
            split_tile(2)
            act.wait_ge(kTp_done, 1)
            act.activation(kT[:, :, :].rearrange("p a b -> p (a b)"), ps[:, 5, :], ACT.Copy).then_inc(kT_done, 1)
            split_tile(3)
            split_tile(4)
            for j, sig in enumerate((probs, probsT)):
                act.wait_ge(z_used, 3 * (T_GC + j + 1))
                act.activation(sig[:, :], mixT[:, 6 + j, :], ACT.Sigmoid).then_inc(gcsig_done, 1)
            act.wait_ge(gc_done, 2)

            with act.Fori(0, 4) as i:
                for u in range(2):
                    m, s = i * 2 + (ATT0 + u), i * 2 + u
                    split_w(m + 1, 1 - u, i * 16 + 16 * (3 + u))
                    act.wait_ge(negm_done, s + 1)
                    for h in range(NH):
                        t, hh = h // 2, h % 2
                        n = hh * 2 + t
                        act.activation(probs[:, h * NM:(h + 1) * NM], ps[:, 3 + hh, t * NM:(t + 1) * NM],
                                       ACT.Exp, bias=negm[:, n:n + 1], scale=HD ** -0.5,
                                       accum_out=sums[:, h:h + 1]).then_inc(p_done, 1)
                    act.wait_ge(pTp_done, s * 2 + 1)
                    act.activation(probsT[:, 0:512], ps[:, 5, :], ACT.Copy).then_inc(pTa_done, 1)

            def gate_sigmoids(j, g):
                for gate, (dst, bias) in enumerate(((s_r, "b_a"), (s_i, "b_x"))):
                    n = (j * 3 + g) * 2 + gate
                    act.wait_ge(gate_done, n + 1)
                    act.activation(dst[:, g * GN:(g + 1) * GN], ps[:, 3 + n % 3, 0:GN], ACT.Sigmoid,
                                   bias=pc(bias, j)).then_inc(gate_used, 1)

            def decay(j):
                act.wait_ge(gate_used, 6 * (j + 1))
                act.wait_ge(placed, 2 * j)
                act.activation(s_th, s_r, ACT.Tanh, scale=nsp[:, j:j + 1]).then_inc(decay_done, 1)
                act.activation(s_a2, s_r, ACT.Exp, scale=lt[:, 5, j:j + 1]).then_inc(decay_done, 1)
                act.wait_ge(decay_done, 3 * j + 2)
                act.activation(s_r, s_r, ACT.Exp, scale=nsp[:, j:j + 1]).then_inc(decay_done, 1)

            def root_b(j):
                act.wait_ge(rest_done, j + 1)
                act.activation(s_th, s_th, ACT.Sqrt, scale=-1.0).then_inc(root_b_done, 1)

            split_tile(13)
            act.wait_ge(qc_done, NCH)
            for j in range(2):
                act.wait_ge(z_used, 3 * (T_GA + j + 1))
                act.activation(zT[:, 9 + j, :], mixT[:, j, :], ACT.Sigmoid).then_inc(gasig_done, 1)
            act.wait_ge(pTp_done, 16)
            act.wait_ge(qb_done, 4)
            act.wait_ge(conv_done, 3)
            act.wait_ge(conv_stored, 48)
            for g in range(NG):
                gate_sigmoids(0, g)
                for c in range(3 * g, 3 * g + 3):
                    act.wait_ge(vt_done, c + 1)
                    act.activation(v_tok[:, c, :], ps[:, 6 + c % 2, 0:AW], ACT.Copy).then_inc(vt_used, 1)
            act.wait_ge(z_used, 3 * T_GB)
            act.wait_ge(pv_done, NCH)
            act.activation(s_th, mixT[:, 2, :], ACT.Sigmoid).then_inc(gasig_done, 1)
            split_tile(14)
            act.wait_ge(vsum_done, 3)
            act.wait_ge(ga_done, 3)
            act.wait_ge(nsp_done, 1)
            decay(0)
            act.wait_ge(vms_done, 1)
            act.activation(rstdv[:, :], ssv[:, :], ACT.Sqrt).then_inc(vroot_done, 1)
            root_b(0)
            split_tile(15)
            act.wait_ge(scan_done, 2)
            for g in range(NG):
                gate_sigmoids(1, g)
            split_tile(16)
            decay(1)
            root_b(1)
            split_tile(17)
            act.wait_ge(scan_done, 4)
            for g in range(NG):
                gate_sigmoids(2, g)
            split_tile(18)
            act.wait_ge(kc_read, NS)
            act.activation(sT_s, ps[:, 6, 0:64], ACT.Copy).then_inc(s1c_done, 1)
            decay(2)
            act.wait_ge(snegm_done, 1)
            act.wait_ge(kv_stored, 16)
            act.activation(p_s, ps[0:32, 7, 0:NM], ACT.Exp, bias=sst[:, 1:2], scale=HD ** -0.5,
                           accum_out=sst[:, 2:3]).then_inc(sp_exp, 1)
            root_b(2)
            for j in range(3):
                act.wait_ge(z_used, 3 * (T_GB + j + 1))
                act.wait_ge(gbm_done, j)
                act.activation(s_sig, zT[:, 8 + j, :], ACT.Sigmoid).then_inc(gbsig_done, 1)
            act.wait_ge(s3_done, 1)
            act.activation(kT[:, 1, 0:64], ps[:, 6, 0:64], ACT.Copy).then_inc(s3c_done, 1)

            act.wait_ge(z_done, 3 * N_TILES)
            for k in range(KT):
                src, s_in, n = wo_source(k)
                act.wait_ge(s_in, n)
                act.activation(wo_hi[:, k, 0:DM], src, ACT.Copy).then_inc(wohi_done, 1)

            def split_o(c0, slot):
                act.activation(o_hi[:, slot, :].rearrange("p (k n) -> p k n", k=KT),
                               mixT[:, :, bass.ds(c0, P)], ACT.Copy).then_inc(ohi_done, 1)

            def y_stats(c, u):
                act.wait_ge(y_done, c + 1)
                if not isinstance(c, int) or c > 0:
                    act.wait_ge(ysq_done, c)
                act.activation(probs[:, 0:DM].rearrange("p (a b) -> p a b", a=2), ps[:, 2 * u:2 * u + 2, :],
                               ACT.Square, accum_out=sy[:, u:u + 1]).then_inc(ysq_done, 1)
                act.wait_ge(yms_done, c + 1)
                act.activation(ry[:, u:u + 1], sy[:, u:u + 1], ACT.Sqrt).then_inc(yroot_done, 1)

            act.wait_ge(z_used, 3 * N_TILES)
            act.wait_ge(b_done, 3)
            act.wait_ge(c_done, NCH)
            act.wait_ge(cs_done, 4)
            split_o(0, 0)
            split_o(P, 1)
            y_stats(0, 0)
            with act.Fori(0, 3) as i:
                for u in range(2):
                    act.wait_ge(y_done, i * 2 + (u + 1))
                    act.wait_ge(o_done, i * 2 + (u + 1))
                    split_o(i * (2 * P) + (u + 2) * P, u)
                    y_stats(i * 2 + (u + 1), 1 - u)
            act.wait_ge(y_done, 7)
            split_o(LASTC, 0)
            y_stats(7, 1)
            y_stats(8, 0)

        @block.gpsimd
        def _(pool):
            own = Tally(pool, pool_own)

            def low_w(m, slot):
                pool.wait_ge(whi_done, m + 1)
                pool.tensor_tensor(w_lo[:, slot, :], w_stage[:, slot, :], w_hi[:, slot, :].bitcast(F),
                                   ALU.subtract).then_inc(wlo_done, 1)

            pool.memset(ones[:, :], 1.0).then_inc(const_set, 1)
            own.link(pool.memset(ident[:, :], 0.0))
            pool.affine_select(out=ident[:, :], in_=ident[:, :], compare_op=ALU.not_equal, fill=1.0, base=0,
                               pattern=[[-1, P]], channel_multiplier=1).then_inc(const_set, 1)
            pool.memset(qb[:, :, :, :], 0.0).then_inc(const_set, 1)
            low_w(0, 0)
            low_w(1, 1)
            pool.wait_ge(wsT_in, 16)
            pool.affine_select(out=wsT[:, :, :], in_=wsT[:, :, :], compare_op=ALU.is_ge, fill=0.0, base=0,
                               pattern=[[0, AH], [1, P]], channel_multiplier=-1).then_inc(w_masked, 1)
            low_w(2, 0)
            low_w(3, 1)
            low_w(4, 0)
            with pool.Fori(0, 4) as i:
                for u in range(2):
                    m, s = i * 2 + (ATT0 + u), i * 2 + u
                    pool.tensor_copy(q_chunk[:, u, :, :], zT[:, 0:2, bass.ds(i * (2 * P) + u * P, P)]).then_inc(qc_done, 1)
                    low_w(m + 1, 1 - u)

            def keep_xc(j):
                pool.wait_ge(gate_used, 6 * (j + 1))
                pool.tensor_tensor(s_i, s_i, mixT[:, 3 + j, :], ALU.mult).then_inc(ixc_done, 1)

            def place(j):
                pool.wait_ge(scan_done, 2 * (j + 1))
                pool.wait_ge(gate_done, 6 * min(j + 2, 3))
                pool.tensor_copy(mixT[:, 3 + j, :], s_th).then_inc(placed, 1)
                pool.tensor_copy(h_last[:, j, :], s_th[:, NT - 1:TT]).then_inc(placed, 1)

            low_w(13, 1)
            pool.wait_ge(xsq_done, 9)
            for q, (c0, n) in enumerate(((0, 4), (4, 4), (8, 1))):
                pool.wait_ge(vt_used, c0 + n)
                if q:
                    pool.wait_ge(vsum_done, q)
                pool.tensor_tensor(v_sq[:, 0:n, :], v_tok[:, c0:c0 + n, :], v_tok[:, c0:c0 + n, :],
                                   ALU.mult).then_inc(vsq_done, 1)
            low_w(14, 0)
            keep_xc(0)
            pool.wait_ge(rows_in, 16)
            for q, (c0, n) in enumerate(((0, 4), (4, 4), (8, 1))):
                pool.wait_ge(vr_done, q + 1)
                pool.tensor_tensor(v_tok[:, c0:c0 + n, :], v_tok[:, c0:c0 + n, :],
                                   rows[:, 0:AW].unsqueeze(1).broadcast_to([P, n, AW]), ALU.mult).then_inc(vn_done, 1)
            for j in range(3):
                pool.wait_ge(ga_done, j + 1)
                pool.tensor_tensor(mixT[:, j, :], mixT[:, j, :], rstdB[:, :], ALU.mult).then_inc(gar_done, 1)
            low_w(15, 1)
            place(0)
            low_w(16, 0)
            keep_xc(1)
            low_w(17, 1)
            place(1)
            low_w(18, 0)
            keep_xc(2)
            place(2)

            def low_o(c0, slot):
                pool.tensor_tensor(o_lo[:, slot, :].rearrange("p (k n) -> p k n", k=KT),
                                   mixT[:, :, bass.ds(c0, P)],
                                   o_hi[:, slot, :].bitcast(F).rearrange("p (k n) -> p k n", k=KT),
                                   ALU.subtract).then_inc(o_done, 1)

            def add_x(c, u, arrived):
                pool.wait_ge(y_used, c + 1)
                pool.wait_ge(x_in[u], arrived)
                pool.tensor_tensor(y_out[:, u, :], y_out[:, u, :], x_ring[:, u, 0:DM], ALU.add).then_inc(y_ready, 1)

            pool.wait_ge(ohi_done, 1)
            low_o(0, 0)
            pool.wait_ge(ohi_done, 2)
            low_o(P, 1)
            add_x(0, 0, 16 * 6)
            with pool.Fori(0, 3) as i:
                for u in range(2):
                    pool.wait_ge(ohi_done, i * 2 + (u + 3))
                    low_o(i * (2 * P) + (u + 2) * P, u)
                    add_x(i * 2 + (u + 1), 1 - u, i * 16 + (16 * 5 if u == 0 else 16 * 7))
            pool.wait_ge(ohi_done, 9)
            low_o(LASTC, 0)
            add_x(7, 1, 16 * 8)
            add_x(8, 0, 16 * 10)

        @block.vector
        def _(dve):
            own = Tally(dve, dve_own)

            def evac(m, g, dst):
                dve.wait_ge(z_done, m * 3 + (g + 1))
                dve.tensor_tensor(dst, ps[:, g, 0:GN], rstdB[:, g * GN:(g + 1) * GN], ALU.mult).then_inc(z_used, 1)

            def grp(g):
                return slice(g * GN, (g + 1) * GN)

            dve.wait_ge(par_in, 16)
            dve.wait_ge(memT_in, 16)
            for i in range(2):
                kk = slice(4 * i, 4 * i + 4)
                dve.tensor_tensor(memT[:, kk, :], memT[:, kk, :],
                                  pc("g_mem", 4 * i, 4).unsqueeze(2).broadcast_to([P, 4, NM]), ALU.mult).then_inc(memg_done, 1)
            own.link(dve.tensor_scalar(lt[:, 2, :], pc("lam", 0, 3), -1.0, None, ALU.mult))
            dve.tensor_tensor(lt[:, 0, :], pc("lam", 0, 3), lt[:, 2, :], ALU.max).then_inc(lam_done, 1)
            for k in range(KT):
                dve.wait_ge(xhi_done, k + 1)
                dve.scalar_tensor_tensor(x_lo[:, k, :], mixT[:, k, :], pc("g_pre", k), x_hi[:, k, :].bitcast(F),
                                         ALU.mult, ALU.subtract).then_inc(xlo_done, 1)
            dve.wait_ge(xsq_done, 9)
            dve.wait_ge(act_own, 2)
            dve.tensor_scalar(ssq[:, :], ssq[:, :], 1.0 / DM, EPS, ALU.mult, ALU.add).then_inc(ms_done, 1)
            dve.wait_ge(elam_done, 1)
            own.link(dve.tensor_scalar(lt[:, 3, :], lt[:, 1, :], 2.0, None, ALU.add))
            own.link(dve.reciprocal(lt[:, 4, :], lt[:, 3, :]))
            own.link(dve.tensor_tensor(lt[:, 3, :], lt[:, 4, :], lt[:, 1, :], ALU.mult))
            own.link(dve.tensor_tensor(lt[:, 4, :], lt[:, 3, :], lt[:, 3, :], ALU.mult))
            own.link(dve.tensor_scalar(lt[:, 5, :], lt[:, 4, :], 1.0 / 17, None, ALU.mult))
            for n in range(15, 2, -2):
                own.link(dve.scalar_tensor_tensor(lt[:, 5, :], lt[:, 5, :], 1.0 / n, lt[:, 4, :], ALU.add, ALU.mult))
            own.link(dve.scalar_tensor_tensor(lt[:, 5, :], lt[:, 5, :], 1.0, lt[:, 3, :], ALU.add, ALU.mult))
            own.link(dve.tensor_scalar(lt[:, 2, :], lt[:, 2, :], 0.0, -LRU_C, ALU.max, ALU.mult))
            own.link(dve.scalar_tensor_tensor(nsp[:, :], lt[:, 5, :], -2.0 * LRU_C, lt[:, 2, :], ALU.mult, ALU.add))
            dve.tensor_scalar(lt[:, 5, :], nsp[:, :], 2.0, None, ALU.mult).then_inc(nsp_done, 1)
            dve.wait_ge(root_done, 1)
            own.link(dve.reciprocal(rstd[:, :], rstd[:, :]))
            dve.wait_ge(const_set, 2)
            dve.wait_ge(act_own, 2)
            dve.tensor_tensor(probs[:, 0:NT].rearrange("p (c n) -> p c n", c=NCH),
                              ident[:, :].unsqueeze(1).broadcast_to([P, NCH, P]),
                              rstd[:, 0:NCH].unsqueeze(2).broadcast_to([P, NCH, P]), ALU.mult).then_inc(diag_done, 1)
            dve.tensor_scalar(probs[:, NT:TT], ident[:, P - NS:P], rstd[:, 8:9], None, ALU.mult).then_inc(diag_done, 1)
            dve.wait_ge(rstdB_done, 3)
            for m in range(4):
                for g in range(NG):
                    evac(m, g, zT[:, m, grp(g)] if m < 2 else mixT[:, 4 + m, grp(g)])
            dve.wait_ge(const_set, 3)
            dve.wait_ge(z_used, 6)
            for t in range(2):
                for hh in range(2):
                    r = slice(hh * HD, (hh + 1) * HD)
                    dve.tensor_copy(qb[r, t, :, 2 * t + hh], zT[r, t, NT:TT]).then_inc(qb_done, 1)
            for j, sig in enumerate((probs, probsT)):
                dve.wait_ge(gcsig_done, j + 1)
                dve.tensor_tensor(mixT[:, 6 + j, :], mixT[:, 6 + j, :], sig[:, :], ALU.mult).then_inc(gc_done, 1)
            dve.wait_ge(gc_done, 2)

            def attend(m, s, c0, dst):
                for hh in range(2):
                    dve.wait_ge(sc_done, s * 2 + (hh + 1))
                    own.mark(dve.tensor_reduce(mx[:, 2 * hh:2 * hh + 2],
                                               ps[:, 3 + hh, :].rearrange("p (t n) -> p t n", t=2), AX.X, ALU.max))
                own.wait()
                dve.tensor_scalar(negm[:, :], mx[:, :], -HD ** -0.5, None, ALU.mult).then_inc(negm_done, 1)
                evac(m, 0, dst(0))
                dve.wait_ge(pTp_done, s * 2 + 2)
                dve.tensor_copy(probsT[:, 512:1024], ps[:, 6, :]).then_inc(pTb_done, 1)
                dve.wait_ge(p_done, s * 4 + 4)
                own.link(dve.reciprocal(rsum[:, :], sums[:, :]))
                evac(m, 1, dst(1))
                dve.wait_ge(pv_done, s + 1)
                dve.tensor_tensor(attn[:, :].rearrange("p (h n) -> p h n", h=NH),
                                  ps[:, 7, 0:256].rearrange("p (h n) -> p h n", h=NH),
                                  rsum[:, :].unsqueeze(2).broadcast_to([P, NH, HD]), ALU.mult).then_inc(attn_done, 1)
                evac(m, 2, dst(2))
                dve.wait_ge(attnT_done, s + 1)
                cols = mixT[:, 6:8, bass.ds(c0, P)]
                dve.tensor_tensor(cols, ps[:, 7, 256:512].rearrange("p (t n) -> p t n", t=2), cols,
                                  ALU.mult).then_inc(c_done, 1)

            def convolve(j):
                xb, xc = zT[:, 2 + j, :], mixT[:, 3 + j, :]
                dve.wait_ge(z_used, 3 * (T_XB + j + 1))
                own.link(dve.tensor_scalar(xc, xb, pc("w_conv", 4 * j + 3), pc("b_conv", j), ALU.mult, ALU.add))
                for back in (1, 2, 3):
                    tap = pc("w_conv", 4 * j + 3 - back)
                    own.mark(dve.scalar_tensor_tensor(xc[:, back:NT], xb[:, 0:NT - back], tap, xc[:, back:NT],
                                                      ALU.mult, ALU.add))
                    last = dve.scalar_tensor_tensor(xc[:, NT:TT], pc("st_conv", 24 * j + 8 * (3 - back), 8), tap,
                                                    xc[:, NT:TT], ALU.mult, ALU.add)
                    if back < 3:
                        own.link(last)
                last.then_inc(conv_done, 1)
                own.wait()

            base = own.k
            per = 3
            own.base, own.k = base, 0
            with dve.Fori(0, 3) as i:
                own.base, own.k = i * per + base, 0
                attend(i + ATT0, i, i * P,
                       lambda g: zf[:, bass.ds(i * TT + (2 * TT + g * GN), GN)])
                assert own.k == per
            own.base, own.k = base + 3 * per, 0
            for m in (7, 8, 9):
                attend(m, m - ATT0, (m - ATT0) * P, lambda g: zT[:, m - 2, grp(g)])
                convolve(m - 7)
            for m in (10, 11):
                attend(m, m - ATT0, (m - ATT0) * P, lambda g: mixT[:, m - 10, grp(g)])

            def gate_a(j):
                dve.wait_ge(gasig_done, j + 1)
                dve.tensor_tensor(mixT[:, j, :], mixT[:, j, :], (zT[:, 9, :], zT[:, 10, :], s_th)[j],
                                  ALU.mult).then_inc(ga_done, 1)

            def v_sums(q):
                n = 4 if q < 2 else 1
                dve.wait_ge(vsq_done, q + 1)
                dve.tensor_reduce(ssv[:, 16 * q:16 * q + 4 * n],
                                  v_sq[:, 0:n, :].rearrange("p c (h n) -> p (c h) n", h=AH), AX.X, ALU.add).then_inc(vsum_done, 1)

            def rest(j):
                dve.wait_ge(decay_done, 3 * (j + 1))
                dve.scalar_tensor_tensor(s_th, s_a2, 1.0, s_th, ALU.add, ALU.mult).then_inc(rest_done, 1)

            def scan(j):
                dve.wait_ge(root_b_done, j + 1)
                dve.wait_ge(ixc_done, j + 1)
                own.link(dve.tensor_tensor(s_i, s_i, s_th, ALU.mult))
                dve.tensor_tensor_scan(s_th[:, 0:NT], s_r[:, 0:NT], s_i[:, 0:NT], 0.0, ALU.mult, ALU.add).then_inc(scan_done, 1)
                own.link(dve.tensor_tensor(s_th[:, NT:TT], s_r[:, NT:TT], pc("st_h", 8 * j, 8), ALU.mult))
                dve.tensor_tensor(s_th[:, NT:TT], s_th[:, NT:TT], s_i[:, NT:TT], ALU.add).then_inc(scan_done, 1)

            evac(12, 0, mixT[:, 2, grp(0)])
            gate_a(0)
            evac(12, 1, mixT[:, 2, grp(1)])
            gate_a(1)
            evac(12, 2, mixT[:, 2, grp(2)])
            gate_a(2)
            evac(13, 0, zT[:, 8, grp(0)])
            v_sums(0)
            v_sums(1)
            evac(13, 1, zT[:, 8, grp(1)])
            v_sums(2)
            dve.wait_ge(vsum_done, 3)
            dve.tensor_scalar(ssv[:, :], ssv[:, :], 1.0 / AD, EPS, ALU.mult, ALU.add).then_inc(vms_done, 1)
            rest(0)
            evac(13, 2, zT[:, 8, grp(2)])
            dve.wait_ge(vroot_done, 1)
            own.link(dve.reciprocal(rstdv[:, :], rstdv[:, :]))
            for q, (c0, n) in enumerate(((0, 4), (4, 4), (8, 1))):
                vv = v_tok[:, c0:c0 + n, :].rearrange("p c (h n) -> p (c h) n", h=AH)
                dve.tensor_tensor(vv, vv, rstdv[:, 16 * q:16 * q + 4 * n].unsqueeze(2).broadcast_to([P, 4 * n, AD]),
                                  ALU.mult).then_inc(vr_done, 1)
            scan(0)
            for g in range(NG):
                evac(14, g, zT[:, 9, grp(g)])
                for c in range(3 * g, 3 * g + 3):
                    vc = v_tok[:, c, :].rearrange("p (h n) -> p h n", h=AH)
                    if c < NCH:
                        dve.wait_ge(sp_done, c + 1)
                        dve.tensor_tensor(vc, ps[:, 6 + c % 2, 0:AW].rearrange("p (h n) -> p h n", h=AH),
                                          pc("b_s", 0, 4).unsqueeze(2).broadcast_to([P, AH, AD]), ALU.add).then_inc(mix_done, 1)
                    else:
                        dve.wait_ge(vn_done, 3)
                        dve.wait_ge(vs_stored, 16)
                        own.link(dve.tensor_tensor(vc, vc, rows[:, AW:AW + 4].unsqueeze(2).broadcast_to([P, AH, AD]), ALU.mult))
                        dve.tensor_tensor(vc, vc, rows[:, AW + 4:AW + 8].unsqueeze(2).broadcast_to([P, AH, AD]),
                                          ALU.add).then_inc(mix_done, 1)
            dve.wait_ge(gar_done, 3)
            for g in range(NG):
                evac(15, g, zT[:, 10, grp(g)])
                for c in range(3 * g, 3 * g + 3):
                    dve.wait_ge(mT_done, c + 1)
                    n, a = (P, 0) if c < NCH else (NS, P - NS)
                    dve.tensor_tensor(mixT[:, 0:3, c * P:c * P + n],
                                      ps[:, 6 + c % 2, 0:AW].rearrange("p (j n) -> p j n", j=3)[:, :, a:a + n],
                                      mixT[:, 0:3, c * P:c * P + n], ALU.mult).then_inc(a_done, 1)
            rest(1)
            scan(1)

            def times_u(m, g):
                out = mixT[:, m - T_U, grp(g)]
                dve.wait_ge(z_done, 3 * m + g + 1)
                dve.tensor_tensor(out, ps[:, g, 0:GN], out, ALU.mult).then_inc(z_used, 1)

            dve.wait_ge(a_done, 9)
            for g in range(NG):
                times_u(16, g)
            times_u(17, 0)
            dve.wait_ge(s2_done, 1)
            own.link(dve.tensor_reduce(sst[:, 0:1], ps[0:32, 7, 0:NM], AX.X, ALU.max))
            dve.tensor_scalar(sst[:, 1:2], sst[:, 0:1], -HD ** -0.5, None, ALU.mult).then_inc(snegm_done, 1)
            times_u(17, 1)
            rest(2)
            times_u(17, 2)
            dve.wait_ge(sp_exp, 1)
            own.link(dve.reciprocal(sst[:, 3:4], sst[:, 2:3]))
            dve.tensor_scalar(p_s, p_s, sst[:, 3:4], None, ALU.mult).then_inc(sp_norm, 1)
            scan(2)
            for j in range(3):
                if j:
                    times_u(18, j - 1)
                dve.wait_ge(gbsig_done, j + 1)
                dve.tensor_tensor(zT[:, 8 + j, :], zT[:, 8 + j, :], s_sig, ALU.mult).then_inc(gbm_done, 1)
            times_u(18, 2)
            for j in range(3):
                dve.wait_ge(placed, 2 * (j + 1))
                dve.wait_ge(gbm_done, j + 1)
                dve.tensor_tensor(mixT[:, 3 + j, :], mixT[:, 3 + j, :], zT[:, 8 + j, :], ALU.mult).then_inc(b_done, 1)
            dve.wait_ge(vc_read, NS)
            for t in range(2):
                for hh in range(2):
                    r = slice(hh * HD, (hh + 1) * HD)
                    got = ps[r, 7, t * 32:(t + 1) * 32].rearrange("p (n h) -> p n h", h=NH)[:, :, 2 * t + hh]
                    dve.tensor_tensor(mixT[r, 6 + t, NT:TT], got, mixT[r, 6 + t, NT:TT], ALU.mult).then_inc(cs_done, 1)
            for k in range(KT):
                dve.wait_ge(wohi_done, k + 1)
                dve.tensor_tensor(wo_lo[:, k, 0:DM], wo_source(k)[0], wo_hi[:, k, 0:DM].bitcast(F),
                                  ALU.subtract).then_inc(wo_done, 1)
            dve.wait_ge(gpost_in, 16)

            def finish(c, u, stored):
                dve.wait_ge(ysq_done, c + 1)
                dve.tensor_scalar(sy[:, u:u + 1], sy[:, u:u + 1], 1.0 / DM, EPS, ALU.mult, ALU.add).then_inc(yms_done, 1)
                dve.wait_ge(yroot_done, c + 1)
                own.link(dve.reciprocal(ry[:, u:u + 1], ry[:, u:u + 1]))
                if not isinstance(stored, int) or stored:
                    dve.wait_ge(y_stored[u], stored)
                dve.scalar_tensor_tensor(y_out[:, u, :].rearrange("p (a b) -> p a b", a=2), ps[:, 2 * u:2 * u + 2, :],
                                         ry[:, u:u + 1], g_post.rearrange("p (a b) -> p a b", a=2),
                                         ALU.mult, ALU.mult).then_inc(y_used, 1)

            for c in range(2):
                finish(c, c, 0)
            base = own.base + own.k
            with dve.Fori(0, 3) as i:
                for u in range(2):
                    own.base, own.k = i * 2 + (base + u), 0
                    finish(i * 2 + (2 + u), u, i * 16 + 16)
            own.base, own.k = base + 6, 0
            finish(8, 0, 16 * 4)


_OUTS = {"o_y": [TT, DM], "o_kv": [P, MT, 512], "o_conv": [P, 3, 3 + NS], "o_st": [P, 72],
         "o_h": [P, 3, 1 + NS], "o_vs": [NS, AW]}


def kernel(**inputs):
    import concourse.bacc as bacc
    from concourse.bass_utils import run_bass_kernel_spmd

    a = {k: np.asarray(v) for k, v in inputs.items()}

    def tiles(w):
        return w.reshape(-1, P, w.shape[-1]).transpose(1, 0, 2)

    def per_part(v):
        return v.reshape(-1, P).T

    x_all = np.concatenate([a["x_prompt"][0], a["x_sample"][:, 0]], axis=0)
    w_in = a["w_in"][0]
    cuts = {"u": 0, "v": AW, "ga": 2 * AW, "xb": 3 * AW, "gb": 4 * AW, "q": 5 * AW, "gc": 5 * AW + 256}
    order = [("q", 2), ("gc", 2), ("xb", 3), ("v", 3), ("ga", 3), ("gb", 3), ("u", 3)]
    cols = np.concatenate([w_in[:, cuts[n]:cuts[n] + P * t] for n, t in order], axis=1)
    w_tiles = cols.reshape(KT, P, N_TILES, P).transpose(2, 1, 0, 3).reshape(N_TILES, P, DM)
    st = a["state_conv"][0].transpose(2, 1, 0).reshape(3, P, 3, NS).transpose(1, 0, 2, 3).reshape(P, 72)
    sh = a["state_h"][0].T.reshape(3, P, NS).transpose(1, 0, 2).reshape(P, 24)
    wc = a["w_conv"][0].T.reshape(3, P, 4).transpose(1, 0, 2).reshape(P, 12)
    par = np.concatenate([per_part(a["g_pre"][0]), per_part(a["g_mem"][0]), wc, per_part(a["b_conv"][0]),
                          per_part(a["b_a"][0]), per_part(a["b_x"][0]), per_part(a["lru_lambda"][0]),
                          st, sh, a["b_s"][0].T], axis=1)
    gate_w = np.zeros((P, 2, len(GATE_PAIRS), P), np.float32)
    for n, name in enumerate(("w_a", "w_x")):
        full = np.zeros((AW, AW), np.float32)
        for b in range(8):
            full[48 * b:48 * b + 48, 48 * b:48 * b + 48] = a[name][0, b]
        for x, (kin, out) in enumerate(GATE_PAIRS):
            gate_w[:, n, x] = full[kin * P:(kin + 1) * P, out * P:(out + 1) * P]
    arrays = {
        "par": par,
        "memT": tiles(a["mem_prompt"][0].T),
        "w_mem": tiles(np.concatenate([a["w_mk"][0], a["w_mv"][0]], axis=1)),
        "w_tiles": w_tiles,
        "xT": tiles(x_all.T),
        "mem_nat": tiles(a["mem_prompt"][0]),
        "x_all": x_all,
        "rows": np.concatenate([a["g_v"][0], a["w_s"][0, :, 0, 0], a["b_s"][0, :, 0]]),
        "wsT": a["w_s"][0].transpose(2, 0, 1),
        "gate_w": gate_w,
        "kcT": a["cache_mem_k"][0].reshape(NS, NM, 2, P).transpose(0, 3, 2, 1).reshape(NS, P, 512),
        "vc": a["cache_mem_v"][0].reshape(NS, MT, P, 256).transpose(0, 2, 1, 3).reshape(NS, P, 512),
        "w_out": a["w_out"][0].reshape(KT, P, DM),
        "g_post": a["g_post"][0],
    }
    nc = bacc.Bacc("TRN2", target_bir_lowering=False, num_devices=1)
    d, feed = {}, {}
    for name, v in arrays.items():
        v = np.ascontiguousarray(v)
        feed["in_" + name] = v
        d[name] = nc.dram_tensor("in_" + name, list(v.shape), F, kind="ExternalInput").ap()
    for name, shape in _OUTS.items():
        d[name] = nc.dram_tensor(name, shape, F, kind="ExternalOutput").ap()
    build(nc, d)
    r = run_bass_kernel_spmd(nc, [feed], core_ids=[0]).results[0]
    y, kvo = r["o_y"], r["o_kv"].transpose(1, 0, 2).reshape(NM, 512)
    cv = r["o_conv"].transpose(1, 0, 2).reshape(AW, 3 + NS)
    stp = r["o_st"].reshape(P, 3, 3, NS).transpose(3, 2, 1, 0).reshape(NS, 3, AW)
    hh = r["o_h"].transpose(1, 0, 2).reshape(AW, 1 + NS)
    new_conv_s = np.concatenate([stp[:, 1:], cv[:, 3:].T[:, None]], axis=1)
    return (y[:NT][None], y[NT:][:, None],
            kvo[:, :256].reshape(1, 1, NM, NH, HD), kvo[:, 256:].reshape(1, 1, NM, NH, HD),
            np.ascontiguousarray(cv[:, :3].T)[None, None], np.ascontiguousarray(hh[:, 0])[None, None],
            new_conv_s[None], np.ascontiguousarray(hh[:, 1:].T)[None], r["o_vs"][None, :, None])
```

```python
from contextlib import ExitStack

import numpy as np
import concourse.bass as bass
from concourse import mybir

F = mybir.dt.float32
R = mybir.dt.float32r
ALU = mybir.AluOpType
ACT = mybir.ActivationFunctionType
AX = mybir.AxisListType

P = 128
DM = 1024
NT, NS = 1024, 8
TT = NT + NS
KT = DM // P
NG = 3
GN = TT // NG
NCH = NT // P
LASTC = TT - P
EPS = 1e-6
NM, MT = 256, 2
NH, HD = 4, 64
AH, AD = 4, 96
AW = AH * AD
LRU_C = 8.0
T_Q, T_GC, T_XB, T_V, T_GA, T_GB, T_U, N_TILES = 0, 2, 4, 7, 10, 13, 16, 19
ATT0 = 4
PAR = {}
_at = 0
for _name, _n in (("g_pre", 8), ("g_mem", 8), ("w_conv", 12), ("b_conv", 3), ("b_a", 3), ("b_x", 3),
                  ("lam", 3), ("st_conv", 72), ("st_h", 24), ("b_s", 4)):
    PAR[_name] = _at
    _at += _n
N_PAR = _at
K_ORDER = [3, 4, 5, 6, 7, 0, 1, 2]
GATE_PAIRS = [(0, 0), (1, 0), (0, 1), (1, 1), (2, 1), (1, 2), (2, 2)]


class Tally:

    def __init__(self, eng, sem):
        self.eng, self.sem, self.base, self.k = eng, sem, 0, 0

    def mark(self, ins):
        ins.then_inc(self.sem, 1)
        self.k += 1

    def wait(self):
        self.eng.wait_ge(self.sem, self.base + self.k)

    def link(self, ins):
        self.mark(ins)
        self.wait()


def build(nc, d):
    with ExitStack() as ctx:
        def sb(name, shape, dt=F):
            return ctx.enter_context(nc.sbuf_tensor(name, shape, dt))

        def sem(name):
            return ctx.enter_context(nc.semaphore(name))

        x_hi, x_lo = sb("x_hi", [P, KT, TT], R), sb("x_lo", [P, KT, TT], R)
        w_stage = sb("w_stage", [P, 2, DM])
        w_hi, w_lo = sb("w_hi", [P, 2, DM], R), sb("w_lo", [P, 2, DM], R)
        mixT = sb("mixT", [P, KT, TT])
        zT = sb("zT", [P, 11, TT])
        rstdB = sb("rstdB", [P, TT])
        probs, probsT = sb("probs", [P, TT]), sb("probsT", [P, TT])
        kv = sb("kv", [P, MT, 512])
        kT = sb("kT", [P, 2, NM])
        x_ring = sb("x_ring", [P, 2, TT])
        rows = sb("rows", [P, AW + 8])
        gate_w = sb("gate_w", [P, 2, len(GATE_PAIRS), P])
        wsT = sb("wsT", [P, AH, P])
        ident = sb("ident", [P, P])
        q_chunk = sb("q_chunk", [P, 2, 2, P])
        attn = sb("attn", [P, NM])
        par = sb("par", [P, N_PAR])
        ssq, rstd = sb("ssq", [P, 11]), sb("rstd", [P, 11])
        ssv, rstdv = sb("ssv", [P, 36]), sb("rstdv", [P, 36])
        mx, negm = sb("mx", [P, 4]), sb("negm", [P, 4])
        sums, rsum = sb("sums", [P, 4]), sb("rsum", [P, 4])
        nba, nsp, lt = sb("nba", [P, 3]), sb("nsp", [P, 3]), sb("lt", [P, 6, 3])
        qb = sb("qb", [P, 2, NS, NH])
        sy, ry = sb("sy", [P, 4]), sb("ry", [P, 2])
        sst = sb("sst", [32, 4])
        h_last = sb("h_last", [P, 3, NS + 1])
        ps = ctx.enter_context(nc.psum_tensor("ps", [P, 8, 512], F))

        zf = zT[:, :, :].rearrange("p a b -> p (a b)")
        memT = zf[:, 2 * TT:2 * TT + KT * NM].rearrange("p (k m) -> p k m", k=KT)
        w_mem = zf[:, 4 * TT:4 * TT + KT * 512].rearrange("p (k m) -> p k m", k=KT)
        mem_nat = zf[:, 8 * TT:8 * TT + MT * DM].rearrange("p (k m) -> p k m", k=MT)
        v_tok = zf[:, TT:TT + 9 * AW].rearrange("p (c n) -> p c n", c=9)
        v_sq = x_ring[:, :, :].rearrange("p a b -> p (a b)")[:, 0:4 * AW].rearrange("p (c n) -> p c n", c=4)
        cache_ring = zf[:, 5 * TT:5 * TT + 6 * 512].rearrange("p (c n) -> p c n", c=6)
        wo_early = zf[:, TT:TT + 4 * DM].rearrange("p (c n) -> p c n", c=4)
        y_out = zf[:, 5 * TT:5 * TT + 2 * DM].rearrange("p (c n) -> p c n", c=2)
        g_post = zf[:, 7 * TT:7 * TT + DM]
        s_r, s_i, s_th = zT[:, 0, :], probs[:, :], probsT[:, :]
        s_a2, s_sig = x_ring[:, 0, :], x_ring[:, 1, :]
        sT_s = kT[:, 0, 0:64]
        p_s = kv[0:32, 0, 0:NM]
        pT_s = kT[:, 1, 0:64].rearrange("p (m n) -> p m n", m=2)
        o_hi, o_lo = w_hi, w_lo
        wo_hi, wo_lo = x_hi, x_lo

        def wo_source(n):
            if n in (0, 1, 7):
                return w_stage[:, n % 7, :], 16
            return (wo_early[:, n - 2, :] if n < 6 else zT[:, 0, 0:DM]), 16

        def pc(name, i=0, n=1):
            return par[:, PAR[name] + i:PAR[name] + i + n]

        par_in, rows_in, gatew_in, wsT_in, memn_in = map(sem, (
            "par_in", "rows_in", "gatew_in", "wsT_in", "memn_in"))
        memT_in = [sem(f"memT_in{i}") for i in range(4)]
        wm_in = [sem(f"wm_in{i}") for i in range(4)]
        xT_in = [sem(f"xT_in{k}") for k in range(KT)]
        w_in = [sem(f"w_in{i}") for i in range(2)]
        x_in = [sem(f"x_in{i}") for i in range(2)]
        c_in = [sem(f"cache_in{i}") for i in range(6)]
        wo_in = [sem(f"wo_in{i}") for i in range(KT)]
        gpost_in = sem("gpost_in")
        y_stored = [sem(f"y_stored{i}") for i in range(2)]
        kv_stored, conv_stored, h_stored, vs_stored = map(sem, (
            "kv_stored", "conv_stored", "h_stored", "vs_stored"))
        const_set, w_masked, wlo_done, qc_done, xsq_done, whi_done, xhi_done = map(sem, (
            "const_set", "w_masked", "wlo_done", "qc_done", "xsq_done", "whi_done", "xhi_done"))
        xlo_done, memg_done, ms_done, root_done, rep_done, rstdB_done = map(sem, (
            "xlo_done", "memg_done", "ms_done", "root_done", "rep_done", "rstdB_done"))
        kvp_done, kv_done, kTp_done, kT_done = map(sem, ("kvp_done", "kv_done", "kTp_done", "kT_done"))
        z_done, z_used, rstdp_done = map(sem, ("z_done", "z_used", "rstdp_done"))
        gcsig_done, gc_done = map(sem, ("gcsig_done", "gc_done"))
        sc_done, negm_done, p_done, pTp_done, pTa_done, pTb_done = map(sem, (
            "sc_done", "negm_done", "p_done", "pTp_done", "pTa_done", "pTb_done"))
        pv_done, attn_done, attnT_done, c_done = map(sem, ("pv_done", "attn_done", "attnT_done", "c_done"))
        lam_done, elam_done, nsp_done, conv_done = map(sem, ("lam_done", "elam_done", "nsp_done", "conv_done"))
        gate_done, gate_used, vt_done, vt_used = map(sem, ("gate_done", "gate_used", "vt_done", "vt_used"))
        ixc_done, gbm_done = sem("ixc_done"), sem("gbm_done")
        q_done = sem("q_done")
        y_half, ysq_half, y_last = map(sem, ("y_half", "ysq_half", "y_last"))
        vsq_done, vsum_done, vroot_done, vms_done, vr_done, vn_done = map(sem, (
            "vsq_done", "vsum_done", "vroot_done", "vms_done", "vr_done", "vn_done"))
        gasig_done, ga_done, gar_done = map(sem, ("gasig_done", "ga_done", "gar_done"))
        sp_done, mix_done, mT_done, a_done = map(sem, ("sp_done", "mix_done", "mT_done", "a_done"))
        decay_done, rest_done, root_b_done, scan_done, placed = map(sem, (
            "decay_done", "rest_done", "root_b_done", "scan_done", "placed"))
        gbsig_done, b_done = map(sem, ("gbsig_done", "b_done"))
        qb_done, s1c_done, s2_done, snegm_done, sp_exp, sp_norm, s3_done, s3c_done, cs_done = map(sem, (
            "qb_done", "s1c_done", "s2_done", "snegm_done", "sp_exp", "sp_norm", "s3_done",
            "s3c_done", "cs_done"))
        cache_read = sem("cache_read")
        wohi_done, wo_done, ohi_done, o_done = map(sem, ("wohi_done", "wo_done", "ohi_done", "o_done"))
        y_done, ysq_done, yms_done, yroot_done, y_used, y_ready = map(sem, (
            "y_done", "ysq_done", "yms_done", "yroot_done", "y_used", "y_ready"))
        dve_own, pool_own, act_own = sem("dve_own"), sem("pool_own"), sem("act_own")

        block = ctx.enter_context(nc.Block())

        @block.sync
        def _(sp):
            def load_w(m, slot):
                sp.dma_start(w_stage[:, slot, :], d["w_tiles"][m]).then_inc(w_in[slot], 16)

            def load_cache(n):
                if n >= 6:
                    sp.wait_ge(cache_read, n - 5)
                src = d["kcT"][n] if n < NS else d["vc"][n - NS]
                sp.dma_start(cache_ring[:, n % 6, :], src).then_inc(c_in[n % 6], 16)

            sp.dma_start(par[:, :], d["par"]).then_inc(par_in, 16)
            load_w(0, 0)
            for k in range(KT):
                if k == 6:
                    load_w(1, 1)
                sp.dma_start(mixT[:, k, :], d["xT"][:, k, :]).then_inc(xT_in[k], 16)
            for i in range(4):
                kk = slice(2 * i, 2 * i + 2)
                sp.dma_start(memT[:, kk, :], d["memT"][:, kk, :]).then_inc(memT_in[i], 16)
                sp.dma_start(w_mem[:, kk, :], d["w_mem"][:, kk, :]).then_inc(wm_in[i], 16)
            sp.dma_start(mem_nat, d["mem_nat"]).then_inc(memn_in, 16)
            for c in range(9):
                if c >= 2:
                    sp.wait_ge(xsq_done, c - 1)
                sp.dma_start(x_ring[:, c % 2, 0:DM],
                             d["x_all"][min(c * P, LASTC):min(c * P, LASTC) + P, :]).then_inc(x_in[c % 2], 16)
                if c == 3:
                    sp.wait_ge(wlo_done, 1)
                    load_w(2, 0)
            sp.dma_start(rows[:, :], d["rows"].partition_broadcast(P)).then_inc(rows_in, 16)
            sp.dma_start(wsT[:, :, :], d["wsT"]).then_inc(wsT_in, 16)
            sp.dma_start(gate_w[:, :, :, :], d["gate_w"]).then_inc(gatew_in, 16)
            sp.wait_ge(wlo_done, 2)
            load_w(3, 1)
            with sp.Fori(0, 4) as i:
                for u in range(2):
                    sp.wait_ge(wlo_done, i * 2 + (3 + u))
                    load_w(i * 2 + (4 + u), u)
            sp.wait_ge(kv_done, 2)
            sp.dma_start(d["o_kv"], kv[:, :, :]).then_inc(kv_stored, 16)
            for j in range(3):
                sp.wait_ge(z_used, 3 * (T_XB + j + 1))
                sp.dma_start(d["o_conv"][:, j, :], zT[:, 2 + j, NT - 3:TT]).then_inc(conv_stored, 16)
            sp.dma_start(d["o_st"], pc("st_conv", 0, 72)).then_inc(h_stored, 16)
            for m in (12, 13, 14, 15):
                sp.wait_ge(wlo_done, m - 1)
                load_w(m, m % 2)
            sp.wait_ge(vt_done, 9)
            for n in range(6):
                load_cache(n)
            sp.wait_ge(wlo_done, 15)
            load_w(16, 0)
            load_cache(6)
            load_cache(7)
            sp.wait_ge(vn_done, 3)
            sp.dma_start(d["o_vs"], v_tok[P - NS:P, 8, :]).then_inc(vs_stored, 16)
            sp.wait_ge(wlo_done, 16)
            load_w(17, 1)
            for n in range(8, 14):
                load_cache(n)
            sp.wait_ge(wlo_done, 17)
            load_w(18, 0)
            sp.wait_ge(mT_done, 9)
            sp.wait_ge(a_done, 9)

            def load_wo(n):
                dst, _ = wo_source(n)
                sp.dma_start(dst, d["w_out"][K_ORDER[n]]).then_inc(wo_in[n], 16)

            for n in range(2, 6):
                load_wo(n)
            sp.wait_ge(wlo_done, 18)
            load_wo(1)
            sp.wait_ge(wlo_done, 19)
            load_wo(0)
            load_cache(14)
            load_cache(15)
            sp.wait_ge(scan_done, 6)
            load_wo(6)
            sp.wait_ge(placed, 6)
            sp.dma_start(d["o_h"], h_last[:, :, :]).then_inc(h_stored, 16)
            def load_x(c0, slot):
                sp.dma_start(x_ring[:, slot, 0:DM], d["x_all"][bass.ds(c0, P), :]).then_inc(x_in[slot], 16)

            sp.wait_ge(b_done, 3)
            load_x(0, 1)
            load_x(P, 0)
            sp.wait_ge(cache_read, 2 * NS)
            sp.dma_start(g_post, d["g_post"].partition_broadcast(P)).then_inc(gpost_in, 16)
            sp.wait_ge(wo_done, 1)
            load_wo(7)
            with sp.Fori(0, 3) as i:
                for v in range(2):
                    u = 1 - v
                    sp.wait_ge(y_ready, i * 2 + (v + 1))
                    sp.dma_start(d["o_y"][bass.ds(i * (2 * P) + v * P, P), :], y_out[:, u, :]).then_inc(y_stored[u], 16)
                    load_x(i * (2 * P) + (2 + v) * P, u)
            for c in (6, 7):
                sp.wait_ge(y_ready, c + 1)
                sp.dma_start(d["o_y"][c * P:(c + 1) * P, :], y_out[:, 1 - c % 2, :]).then_inc(y_stored[1 - c % 2], 16)
                if c == 6:
                    load_x(LASTC, 1)
            for n in range(2):
                half = slice(n * 512, (n + 1) * 512)
                sp.wait_ge(y_last, n + 1)
                sp.dma_start(d["o_y"][NT:TT, half], y_out[P - NS:P, 1, half]).then_inc(y_stored[n], 16)
            sp.wait_ge(y_stored[0], 16 * 5)
            sp.wait_ge(y_stored[1], 16 * 5)
            sp.wait_ge(kv_stored, 16)
            sp.wait_ge(conv_stored, 48)
            sp.wait_ge(h_stored, 32)
            sp.wait_ge(vs_stored, 16)

        @block.tensor
        def _(pe):
            def parts(g, slot, k, cols):
                wk = slice(k * P, (k + 1) * P)
                for n, (w, x) in enumerate(((w_hi, x_hi), (w_hi, x_lo), (w_lo, x_hi))):
                    last = pe.matmul(ps[:, g, 0:GN], w[:, slot, wk], x[:, k, cols],
                                     start=(k == 0 and n == 0), stop=(k == KT - 1 and n == 2))
                return last

            def gemm(m, g, slot):
                if g == 0:
                    pe.wait_ge(wlo_done, m + 1)
                pe.wait_ge(z_used, m * 3 + (g - 2))
                for k in range(KT):
                    last = parts(g, slot, k, slice(g * GN, (g + 1) * GN))
                last.then_inc(z_done, 1)

            pe.wait_ge(wlo_done, 1)
            for k in range(KT):
                pe.wait_ge(xlo_done, k + 1)
                for g in range(NG):
                    last = parts(g, 0, k, slice(g * GN, (g + 1) * GN))
                    if k == KT - 1:
                        last.then_inc(z_done, 1)
            for g in range(NG):
                gemm(1, g, 1)
            for k in range(KT):
                pe.wait_ge(memg_done, k // 2 + 1)
                pe.wait_ge(wm_in[k // 2], 16)
                for mt in range(MT):
                    last = pe.matmul(ps[:, 3 + mt, :], memT[:, k, mt * P:(mt + 1) * P], w_mem[:, k, :],
                                     start=(k == 0), stop=(k == KT - 1))
            last.then_inc(kvp_done, 1)
            for g in range(NG):
                gemm(2, g, 0)
            pe.wait_ge(rep_done, 2)
            pe.wait_ge(const_set, 1)
            for c in range(9):
                src = probs[:, c * P:(c + 1) * P] if c < NCH else probsT[:, 0:P]
                last = pe.transpose(ps[:, 5 + c // 4, (c % 4) * P:(c % 4 + 1) * P], src, ident[:, :])
                if c >= 7:
                    last.then_inc(rstdp_done, 1)
            gemm(3, 0, 1)
            pe.wait_ge(kv_done, 2)
            pe.wait_ge(rstdB_done, 3)
            for t in range(2):
                for mt in range(MT):
                    last = pe.transpose(ps[:, 5, t * NM + mt * P:t * NM + (mt + 1) * P],
                                        kv[:, mt, t * P:(t + 1) * P], ident[:, :])
            last.then_inc(kTp_done, 1)
            gemm(3, 1, 1)
            gemm(3, 2, 1)

            pe.wait_ge(kT_done, 1)
            with pe.Fori(0, 4) as i:
                for u in range(2):
                    m, s = i * 2 + (ATT0 + u), i * 2 + u
                    pe.wait_ge(qc_done, s + 1)
                    for t in range(2):
                        for hh in range(2):
                            rows_h = slice(hh * HD, (hh + 1) * HD)
                            last = pe.matmul(ps[:, 3 + hh, t * NM:(t + 1) * NM], q_chunk[rows_h, u, t, :],
                                             kT[rows_h, t, :], start=True, stop=True)
                            if t == 1:
                                last.then_inc(sc_done, 1)
                    gemm(m, 0, u)
                    for b in range(2):
                        pe.wait_ge(p_done, s * 4 + (2 + 2 * b))
                        for n in range(4):
                            last = pe.transpose(ps[:, 5 + b, n * P:(n + 1) * P],
                                                probs[:, (4 * b + n) * P:(4 * b + n + 1) * P], ident[:, :])
                        last.then_inc(pTp_done, 1)
                    gemm(m, 1, u)
                    pe.wait_ge(pTa_done, s + 1)
                    pe.wait_ge(pTb_done, s + 1)
                    for h in range(NH):
                        for mt in range(MT):
                            n = 2 * h + mt
                            last = pe.matmul(ps[:, 7, h * HD:(h + 1) * HD], probsT[:, n * P:(n + 1) * P],
                                             kv[:, mt, 256 + h * HD:256 + (h + 1) * HD],
                                             start=(mt == 0), stop=(mt == 1))
                    last.then_inc(pv_done, 1)
                    gemm(m, 2, u)
                    pe.wait_ge(attn_done, s + 1)
                    for t in range(2):
                        last = pe.transpose(ps[:, 7, 256 + t * P:256 + (t + 1) * P],
                                            attn[:, t * P:(t + 1) * P], ident[:, :])
                    last.then_inc(attnT_done, 1)

            def gates(j, g):
                for gate in range(2):
                    n = (j * 3 + g) * 2 + gate
                    if n >= 3:
                        pe.wait_ge(gate_used, n - 2)
                    pairs = [(x, kin) for x, (kin, out) in enumerate(GATE_PAIRS) if out == j]
                    if n == 8:
                        pe.wait_ge(sp_exp, 1)
                    cols, bank = slice(g * GN, (g + 1) * GN), 3 + n % 3
                    x = GATE_PAIRS.index((j, j))
                    last = pe.matmul(ps[:, bank, 0:GN], gate_w[:, gate, x, :], mixT[:, 3 + j, cols],
                                     start=True, stop=True)
                    for x, kin in pairs:
                        if kin != j:
                            r, c = (slice(96, 128), slice(0, 32)) if kin < j else (slice(0, 32), slice(96, 128))
                            last = pe.matmul(ps[c, bank, 0:GN], gate_w[r, gate, x, c], mixT[r, 3 + kin, cols],
                                             start=False, stop=True, skip_group_check=True)
                    last.then_inc(gate_done, 1)

            def col0(c):
                return min(c * P, LASTC)

            pe.wait_ge(conv_done, 3)
            pe.wait_ge(gatew_in, 16)
            pe.wait_ge(p_done, 32)
            pe.wait_ge(pTa_done, 8)
            pe.wait_ge(pTb_done, 8)
            pe.wait_ge(c_done, 8)
            for g in range(NG):
                gemm(12, g, 0)
                gates(0, g)
                for c in range(3 * g, 3 * g + 3):
                    if c >= 2:
                        pe.wait_ge(vt_used, c - 1)
                    for j in range(3):
                        last = pe.transpose(ps[:, 6 + c % 2, j * P:(j + 1) * P],
                                            zT[:, 5 + j, col0(c):col0(c) + P], ident[:, :])
                    last.then_inc(vt_done, 1)
            def sample_scores(n):
                pe.wait_ge(c_in[n % 6], 16 * (n // 6 + 1))
                for mt in range(MT):
                    for t in range(2):
                        last = pe.matmul(ps[:, 5, mt * 32 + n * NH:mt * 32 + (n + 1) * NH],
                                         cache_ring[:, n % 6, t * NM + mt * P:t * NM + (mt + 1) * P],
                                         qb[:, t, n, :], start=(t == 0), stop=(t == 1))
                last.then_inc(cache_read, 1)

            def sample_values(n):
                part = NS + n
                pe.wait_ge(c_in[part % 6], 16 * (part // 6 + 1))
                for t in range(2):
                    at = (t * NS + n) * NH
                    for mt in range(MT):
                        last = pe.matmul(ps[:, 7, at:at + NH],
                                         cache_ring[:, part % 6, mt * NM + t * P:mt * NM + (t + 1) * P],
                                         pT_s[:, mt, n * NH:(n + 1) * NH], start=(mt == 0), stop=(mt == 1))
                last.then_inc(cache_read, 1)

            pe.wait_ge(qb_done, 4)
            for g in range(NG):
                gemm(13, g, 1)
                pe.wait_ge(gate_used, 6)
                for n in range(3 * g, min(3 * g + 3, NS)):
                    sample_scores(n)
            pe.wait_ge(w_masked, 1)
            for g in range(NG):
                gemm(14, g, 0)
                if g == 0:
                    pe.wait_ge(s1c_done, 1)
                    for mt in range(MT):
                        last = pe.matmul(ps[0:32, 5, mt * P:(mt + 1) * P], sT_s[:, mt * 32:(mt + 1) * 32],
                                         ident[:, :], start=True, stop=True)
                    last.then_inc(s2_done, 1)
                gates(1, g)
                for c in range(3 * g, 3 * g + 3):
                    if c < NCH:
                        pe.wait_ge(vn_done, c // 4 + 1)
                        pe.wait_ge(vt_used if c < 2 else mix_done, 9 if c < 2 else c - 1)
                        for h in range(AH):
                            last = pe.matmul(ps[:, 6 + c % 2, h * AD:(h + 1) * AD], wsT[:, h, :],
                                             v_tok[:, c, h * AD:(h + 1) * AD], start=True, stop=True)
                        last.then_inc(sp_done, 1)
            for g in range(NG):
                gemm(15, g, 1)
                if g == 1:
                    pe.wait_ge(sp_norm, 1)
                    pe.wait_ge(gate_used, 12)
                    for mt in range(MT):
                        last = pe.matmul(ps[:, 5, mt * 32:(mt + 1) * 32], p_s[:, mt * P:(mt + 1) * P],
                                         ident[0:32, 0:32], start=True, stop=True)
                    last.then_inc(s3_done, 1)
                for c in range(3 * g, 3 * g + 3):
                    pe.wait_ge(mix_done, 9)
                    if c >= 2:
                        pe.wait_ge(a_done, c - 1)
                    for j in range(3):
                        last = pe.transpose(ps[:, 6 + c % 2, j * P:(j + 1) * P],
                                            v_tok[:, c, j * P:(j + 1) * P], ident[:, :])
                    last.then_inc(mT_done, 1)
            pe.wait_ge(s3c_done, 1)
            for g in range(NG):
                gemm(16, g, 0)
                gates(2, g)
            pe.wait_ge(a_done, 9)
            for g, samples in enumerate(((0, 1), (2,), (3, 4), (5,), (6,), (7,))):
                gemm(17 + g // 3, g % 3, 1 - g // 3)
                for n in samples:
                    sample_values(n)

            def project(c, u, first=False):
                pe.wait_ge(o_done, c + 1)
                for x, k in enumerate(K_ORDER):
                    if first:
                        pe.wait_ge(wo_done, x + 1)
                    for n in range(2):
                        last = product(u, k, n, x)
                last.then_inc(y_done, 1)

            def product(u, k, n, x):
                ok, cols = slice(k * P, (k + 1) * P), slice(n * 512, (n + 1) * 512)
                for part, (o, w) in enumerate(((o_hi, wo_hi), (o_hi, wo_lo), (o_lo, wo_hi))):
                    last = pe.matmul(ps[:, 2 * u + n, :], o[:, u, ok], w[:, k, cols],
                                     start=(x == 0 and part == 0), stop=(x == KT - 1 and part == 2))
                return last

            pe.wait_ge(z_used, 3 * N_TILES)
            pe.wait_ge(gate_used, 18)
            project(0, 1, first=True)
            project(1, 0)
            with pe.Fori(0, 3) as i:
                for v in range(2):
                    pe.wait_ge(y_used, i * 2 + (v + 1))
                    project(i * 2 + (v + 2), 1 - v)
            pe.wait_ge(y_used, 7)
            pe.wait_ge(o_done, 9)
            for n in range(2):
                for x, k in enumerate(K_ORDER):
                    last = product(1, k, n, x)
                last.then_inc(y_half, 1)

        @block.scalar
        def _(act):
            own = Tally(act, act_own)

            def split_w(m, slot, arrived):
                act.wait_ge(w_in[slot], arrived)
                if not isinstance(m, int) or m >= 2:
                    act.wait_ge(z_done, m * 3 + (-3))
                act.activation(w_hi[:, slot, :], w_stage[:, slot, :], ACT.Copy).then_inc(whi_done, 1)

            def split_tile(m):
                split_w(m, m % 2, 16 * (m // 2 + 1))

            act.wait_ge(lam_done, 1)
            act.activation(lt[:, 1, :], lt[:, 0, :], ACT.Exp, scale=-1.0).then_inc(elam_done, 1)
            split_tile(0)
            act.wait_ge(par_in, 16)
            for k in range(KT):
                if k == 6:
                    split_tile(1)
                act.wait_ge(xT_in[k], 16)
                act.activation(x_hi[:, k, :], mixT[:, k, :], ACT.Copy, scale=pc("g_pre", k)).then_inc(xhi_done, 1)
            act.wait_ge(memn_in, 16)
            for mt in range(MT):
                own.link(act.activation(probsT[:, 0:DM], mem_nat[:, mt, :], ACT.Square, accum_out=ssq[:, 9 + mt:10 + mt]))
            for c in range(9):
                act.wait_ge(x_in[c % 2], 16 * (c // 2 + 1))
                if c:
                    act.wait_ge(xsq_done, c)
                act.activation(probsT[:, 0:DM], x_ring[:, c % 2, 0:DM], ACT.Square,
                               accum_out=ssq[:, c:c + 1]).then_inc(xsq_done, 1)
                if c == 3:
                    split_tile(2)
            split_tile(3)
            act.wait_ge(ms_done, 1)
            act.activation(rstd[:, :], ssq[:, :], ACT.Sqrt).then_inc(root_done, 1)
            act.wait_ge(kvp_done, 1)
            act.wait_ge(rep_done, 1)
            for mt in range(MT):
                act.activation(kv[:, mt, :], ps[:, 3 + mt, :], ACT.Copy, scale=rstd[:, 9 + mt:10 + mt]).then_inc(kv_done, 1)
            for b, (a, n) in enumerate(((0, 512), (0, 512), (P - NS, NS))):
                act.wait_ge(rstdp_done, 1 + b // 2)
                act.activation(rstdB[:, b * 512:b * 512 + n], ps[:, 5 + b, a:a + n], ACT.Copy).then_inc(rstdB_done, 1)
            act.wait_ge(kTp_done, 1)
            act.activation(kT[:, :, :].rearrange("p a b -> p (a b)"), ps[:, 5, :], ACT.Copy).then_inc(kT_done, 1)
            split_tile(4)
            for j, sig in enumerate((probs, probsT)):
                act.wait_ge(q_done, 3)
                act.wait_ge(z_used, 3 * (T_GC + j + 1))
                act.activation(sig[:, :], mixT[:, 6 + j, :], ACT.Sigmoid).then_inc(gcsig_done, 1)
            act.wait_ge(gc_done, 2)

            with act.Fori(0, 4) as i:
                for u in range(2):
                    m, s = i * 2 + (ATT0 + u), i * 2 + u
                    split_w(m + 1, 1 - u, i * 16 + 16 * (3 + u))
                    act.wait_ge(negm_done, s + 1)
                    for h in range(NH):
                        t, hh = h // 2, h % 2
                        n = hh * 2 + t
                        act.activation(probs[:, h * NM:(h + 1) * NM], ps[:, 3 + hh, t * NM:(t + 1) * NM],
                                       ACT.Exp, bias=negm[:, n:n + 1], scale=HD ** -0.5,
                                       accum_out=sums[:, h:h + 1]).then_inc(p_done, 1)
                    act.wait_ge(pTp_done, s * 2 + 1)
                    act.activation(probsT[:, 0:512], ps[:, 5, :], ACT.Copy).then_inc(pTa_done, 1)

            def gate_sigmoids(j, g):
                for gate, (dst, bias) in enumerate(((s_r, "b_a"), (s_i, "b_x"))):
                    n = (j * 3 + g) * 2 + gate
                    act.wait_ge(gate_done, n + 1)
                    act.activation(dst[:, g * GN:(g + 1) * GN], ps[:, 3 + n % 3, 0:GN], ACT.Sigmoid,
                                   bias=pc(bias, j)).then_inc(gate_used, 1)

            def decay(j):
                act.wait_ge(gate_used, 6 * (j + 1))
                act.wait_ge(placed, 2 * j)
                act.activation(s_th, s_r, ACT.Tanh, scale=nsp[:, j:j + 1]).then_inc(decay_done, 1)
                act.activation(s_a2, s_r, ACT.Exp, scale=lt[:, 5, j:j + 1]).then_inc(decay_done, 1)
                act.wait_ge(decay_done, 3 * j + 2)
                act.activation(s_r, s_r, ACT.Exp, scale=nsp[:, j:j + 1]).then_inc(decay_done, 1)

            def place(j):
                act.wait_ge(scan_done, 2 * (j + 1))
                act.wait_ge(gate_done, 6 * min(j + 2, 3))
                act.wait_ge(ixc_done, j + 1)
                act.activation(mixT[:, 3 + j, :], s_th, ACT.Copy).then_inc(placed, 1)
                act.activation(h_last[:, j, :], s_th[:, NT - 1:TT], ACT.Copy).then_inc(placed, 1)

            def root_b(j):
                act.wait_ge(rest_done, j + 1)
                act.activation(s_th, s_th, ACT.Sqrt, scale=-1.0).then_inc(root_b_done, 1)

            split_tile(13)
            act.wait_ge(qc_done, NCH)
            for j in range(2):
                act.wait_ge(z_used, 3 * (T_GA + j + 1))
                act.activation(zT[:, 9 + j, :], mixT[:, j, :], ACT.Sigmoid).then_inc(gasig_done, 1)
            act.wait_ge(pTp_done, 16)
            act.wait_ge(qb_done, 4)
            act.wait_ge(conv_done, 3)
            act.wait_ge(conv_stored, 48)
            for g in range(NG):
                gate_sigmoids(0, g)
                for c in range(3 * g, 3 * g + 3):
                    act.wait_ge(vt_done, c + 1)
                    if c >= 4:
                        act.wait_ge(vsum_done, c - 3)
                    act.activation(v_sq[:, c % 4, :], ps[:, 6 + c % 2, 0:AW], ACT.Square).then_inc(vsq_done, 1)
                    act.activation(v_tok[:, c, :], ps[:, 6 + c % 2, 0:AW], ACT.Copy).then_inc(vt_used, 1)
            act.wait_ge(z_used, 3 * T_GB)
            act.wait_ge(pv_done, NCH)
            act.activation(s_th, mixT[:, 2, :], ACT.Sigmoid).then_inc(gasig_done, 1)
            split_tile(14)
            act.wait_ge(vms_done, 1)
            act.activation(rstdv[:, :], ssv[:, :], ACT.Sqrt).then_inc(vroot_done, 1)
            act.wait_ge(vsum_done, 9)
            act.wait_ge(ga_done, 3)
            act.wait_ge(nsp_done, 1)
            decay(0)
            root_b(0)
            act.wait_ge(cache_read, NS)
            act.activation(sT_s, ps[:, 5, 0:64], ACT.Copy).then_inc(s1c_done, 1)
            split_tile(15)
            act.wait_ge(scan_done, 2)
            gate_sigmoids(1, 0)
            act.wait_ge(snegm_done, 1)
            act.wait_ge(kv_stored, 16)
            act.activation(p_s, ps[0:32, 5, 0:NM], ACT.Exp, bias=sst[:, 1:2], scale=HD ** -0.5,
                           accum_out=sst[:, 2:3]).then_inc(sp_exp, 1)
            gate_sigmoids(1, 1)
            gate_sigmoids(1, 2)
            place(0)
            split_tile(16)
            decay(1)
            root_b(1)
            act.wait_ge(s3_done, 1)
            act.activation(kT[:, 1, 0:64], ps[:, 5, 0:64], ACT.Copy).then_inc(s3c_done, 1)
            split_tile(17)
            for g in range(NG):
                act.wait_ge(z_used, 3 * (T_GB + g + 1))
                act.wait_ge(gbm_done, g)
                act.activation(s_sig, zT[:, 8 + g, :], ACT.Sigmoid).then_inc(gbsig_done, 1)
                act.wait_ge(scan_done, 4)
                gate_sigmoids(2, g)
            place(1)
            split_tile(18)
            decay(2)
            root_b(2)
            place(2)

            def split_o(c0, slot):
                act.activation(o_hi[:, slot, :].rearrange("p (k n) -> p k n", k=KT),
                               mixT[:, :, bass.ds(c0, P)], ACT.Copy).then_inc(ohi_done, 1)

            def y_stats(c, u):
                act.wait_ge(y_done, c + 1)
                if not isinstance(c, int) or c > 0:
                    act.wait_ge(ysq_done, c)
                act.activation(probs[:, 0:DM].rearrange("p (a b) -> p a b", a=2), ps[:, 2 * u:2 * u + 2, :],
                               ACT.Square, accum_out=sy[:, u:u + 1]).then_inc(ysq_done, 1)
                act.wait_ge(yms_done, c + 1)
                act.activation(ry[:, u:u + 1], sy[:, u:u + 1], ACT.Sqrt).then_inc(yroot_done, 1)

            act.wait_ge(z_done, 3 * (N_TILES - 1))
            act.wait_ge(c_done, NCH)
            act.wait_ge(b_done, 3)
            act.wait_ge(z_used, 3 * (N_TILES - 1) + 1)
            split_o(0, 1)
            act.wait_ge(z_done, 3 * N_TILES)
            for n, k in enumerate(K_ORDER):
                act.wait_ge(wo_in[n], 16)
                act.activation(wo_hi[:, k, 0:DM], wo_source(n)[0], ACT.Copy).then_inc(wohi_done, 1)
            act.wait_ge(z_used, 3 * N_TILES)
            act.wait_ge(cs_done, 4)
            split_o(P, 0)
            y_stats(0, 1)
            with act.Fori(0, 3) as i:
                for v in range(2):
                    act.wait_ge(y_done, i * 2 + (v + 1))
                    act.wait_ge(o_done, i * 2 + (v + 1))
                    split_o(i * (2 * P) + (v + 2) * P, 1 - v)
                    y_stats(i * 2 + (v + 1), v)
            act.wait_ge(y_done, 7)
            split_o(LASTC, 1)
            y_stats(7, 0)
            for n in range(2):
                act.wait_ge(y_half, n + 1)
                act.activation(probs[:, n * 512:(n + 1) * 512], ps[:, 2 + n, :], ACT.Square,
                               accum_out=sy[:, 2 + n:3 + n]).then_inc(ysq_half, 1)
            act.wait_ge(yms_done, 9)
            act.activation(ry[:, 1:2], sy[:, 1:2], ACT.Sqrt).then_inc(yroot_done, 1)

        @block.gpsimd
        def _(pool):
            own = Tally(pool, pool_own)

            def low_w(m, slot):
                pool.wait_ge(whi_done, m + 1)
                pool.tensor_tensor(w_lo[:, slot, :], w_stage[:, slot, :], w_hi[:, slot, :].bitcast(F),
                                   ALU.subtract).then_inc(wlo_done, 1)

            own.link(pool.memset(ident[:, :], 0.0))
            pool.affine_select(out=ident[:, :], in_=ident[:, :], compare_op=ALU.not_equal, fill=1.0, base=0,
                               pattern=[[-1, P]], channel_multiplier=1).then_inc(const_set, 1)
            pool.memset(qb[:, :, :, :], 0.0).then_inc(const_set, 1)
            pool.wait_ge(wlo_done, 1)
            low_w(1, 1)
            low_w(2, 0)
            low_w(3, 1)
            pool.wait_ge(wsT_in, 16)
            pool.affine_select(out=wsT[:, :, :], in_=wsT[:, :, :], compare_op=ALU.is_ge, fill=0.0, base=0,
                               pattern=[[0, AH], [1, P]], channel_multiplier=-1).then_inc(w_masked, 1)
            low_w(4, 0)
            pool.wait_ge(q_done, 3)
            with pool.Fori(0, 4) as i:
                for u in range(2):
                    m, s = i * 2 + (ATT0 + u), i * 2 + u
                    pool.tensor_copy(q_chunk[:, u, :, :], zT[:, 0:2, bass.ds(i * (2 * P) + u * P, P)]).then_inc(qc_done, 1)
                    low_w(m + 1, 1 - u)

            def keep_xc(j):
                pool.wait_ge(gate_used, 6 * (j + 1))
                pool.tensor_tensor(s_i, s_i, mixT[:, 3 + j, :], ALU.mult).then_inc(ixc_done, 1)

            low_w(13, 1)
            low_w(14, 0)
            keep_xc(0)
            pool.wait_ge(rows_in, 16)
            for q, (c0, n) in enumerate(((0, 4), (4, 4), (8, 1))):
                pool.wait_ge(vr_done, q + 1)
                pool.tensor_tensor(v_tok[:, c0:c0 + n, :], v_tok[:, c0:c0 + n, :],
                                   rows[:, 0:AW].unsqueeze(1).broadcast_to([P, n, AW]), ALU.mult).then_inc(vn_done, 1)
            low_w(15, 1)
            for j in range(3):
                pool.wait_ge(ga_done, j + 1)
                pool.tensor_tensor(mixT[:, j, :], mixT[:, j, :], rstdB[:, :], ALU.mult).then_inc(gar_done, 1)
            low_w(16, 0)
            keep_xc(1)
            low_w(17, 1)
            low_w(18, 0)
            keep_xc(2)

            def low_o(c0, slot):
                pool.tensor_tensor(o_lo[:, slot, :].rearrange("p (k n) -> p k n", k=KT),
                                   mixT[:, :, bass.ds(c0, P)],
                                   o_hi[:, slot, :].bitcast(F).rearrange("p (k n) -> p k n", k=KT),
                                   ALU.subtract).then_inc(o_done, 1)

            def add_x(c, u, arrived):
                pool.wait_ge(y_used, c + 1)
                pool.wait_ge(x_in[u], arrived)
                pool.tensor_tensor(y_out[:, u, :], y_out[:, u, :], x_ring[:, u, 0:DM], ALU.add).then_inc(y_ready, 1)

            pool.wait_ge(ohi_done, 1)
            low_o(0, 1)
            pool.wait_ge(ohi_done, 2)
            low_o(P, 0)
            add_x(0, 1, 16 * 5)
            with pool.Fori(0, 3) as i:
                for v in range(2):
                    pool.wait_ge(ohi_done, i * 2 + (v + 3))
                    low_o(i * (2 * P) + (v + 2) * P, 1 - v)
                    add_x(i * 2 + (v + 1), v, i * 16 + 16 * 6)
            pool.wait_ge(ohi_done, 9)
            low_o(LASTC, 1)
            add_x(7, 0, 16 * 9)

        @block.vector
        def _(dve):
            own = Tally(dve, dve_own)

            def evac(m, g, dst):
                dve.wait_ge(z_done, m * 3 + (g + 1))
                dve.tensor_tensor(dst, ps[:, g, 0:GN], rstdB[:, g * GN:(g + 1) * GN], ALU.mult).then_inc(z_used, 1)

            def raw(m, g, dst):
                dve.wait_ge(z_done, m * 3 + (g + 1))
                dve.tensor_copy(dst, ps[:, g, 0:GN]).then_inc(z_used, 1)

            def grp(g):
                return slice(g * GN, (g + 1) * GN)

            dve.wait_ge(par_in, 16)
            own.link(dve.tensor_scalar(lt[:, 2, :], pc("lam", 0, 3), -1.0, None, ALU.mult))
            dve.tensor_tensor(lt[:, 0, :], pc("lam", 0, 3), lt[:, 2, :], ALU.max).then_inc(lam_done, 1)
            dve.wait_ge(whi_done, 1)
            dve.tensor_tensor(w_lo[:, 0, :], w_stage[:, 0, :], w_hi[:, 0, :].bitcast(F),
                              ALU.subtract).then_inc(wlo_done, 1)
            for k in range(KT):
                dve.wait_ge(xhi_done, k + 1)
                dve.scalar_tensor_tensor(x_lo[:, k, :], mixT[:, k, :], pc("g_pre", k), x_hi[:, k, :].bitcast(F),
                                         ALU.mult, ALU.subtract).then_inc(xlo_done, 1)
            for g in range(NG):
                raw(0, g, zT[:, 0, grp(g)])
            for i in range(4):
                kk = slice(2 * i, 2 * i + 2)
                dve.wait_ge(memT_in[i], 16)
                dve.tensor_tensor(memT[:, kk, :], memT[:, kk, :],
                                  pc("g_mem", 2 * i, 2).unsqueeze(2).broadcast_to([P, 2, NM]), ALU.mult).then_inc(memg_done, 1)
            for g in range(NG):
                raw(1, g, zT[:, 1, grp(g)])
            dve.wait_ge(elam_done, 1)
            own.link(dve.tensor_scalar(lt[:, 3, :], lt[:, 1, :], 2.0, None, ALU.add))
            own.link(dve.reciprocal(lt[:, 4, :], lt[:, 3, :]))
            own.link(dve.tensor_tensor(lt[:, 3, :], lt[:, 4, :], lt[:, 1, :], ALU.mult))
            own.link(dve.tensor_tensor(lt[:, 4, :], lt[:, 3, :], lt[:, 3, :], ALU.mult))
            own.link(dve.tensor_scalar(lt[:, 5, :], lt[:, 4, :], 1.0 / 17, None, ALU.mult))
            for n in range(15, 2, -2):
                own.link(dve.scalar_tensor_tensor(lt[:, 5, :], lt[:, 5, :], 1.0 / n, lt[:, 4, :], ALU.add, ALU.mult))
            own.link(dve.scalar_tensor_tensor(lt[:, 5, :], lt[:, 5, :], 1.0, lt[:, 3, :], ALU.add, ALU.mult))
            own.link(dve.tensor_scalar(lt[:, 2, :], lt[:, 2, :], 0.0, -LRU_C, ALU.max, ALU.mult))
            own.link(dve.scalar_tensor_tensor(nsp[:, :], lt[:, 5, :], -2.0 * LRU_C, lt[:, 2, :], ALU.mult, ALU.add))
            dve.tensor_scalar(lt[:, 5, :], nsp[:, :], 2.0, None, ALU.mult).then_inc(nsp_done, 1)
            dve.wait_ge(xsq_done, 9)
            dve.wait_ge(act_own, 2)
            dve.tensor_scalar(ssq[:, :], ssq[:, :], 1.0 / DM, EPS, ALU.mult, ALU.add).then_inc(ms_done, 1)
            dve.wait_ge(root_done, 1)
            own.link(dve.reciprocal(rstd[:, :], rstd[:, :]))
            dve.tensor_copy(probs[:, 0:NT].rearrange("p (c n) -> p c n", c=NCH),
                            rstd[:, 0:NCH].unsqueeze(2).broadcast_to([P, NCH, P])).then_inc(rep_done, 1)
            dve.tensor_copy(probsT[:, 0:P], rstd[:, 8:9].broadcast_to([P, P])).then_inc(rep_done, 1)
            for g in range(NG):
                raw(2, g, mixT[:, 6, grp(g)])
            dve.wait_ge(rstdB_done, 3)
            dve.wait_ge(z_used, 9)
            for tile in (mixT[:, 6, :], zT[:, 0, :], zT[:, 1, :]):
                dve.tensor_tensor(tile, tile, rstdB[:, :], ALU.mult).then_inc(q_done, 1)
            for g in range(NG):
                evac(3, g, mixT[:, 7, grp(g)])
            dve.wait_ge(const_set, 2)
            dve.wait_ge(q_done, 3)
            for t in range(2):
                for hh in range(2):
                    r = slice(hh * HD, (hh + 1) * HD)
                    dve.tensor_copy(qb[r, t, :, 2 * t + hh], zT[r, t, NT:TT]).then_inc(qb_done, 1)
            for j, sig in enumerate((probs, probsT)):
                dve.wait_ge(gcsig_done, j + 1)
                dve.tensor_tensor(mixT[:, 6 + j, :], mixT[:, 6 + j, :], sig[:, :], ALU.mult).then_inc(gc_done, 1)
            dve.wait_ge(gc_done, 2)

            def attend(m, s, c0, dst, between=(None,) * 3):
                for hh in range(2):
                    dve.wait_ge(sc_done, s * 2 + (hh + 1))
                    own.mark(dve.tensor_reduce(mx[:, 2 * hh:2 * hh + 2],
                                               ps[:, 3 + hh, :].rearrange("p (t n) -> p t n", t=2), AX.X, ALU.max))
                own.wait()
                dve.tensor_scalar(negm[:, :], mx[:, :], -HD ** -0.5, None, ALU.mult).then_inc(negm_done, 1)
                if between[0]:
                    between[0]()
                evac(m, 0, dst(0))
                dve.wait_ge(pTp_done, s * 2 + 2)
                dve.tensor_copy(probsT[:, 512:1024], ps[:, 6, :]).then_inc(pTb_done, 1)
                dve.wait_ge(p_done, s * 4 + 4)
                own.link(dve.reciprocal(rsum[:, :], sums[:, :]))
                if between[1]:
                    between[1]()
                evac(m, 1, dst(1))
                dve.wait_ge(pv_done, s + 1)
                dve.tensor_tensor(attn[:, :].rearrange("p (h n) -> p h n", h=NH),
                                  ps[:, 7, 0:256].rearrange("p (h n) -> p h n", h=NH),
                                  rsum[:, :].unsqueeze(2).broadcast_to([P, NH, HD]), ALU.mult).then_inc(attn_done, 1)
                if between[2]:
                    between[2]()
                evac(m, 2, dst(2))
                dve.wait_ge(attnT_done, s + 1)
                cols = mixT[:, 6:8, bass.ds(c0, P)]
                dve.tensor_tensor(cols, ps[:, 7, 256:512].rearrange("p (t n) -> p t n", t=2), cols,
                                  ALU.mult).then_inc(c_done, 1)

            def convolve(j):
                xb, xc = zT[:, 2 + j, :], mixT[:, 3 + j, :]

                def tap(back):
                    w = pc("w_conv", 4 * j + 3 - back)
                    own.mark(dve.scalar_tensor_tensor(xc[:, back:NT], xb[:, 0:NT - back], w, xc[:, back:NT],
                                                      ALU.mult, ALU.add))
                    return dve.scalar_tensor_tensor(xc[:, NT:TT], pc("st_conv", 24 * j + 8 * (3 - back), 8), w,
                                                    xc[:, NT:TT], ALU.mult, ALU.add)

                def first():
                    dve.wait_ge(z_used, 3 * (T_XB + j + 1))
                    own.link(dve.tensor_scalar(xc, xb, pc("w_conv", 4 * j + 3), pc("b_conv", j), ALU.mult, ALU.add))
                    own.mark(tap(1))

                def second():
                    own.wait()
                    own.mark(tap(2))

                def third():
                    own.wait()
                    tap(3).then_inc(conv_done, 1)

                return first, second, third

            base = own.k
            per = 3
            own.base, own.k = base, 0
            with dve.Fori(0, 3) as i:
                own.base, own.k = i * per + base, 0
                attend(i + ATT0, i, i * P,
                       lambda g: zf[:, bass.ds(i * TT + (2 * TT + g * GN), GN)])
                assert own.k == per
            own.base, own.k = base + 3 * per, 0
            for m in (7, 8, 9):
                attend(m, m - ATT0, (m - ATT0) * P, lambda g: zT[:, m - 2, grp(g)], convolve(m - 7))
            for m in (10, 11):
                attend(m, m - ATT0, (m - ATT0) * P, lambda g: mixT[:, m - 10, grp(g)])

            def gate_a(j):
                dve.wait_ge(gasig_done, j + 1)
                dve.tensor_tensor(mixT[:, j, :], mixT[:, j, :], (zT[:, 9, :], zT[:, 10, :], s_th)[j],
                                  ALU.mult).then_inc(ga_done, 1)

            def v_sums(c):
                dve.wait_ge(vsq_done, c + 1)
                dve.tensor_reduce(ssv[:, 4 * c:4 * c + 4], v_sq[:, c % 4, :].rearrange("p (h n) -> p h n", h=AH),
                                  AX.X, ALU.add).then_inc(vsum_done, 1)

            def rest(j):
                dve.wait_ge(decay_done, 3 * (j + 1))
                dve.scalar_tensor_tensor(s_th, s_a2, 1.0, s_th, ALU.add, ALU.mult).then_inc(rest_done, 1)

            def scan(j):
                dve.wait_ge(root_b_done, j + 1)
                dve.wait_ge(ixc_done, j + 1)
                own.link(dve.tensor_tensor(s_i, s_i, s_th, ALU.mult))
                dve.tensor_tensor_scan(s_th[:, 0:NT], s_r[:, 0:NT], s_i[:, 0:NT], 0.0, ALU.mult, ALU.add).then_inc(scan_done, 1)
                own.link(dve.tensor_tensor(s_th[:, NT:TT], s_r[:, NT:TT], pc("st_h", 8 * j, 8), ALU.mult))
                dve.tensor_tensor(s_th[:, NT:TT], s_th[:, NT:TT], s_i[:, NT:TT], ALU.add).then_inc(scan_done, 1)

            for g in range(NG):
                evac(12, g, mixT[:, 2, grp(g)])
                if g < 2:
                    gate_a(g)
                for c in range(3 * g, 3 * g + 3):
                    v_sums(c)
            dve.wait_ge(vsum_done, 9)
            dve.tensor_scalar(ssv[:, :], ssv[:, :], 1.0 / AD, EPS, ALU.mult, ALU.add).then_inc(vms_done, 1)
            gate_a(2)
            dve.wait_ge(vroot_done, 1)
            own.link(dve.reciprocal(rstdv[:, :], rstdv[:, :]))
            for q, (c0, n) in enumerate(((0, 4), (4, 4), (8, 1))):
                vv = v_tok[:, c0:c0 + n, :].rearrange("p c (h n) -> p (c h) n", h=AH)
                dve.tensor_tensor(vv, vv, rstdv[:, 16 * q:16 * q + 4 * n].unsqueeze(2).broadcast_to([P, 4 * n, AD]),
                                  ALU.mult).then_inc(vr_done, 1)
            evac(13, 0, zT[:, 8, grp(0)])
            rest(0)
            evac(13, 1, zT[:, 8, grp(1)])
            scan(0)
            evac(13, 2, zT[:, 8, grp(2)])
            for g in range(NG):
                evac(14, g, zT[:, 9, grp(g)])
                if g == 0:
                    dve.wait_ge(s2_done, 1)
                    own.link(dve.tensor_reduce(sst[:, 0:1], ps[0:32, 5, 0:NM], AX.X, ALU.max))
                    dve.tensor_scalar(sst[:, 1:2], sst[:, 0:1], -HD ** -0.5, None, ALU.mult).then_inc(snegm_done, 1)
                if g == 2:
                    dve.wait_ge(sp_exp, 1)
                    own.link(dve.reciprocal(sst[:, 3:4], sst[:, 2:3]))
                    dve.tensor_scalar(p_s, p_s, sst[:, 3:4], None, ALU.mult).then_inc(sp_norm, 1)
                for c in range(3 * g, 3 * g + 3):
                    vc = v_tok[:, c, :].rearrange("p (h n) -> p h n", h=AH)
                    if c < NCH:
                        dve.wait_ge(sp_done, c + 1)
                        dve.tensor_tensor(vc, ps[:, 6 + c % 2, 0:AW].rearrange("p (h n) -> p h n", h=AH),
                                          pc("b_s", 0, 4).unsqueeze(2).broadcast_to([P, AH, AD]), ALU.add).then_inc(mix_done, 1)
                    else:
                        dve.wait_ge(vn_done, 3)
                        dve.wait_ge(vs_stored, 16)
                        own.link(dve.tensor_tensor(vc, vc, rows[:, AW:AW + 4].unsqueeze(2).broadcast_to([P, AH, AD]), ALU.mult))
                        dve.tensor_tensor(vc, vc, rows[:, AW + 4:AW + 8].unsqueeze(2).broadcast_to([P, AH, AD]),
                                          ALU.add).then_inc(mix_done, 1)
            dve.wait_ge(gar_done, 3)
            for g in range(NG):
                evac(15, g, zT[:, 10, grp(g)])
                for c in range(3 * g, 3 * g + 3):
                    dve.wait_ge(mT_done, c + 1)
                    n, a = (P, 0) if c < NCH else (NS, P - NS)
                    dve.tensor_tensor(mixT[:, 0:3, c * P:c * P + n],
                                      ps[:, 6 + c % 2, 0:AW].rearrange("p (j n) -> p j n", j=3)[:, :, a:a + n],
                                      mixT[:, 0:3, c * P:c * P + n], ALU.mult).then_inc(a_done, 1)
            rest(1)
            scan(1)

            def times_u(m, g):
                out = mixT[:, m - T_U, grp(g)]
                dve.wait_ge(z_done, 3 * m + g + 1)
                dve.tensor_tensor(out, ps[:, g, 0:GN], out, ALU.mult).then_inc(z_used, 1)

            dve.wait_ge(a_done, 9)
            def close_b(j):
                dve.wait_ge(placed, 2 * (j + 1))
                dve.wait_ge(gbm_done, j + 1)
                dve.tensor_tensor(mixT[:, 3 + j, :], mixT[:, 3 + j, :], zT[:, 8 + j, :], ALU.mult).then_inc(b_done, 1)

            for g in range(NG):
                times_u(16, g)
                dve.wait_ge(gbsig_done, g + 1)
                dve.tensor_tensor(zT[:, 8 + g, :], zT[:, 8 + g, :], s_sig, ALU.mult).then_inc(gbm_done, 1)
            times_u(17, 0)
            close_b(0)
            rest(2)
            times_u(17, 1)
            close_b(1)
            times_u(17, 2)
            scan(2)
            close_b(2)
            for g in range(NG):
                times_u(18, g)
            dve.wait_ge(cache_read, 2 * NS)
            for t in range(2):
                for hh in range(2):
                    r = slice(hh * HD, (hh + 1) * HD)
                    got = ps[r, 7, t * 32:(t + 1) * 32].rearrange("p (n h) -> p n h", h=NH)[:, :, 2 * t + hh]
                    dve.tensor_tensor(mixT[r, 6 + t, NT:TT], got, mixT[r, 6 + t, NT:TT], ALU.mult).then_inc(cs_done, 1)
            for n, k in enumerate(K_ORDER):
                dve.wait_ge(wohi_done, n + 1)
                dve.tensor_tensor(wo_lo[:, k, 0:DM], wo_source(n)[0], wo_hi[:, k, 0:DM].bitcast(F),
                                  ALU.subtract).then_inc(wo_done, 1)
            dve.wait_ge(gpost_in, 16)

            def finish(c, u, stored):
                dve.wait_ge(ysq_done, c + 1)
                dve.tensor_scalar(sy[:, u:u + 1], sy[:, u:u + 1], 1.0 / DM, EPS, ALU.mult, ALU.add).then_inc(yms_done, 1)
                dve.wait_ge(yroot_done, c + 1)
                own.link(dve.reciprocal(ry[:, u:u + 1], ry[:, u:u + 1]))
                if not isinstance(stored, int) or stored:
                    dve.wait_ge(y_stored[u], stored)
                dve.scalar_tensor_tensor(y_out[:, u, :].rearrange("p (a b) -> p a b", a=2), ps[:, 2 * u:2 * u + 2, :],
                                         ry[:, u:u + 1], g_post.rearrange("p (a b) -> p a b", a=2),
                                         ALU.mult, ALU.mult).then_inc(y_used, 1)

            for c in range(2):
                finish(c, 1 - c, 0)
            base = own.base + own.k
            with dve.Fori(0, 3) as i:
                for v in range(2):
                    own.base, own.k = i * 2 + (base + v), 0
                    finish(i * 2 + (2 + v), 1 - v, i * 16 + 16)
            own.base, own.k = base + 6, 0
            dve.wait_ge(ysq_half, 2)
            own.link(dve.tensor_tensor(sy[:, 1:2], sy[:, 2:3], sy[:, 3:4], ALU.add))
            dve.tensor_scalar(sy[:, 1:2], sy[:, 1:2], 1.0 / DM, EPS, ALU.mult, ALU.add).then_inc(yms_done, 1)
            dve.wait_ge(yroot_done, 9)
            own.link(dve.reciprocal(ry[:, 1:2], ry[:, 1:2]))
            dve.wait_ge(y_stored[1], 16 * 4)
            dve.wait_ge(x_in[1], 16 * 9)
            for n in range(2):
                half = slice(n * 512, (n + 1) * 512)
                own.link(dve.scalar_tensor_tensor(y_out[:, 1, half], ps[:, 2 + n, :], ry[:, 1:2], g_post[:, half],
                                                  ALU.mult, ALU.mult))
                dve.tensor_tensor(y_out[:, 1, half], y_out[:, 1, half], x_ring[:, 1, half], ALU.add).then_inc(y_last, 1)


_OUTS = {"o_y": [TT, DM], "o_kv": [P, MT, 512], "o_conv": [P, 3, 3 + NS], "o_st": [P, 72],
         "o_h": [P, 3, 1 + NS], "o_vs": [NS, AW]}


def kernel(**inputs):
    import concourse.bacc as bacc
    from concourse.bass_utils import run_bass_kernel_spmd

    a = {k: np.asarray(v) for k, v in inputs.items()}

    def tiles(w):
        return w.reshape(-1, P, w.shape[-1]).transpose(1, 0, 2)

    def per_part(v):
        return v.reshape(-1, P).T

    x_all = np.concatenate([a["x_prompt"][0], a["x_sample"][:, 0]], axis=0)
    w_in = a["w_in"][0]
    cuts = {"u": 0, "v": AW, "ga": 2 * AW, "xb": 3 * AW, "gb": 4 * AW, "q": 5 * AW, "gc": 5 * AW + 256}
    order = [("q", 2), ("gc", 2), ("xb", 3), ("v", 3), ("ga", 3), ("gb", 3), ("u", 3)]
    cols = np.concatenate([w_in[:, cuts[n]:cuts[n] + P * t] for n, t in order], axis=1)
    w_tiles = cols.reshape(KT, P, N_TILES, P).transpose(2, 1, 0, 3).reshape(N_TILES, P, DM)
    st = a["state_conv"][0].transpose(2, 1, 0).reshape(3, P, 3, NS).transpose(1, 0, 2, 3).reshape(P, 72)
    sh = a["state_h"][0].T.reshape(3, P, NS).transpose(1, 0, 2).reshape(P, 24)
    wc = a["w_conv"][0].T.reshape(3, P, 4).transpose(1, 0, 2).reshape(P, 12)
    par = np.concatenate([per_part(a["g_pre"][0]), per_part(a["g_mem"][0]), wc, per_part(a["b_conv"][0]),
                          per_part(a["b_a"][0]), per_part(a["b_x"][0]), per_part(a["lru_lambda"][0]),
                          st, sh, a["b_s"][0].T], axis=1)
    gate_w = np.zeros((P, 2, len(GATE_PAIRS), P), np.float32)
    for n, name in enumerate(("w_a", "w_x")):
        full = np.zeros((AW, AW), np.float32)
        for b in range(8):
            full[48 * b:48 * b + 48, 48 * b:48 * b + 48] = a[name][0, b]
        for x, (kin, out) in enumerate(GATE_PAIRS):
            gate_w[:, n, x] = full[kin * P:(kin + 1) * P, out * P:(out + 1) * P]
    arrays = {
        "par": par,
        "memT": tiles(a["mem_prompt"][0].T),
        "w_mem": tiles(np.concatenate([a["w_mk"][0], a["w_mv"][0]], axis=1)),
        "w_tiles": w_tiles,
        "xT": tiles(x_all.T),
        "mem_nat": tiles(a["mem_prompt"][0]),
        "x_all": x_all,
        "rows": np.concatenate([a["g_v"][0], a["w_s"][0, :, 0, 0], a["b_s"][0, :, 0]]),
        "wsT": a["w_s"][0].transpose(2, 0, 1),
        "gate_w": gate_w,
        "kcT": a["cache_mem_k"][0].reshape(NS, NM, 2, P).transpose(0, 3, 2, 1).reshape(NS, P, 512),
        "vc": a["cache_mem_v"][0].reshape(NS, MT, P, 256).transpose(0, 2, 1, 3).reshape(NS, P, 512),
        "w_out": a["w_out"][0].reshape(KT, P, DM),
        "g_post": a["g_post"][0],
    }
    nc = bacc.Bacc("TRN2", target_bir_lowering=False, num_devices=1)
    d, feed = {}, {}
    for name, v in arrays.items():
        v = np.ascontiguousarray(v)
        feed["in_" + name] = v
        d[name] = nc.dram_tensor("in_" + name, list(v.shape), F, kind="ExternalInput").ap()
    for name, shape in _OUTS.items():
        d[name] = nc.dram_tensor(name, shape, F, kind="ExternalOutput").ap()
    build(nc, d)
    r = run_bass_kernel_spmd(nc, [feed], core_ids=[0]).results[0]
    y, kvo = r["o_y"], r["o_kv"].transpose(1, 0, 2).reshape(NM, 512)
    cv = r["o_conv"].transpose(1, 0, 2).reshape(AW, 3 + NS)
    stp = r["o_st"].reshape(P, 3, 3, NS).transpose(3, 2, 1, 0).reshape(NS, 3, AW)
    hh = r["o_h"].transpose(1, 0, 2).reshape(AW, 1 + NS)
    new_conv_s = np.concatenate([stp[:, 1:], cv[:, 3:].T[:, None]], axis=1)
    return (y[:NT][None], y[NT:][:, None],
            kvo[:, :256].reshape(1, 1, NM, NH, HD), kvo[:, 256:].reshape(1, 1, NM, NH, HD),
            np.ascontiguousarray(cv[:, :3].T)[None, None], np.ascontiguousarray(hh[:, 0])[None, None],
            new_conv_s[None], np.ascontiguousarray(hh[:, 1:].T)[None], r["o_vs"][None, :, None])
```

```python
from contextlib import ExitStack

import numpy as np
import concourse.bass as bass
from concourse import mybir

F = mybir.dt.float32
R = mybir.dt.float32r
ALU = mybir.AluOpType
ACT = mybir.ActivationFunctionType
AX = mybir.AxisListType

P = 128
DM = 1024
NT, NS = 1024, 8
TT = NT + NS
KT = DM // P
NG = 3
GN = TT // NG
NCH = NT // P
LASTC = TT - P
WF = 2 * P
NL = 32
EPS = 1e-6
NM, MT = 256, 2
NH, HD = 4, 64
AH, AD = 4, 96
AW = AH * AD
LRU_C = 8.0
T_Q, T_GC, T_XB, T_V, T_GA, T_GB, T_U, N_TILES = 0, 2, 4, 7, 10, 13, 16, 19
ATT0 = 4
PAR = {}
_at = 0
for _name, _n in (("g_pre", 8), ("g_mem", 8), ("w_conv", 12), ("b_conv", 3), ("b_a", 3), ("b_x", 3),
                  ("lam", 3), ("st_conv", 72), ("st_h", 24), ("b_s", 4)):
    PAR[_name] = _at
    _at += _n
N_PAR = _at
K_ORDER = [3, 4, 5, 6, 7, 0, 1, 2]
MIX_BANKS = (6, 7, 4)
GATE_PAIRS = [(0, 0), (1, 0), (0, 1), (1, 1), (2, 1), (1, 2), (2, 2)]


class Tally:

    def __init__(self, eng, sem):
        self.eng, self.sem, self.base, self.k = eng, sem, 0, 0

    def mark(self, ins):
        ins.then_inc(self.sem, 1)
        self.k += 1

    def wait(self):
        self.eng.wait_ge(self.sem, self.base + self.k)

    def link(self, ins):
        self.mark(ins)
        self.wait()


def build(nc, d):
    with ExitStack() as ctx:
        def sb(name, shape, dt=F):
            return ctx.enter_context(nc.sbuf_tensor(name, shape, dt))

        def sem(name):
            return ctx.enter_context(nc.semaphore(name))

        x_hi, x_lo = sb("x_hi", [P, KT, TT], R), sb("x_lo", [P, KT, TT], R)
        w_stage = sb("w_stage", [P, 2, DM])
        w_hi, w_lo = sb("w_hi", [P, 2, DM], R), sb("w_lo", [P, 2, DM], R)
        rstdB = sb("rstdB", [P, TT])
        probs = sb("probs", [P, TT])
        kv = sb("kv", [P, MT, 512])
        small_T = sb("small_T", [P, 2, 64])
        rows = sb("rows", [P, AW + 8])
        gate_w = sb("gate_w", [P, 2, len(GATE_PAIRS), P])
        wsT = sb("wsT", [P, AH, P])
        ident, ones = sb("ident", [P, P]), sb("ones", [P, P])
        attn = sb("attn", [P, NM])
        par = sb("par", [P, N_PAR])
        ssq, rstd = sb("ssq", [P, MT]), sb("rstd", [P, MT])
        ssv, rstdv = sb("ssv", [P, 36]), sb("rstdv", [P, 36])
        mx, negm = sb("mx", [P, 4]), sb("negm", [P, 4])
        sums, rsum = sb("sums", [P, 4]), sb("rsum", [P, 4])
        nsp, lt = sb("nsp", [P, 3]), sb("lt", [P, 6, 3])
        qb = sb("qb", [P, 2, NS, NH])
        sy, ry, sl = sb("sy", [P, 4]), sb("ry", [P, 2]), sb("sl", [P, 2])
        sst = sb("sst", [32, 4])
        h_last = sb("h_last", [P, 3, NS + 1])
        o_s = sb("o_s", [P, KT, 2 * NL], R)
        ps = ctx.enter_context(nc.psum_tensor("ps", [P, 8, 512], F))

        with nc.sbuf_tensor("mixT", [P, KT, TT], F) as mixT, \
             nc.sbuf_tensor("zT", [P, 11, TT], F) as zT, \
             nc.sbuf_tensor("x_ring", [P, 2, TT], F) as x_ring, \
             nc.sbuf_tensor("probsT", [P, TT], F) as probsT:
            pass
        MIX0, Z0 = 0, KT * TT
        XR0 = Z0 + 11 * TT
        PT0 = XR0 + 2 * TT
        filled = 0

        def over(name, at, shape):
            nonlocal filled
            if at > filled:
                sb(f"gap_{name}", [P, at - filled])
            filled = at + int(np.prod(shape[1:]))
            return sb(name, shape, R)

        memT_hi = over("memT_hi", MIX0, [P, KT, NM])
        w_mem_hi = over("w_mem_hi", MIX0 + 2 * TT, [P, KT, 512])
        memT_lo = over("memT_lo", Z0 + 2 * TT, [P, KT, NM])
        w_mem_lo = over("w_mem_lo", Z0 + 4 * TT, [P, KT, 512])
        k_hh = over("k_hh", Z0 + 8 * TT, [P, 2, 2, NM])
        q_st = over("q_st", Z0 + 8 * TT + 1024, [P, 2, 2, 2, P])
        probsT_lo = over("probsT_lo", Z0 + 8 * TT + 2048, [P, 1024])
        v_hl = over("v_hl", XR0, [P, MT, NH, 2 * HD])
        k_lo = over("k_lo", XR0 + 1024, [P, 2, NM])
        probsT_hi = over("probsT_hi", PT0, [P, 1024])

        zf = zT[:, :, :].rearrange("p a b -> p (a b)")
        memT = zf[:, 2 * TT:2 * TT + KT * NM].rearrange("p (k m) -> p k m", k=KT)
        w_mem = zf[:, 4 * TT:4 * TT + KT * 512].rearrange("p (k m) -> p k m", k=KT)
        mem_nat = zf[:, 8 * TT:8 * TT + MT * DM].rearrange("p (k m) -> p k m", k=MT)
        xf = x_ring[:, :, :].rearrange("p a b -> p (a b)")
        sig_c = (zT[:, 3, :], zT[:, 4, :])
        v_tok = zf[:, TT:TT + 9 * AW].rearrange("p (c n) -> p c n", c=9)
        v_sq = xf[:, 0:4 * AW].rearrange("p (c n) -> p c n", c=4)
        cache_ring = zf[:, 5 * TT:5 * TT + 6 * 512].rearrange("p (c n) -> p c n", c=6)
        wo_early = zf[:, TT:TT + 4 * DM].rearrange("p (c n) -> p c n", c=4)
        x_s, y_s = zT[0:NL, 8, 0:DM], kv[0:NL, :, :]
        y_out = zf[:, 5 * TT:5 * TT + 2 * DM].rearrange("p (c n) -> p c n", c=2)
        g_post = zf[:, 7 * TT:7 * TT + DM]
        s_r, s_i, s_th = zT[:, 0, :], probs[:, :], probsT[:, :]
        s_a2, s_sig = x_ring[:, 0, :], x_ring[:, 1, :]
        sT_s = small_T[:, 0, :]
        p_s = kv[0:32, 0, 0:NM]
        pT_s = small_T[:, 1, :].rearrange("p (m n) -> p m n", m=2)
        o_hi, o_lo = w_hi, w_lo
        wo_hi, wo_lo = x_hi, x_lo

        def wo_source(n):
            if n in (0, 1, 7):
                return w_stage[:, n % 7, :]
            return wo_early[:, n - 2, :] if n < 6 else zT[:, 0, 0:DM]

        def pc(name, i=0, n=1):
            return par[:, PAR[name] + i:PAR[name] + i + n]

        par_in, rows_in, gatew_in, wsT_in, memn_in = map(sem, (
            "par_in", "rows_in", "gatew_in", "wsT_in", "memn_in"))
        memT_in = [sem(f"memT_in{i}") for i in range(4)]
        wm_in = [sem(f"wm_in{i}") for i in range(4)]
        xT_in = [sem(f"xT_in{k}") for k in range(KT)]
        w_in = [sem(f"w_in{i}") for i in range(2)]
        x_in = [sem(f"x_in{i}") for i in range(2)]
        c_in = [sem(f"cache_in{i}") for i in range(6)]
        wo_in = [sem(f"wo_in{i}") for i in range(KT)]
        gpost_in = sem("gpost_in")
        y_stored = [sem(f"y_stored{i}") for i in range(2)]
        kv_stored, conv_stored, h_stored, vs_stored, ys_stored = map(sem, (
            "kv_stored", "conv_stored", "h_stored", "vs_stored", "ys_stored"))
        const_set, w_masked, wlo_done, qc_done, xsq_done, whi_done, xhi_done = map(sem, (
            "const_set", "w_masked", "wlo_done", "qc_done", "xsq_done", "whi_done", "xhi_done"))
        xlo_done, memg_done, ms_done, root_done, xsum_done, rstdB_done = map(sem, (
            "xlo_done", "memg_done", "ms_done", "root_done", "xsum_done", "rstdB_done"))
        kvp_done, kv_done, kTp_done, khi_done, klo_done, vhi_done, vlo_done = map(sem, (
            "kvp_done", "kv_done", "kTp_done", "khi_done", "klo_done", "vhi_done", "vlo_done"))
        mhi_done, mlo_done, wmlo_done = map(sem, ("mhi_done", "mlo_done", "wmlo_done"))
        qhi_done = sem("qhi_done")
        wfirst_in, wfirsthi_done, wfirstlo_done = map(sem, ("wfirst_in", "wfirsthi_done", "wfirstlo_done"))
        z_done, z_used, rstdp_done = map(sem, ("z_done", "z_used", "rstdp_done"))
        gcsig_done = sem("gcsig_done")
        sc_done, negm_done, p_done, pTp_done, pThi_done, pTlo_done = map(sem, (
            "sc_done", "negm_done", "p_done", "pTp_done", "pThi_done", "pTlo_done"))
        pv_done, attn_done, attnT_done, c_done = map(sem, ("pv_done", "attn_done", "attnT_done", "c_done"))
        lam_done, elam_done, nsp_done, conv_done = map(sem, ("lam_done", "elam_done", "nsp_done", "conv_done"))
        gate_done, gate_used, vt_done, vt_used = map(sem, ("gate_done", "gate_used", "vt_done", "vt_used"))
        ixc_done, gbm_done = sem("ixc_done"), sem("gbm_done")
        q_done = sem("q_done")
        y_half, ysq_half, yg_half, y_last, x_free = map(sem, ("y_half", "ysq_half", "yg_half", "y_last", "x_free"))
        (oshi_done, os_done, ys_done, yslo_done, ysum_done, yssq_done, ysms_done, ysroot_done, ys_ready,
         xs_in) = map(sem, (
            "oshi_done", "os_done", "ys_done", "yslo_done", "ysum_done", "yssq_done", "ysms_done",
            "ysroot_done", "ys_ready", "xs_in"))
        vsq_done, vsum_done, vroot_done, vms_done, vr_done, vn_done = map(sem, (
            "vsq_done", "vsum_done", "vroot_done", "vms_done", "vr_done", "vn_done"))
        gasig_done, ga_done, gar_done = map(sem, ("gasig_done", "ga_done", "gar_done"))
        sp_done, mix_done, mT_done, a_done = map(sem, ("sp_done", "mix_done", "mT_done", "a_done"))
        decay_done, rest_done, root_b_done, scan_done, placed = map(sem, (
            "decay_done", "rest_done", "root_b_done", "scan_done", "placed"))
        gbsig_done, b_done = map(sem, ("gbsig_done", "b_done"))
        qb_done, s1c_done, s2_done, snegm_done, sp_exp, sp_norm, s3_done, s3c_done, cs_done = map(sem, (
            "qb_done", "s1c_done", "s2_done", "snegm_done", "sp_exp", "sp_norm", "s3_done",
            "s3c_done", "cs_done"))
        cache_read = sem("cache_read")
        wohi_done, wo_done, ohi_done, o_done = map(sem, ("wohi_done", "wo_done", "ohi_done", "o_done"))
        y_done, ysq_done, yms_done, yroot_done, y_used, y_ready = map(sem, (
            "y_done", "ysq_done", "yms_done", "yroot_done", "y_used", "y_ready"))
        dve_own, act_own = sem("dve_own"), sem("act_own")

        block = ctx.enter_context(nc.Block())

        @block.sync
        def _(sp):
            def load_w(m, slot):
                sp.dma_start(w_stage[:, slot, :], d["w_tiles"][m]).then_inc(w_in[slot], 16)

            def load_cache(n):
                if n >= 6:
                    sp.wait_ge(cache_read, n - 5)
                src = d["kcT"][n] if n < NS else d["vc"][n - NS]
                sp.dma_start(cache_ring[:, n % 6, :], src).then_inc(c_in[n % 6], 16)

            sp.dma_start(par[:, :], d["par"]).then_inc(par_in, 16)
            sp.dma_start(w_stage[:, 0, 0:WF], d["w_tiles"][0, :, 0:WF]).then_inc(wfirst_in, 16)
            for k in range(KT):
                if k == 1:
                    sp.dma_start(w_stage[:, 0, WF:DM], d["w_tiles"][0, :, WF:DM]).then_inc(w_in[0], 16)
                if k == 2:
                    load_w(1, 1)
                sp.dma_start(mixT[:, k, :], d["xT"][:, k, :]).then_inc(xT_in[k], 16)
            sp.wait_ge(wlo_done, 1)
            load_w(2, 0)
            for i in range(4):
                kk = slice(2 * i, 2 * i + 2)
                sp.dma_start(memT[:, kk, :], d["memT"][:, kk, :]).then_inc(memT_in[i], 16)
                sp.dma_start(w_mem[:, kk, :], d["w_mem"][:, kk, :]).then_inc(wm_in[i], 16)
            sp.dma_start(mem_nat, d["mem_nat"]).then_inc(memn_in, 16)
            sp.wait_ge(wlo_done, 2)
            load_w(3, 1)
            sp.dma_start(rows[:, :], d["rows"].partition_broadcast(P)).then_inc(rows_in, 16)
            sp.dma_start(wsT[:, :, :], d["wsT"]).then_inc(wsT_in, 16)
            sp.dma_start(gate_w[:, :, :, :], d["gate_w"]).then_inc(gatew_in, 16)
            with sp.Fori(0, 4) as i:
                for u in range(2):
                    sp.wait_ge(wlo_done, i * 2 + (3 + u))
                    load_w(i * 2 + (4 + u), u)
            sp.wait_ge(kv_done, 2)
            sp.dma_start(d["o_kv"], kv[:, :, :]).then_inc(kv_stored, 16)
            for j in range(3):
                sp.wait_ge(z_used, 3 * (T_XB + j + 1))
                sp.dma_start(d["o_conv"][:, j, :], zT[:, 2 + j, NT - 3:TT]).then_inc(conv_stored, 16)
            sp.dma_start(d["o_st"], pc("st_conv", 0, 72)).then_inc(h_stored, 16)
            for m in (12, 13, 14, 15):
                sp.wait_ge(wlo_done, m - 1)
                load_w(m, m % 2)
            sp.wait_ge(vt_done, 9)
            for n in range(6):
                load_cache(n)
            sp.wait_ge(wlo_done, 15)
            load_w(16, 0)
            load_cache(6)
            load_cache(7)
            sp.wait_ge(vn_done, 3)
            sp.dma_start(d["o_vs"], v_tok[P - NS:P, 8, :]).then_inc(vs_stored, 16)
            sp.wait_ge(wlo_done, 16)
            load_w(17, 1)
            for n in range(8, 14):
                load_cache(n)
            sp.wait_ge(wlo_done, 17)
            load_w(18, 0)
            sp.wait_ge(mT_done, 9)
            sp.wait_ge(a_done, 9)

            def load_wo(n):
                sp.dma_start(wo_source(n), d["w_out"][K_ORDER[n]]).then_inc(wo_in[n], 16)

            for n in range(2, 6):
                load_wo(n)
            sp.wait_ge(wlo_done, 18)
            load_wo(1)
            sp.wait_ge(wlo_done, 19)
            load_wo(0)
            load_cache(14)
            load_cache(15)
            sp.wait_ge(scan_done, 6)
            load_wo(6)
            sp.wait_ge(placed, 6)
            sp.dma_start(d["o_h"], h_last[:, :, :]).then_inc(h_stored, 16)

            def load_x(c0, slot):
                sp.dma_start(x_ring[:, slot, 0:DM], d["x_all"][bass.ds(c0, P), :]).then_inc(x_in[slot], 16)

            sp.wait_ge(b_done, 3)
            load_x(0, 1)
            load_x(P, 0)
            sp.dma_start(x_s, d["x_all"][TT - NL:TT, :]).then_inc(xs_in, 16)
            sp.wait_ge(cache_read, 2 * NS)
            sp.dma_start(g_post, d["g_post"].partition_broadcast(P)).then_inc(gpost_in, 16)
            sp.wait_ge(wo_done, 1)
            load_wo(7)
            with sp.Fori(0, 3) as i:
                for v in range(2):
                    u = 1 - v
                    sp.wait_ge(y_ready, i * 2 + (v + 1))
                    sp.dma_start(d["o_y"][bass.ds(i * (2 * P) + v * P, P), :], y_out[:, u, :]).then_inc(y_stored[u], 16)
                    load_x(i * (2 * P) + (2 + v) * P, u)
            sp.wait_ge(ys_ready, 1)
            sp.dma_start(d["o_y"][NT:TT, :], y_s[NL - NS:NL].rearrange("p a b -> p (a b)")).then_inc(ys_stored, 16)
            sp.wait_ge(y_ready, 7)
            sp.dma_start(d["o_y"][6 * P:7 * P, :], y_out[:, 1, :]).then_inc(y_stored[1], 16)
            for n in range(2):
                half = slice(n * 512, (n + 1) * 512)
                sp.wait_ge(y_last, n + 1)
                sp.dma_start(d["o_y"][7 * P:NT, half], y_out[:, 0, half]).then_inc(y_stored[0], 16)
            sp.wait_ge(y_stored[0], 16 * 5)
            sp.wait_ge(y_stored[1], 16 * 4)
            sp.wait_ge(ys_stored, 16)
            sp.wait_ge(kv_stored, 16)
            sp.wait_ge(conv_stored, 48)
            sp.wait_ge(h_stored, 32)
            sp.wait_ge(vs_stored, 16)

        @block.tensor
        def _(pe):
            def parts(g, slot, k, cols, x, bank):
                wk = slice(k * P, (k + 1) * P)
                for n, (w, xx) in enumerate(((w_hi, x_hi), (w_hi, x_lo), (w_lo, x_hi))):
                    last = pe.matmul(ps[:, bank, 0:GN], w[:, slot, wk], xx[:, k, cols],
                                     start=(x == 0 and n == 0), stop=(x == KT - 1 and n == 2))
                return last

            def gemm(m, g, slot, between=None):
                if g == 0:
                    pe.wait_ge(wlo_done, m + 1)
                pe.wait_ge(z_used, g + 1 if isinstance(m, int) and m == 2 else m * 3 + (g - 2))
                last_use = isinstance(m, int) and m == N_TILES - 1 and g == NG - 1
                for x, k in enumerate(K_ORDER if last_use else range(KT)):
                    last = parts(g, slot, k, slice(g * GN, (g + 1) * GN), x, g)
                    if between and x < KT - 1:
                        between(x)
                    if last_use and x < KT - 1:
                        last.then_inc(x_free, 1)
                last.then_inc(z_done, 1)

            def start_tiles(m, k):
                if m == 0 and k == 0:
                    pe.wait_ge(wfirstlo_done, 1)
                elif (m, k) in ((0, WF // P), (1, 0)):
                    pe.wait_ge(wlo_done, m + 1)
                if m == 0:
                    pe.wait_ge(xlo_done, k + 1)
                for g in range(NG):
                    last = parts(g, m, k, slice(g * GN, (g + 1) * GN), k, 3 * m + g)
                    if k == KT - 1:
                        last.then_inc(z_done, 1)

            for k in range(KT):
                start_tiles(0, k)
                if k in (2, 4, 6):
                    start_tiles(1, k // 2 - 1)
            for k in range(3, KT):
                start_tiles(1, k)
            gemm(2, 0, 0)
            pe.wait_ge(xsum_done, KT - 1)
            pe.wait_ge(const_set, 4)
            pe.wait_ge(z_used, 6)
            for g in range(NG):
                pe.matmul(ps[:, 5 + g, 0:GN], ones[:, :], probs[:, g * GN:(g + 1) * GN],
                          start=True, stop=True).then_inc(rstdp_done, 1)
            gemm(2, 1, 0)
            gemm(2, 2, 0)
            for k in range(KT):
                pe.wait_ge(mlo_done, k // 2 + 1)
                pe.wait_ge(wmlo_done, k // 2 + 1)
                for mt in range(MT):
                    for n, (a, w) in enumerate(((memT_hi, w_mem_hi), (memT_lo, w_mem_hi),
                                                (memT_hi, w_mem_lo))):
                        last = pe.matmul(ps[:, 3 + mt, :], a[:, k, mt * P:(mt + 1) * P], w[:, k, :],
                                         start=(k == 0 and n == 0), stop=(k == KT - 1 and n == 2))
            last.then_inc(kvp_done, 1)
            gemm(3, 0, 1)
            pe.wait_ge(kv_done, 2)
            pe.wait_ge(ms_done, 3)
            for t in range(2):
                for mt in range(MT):
                    last = pe.transpose(ps[:, 5, t * NM + mt * P:t * NM + (mt + 1) * P],
                                        kv[:, mt, t * P:(t + 1) * P], ident[:, :])
            last.then_inc(kTp_done, 1)
            gemm(3, 1, 1)
            gemm(3, 2, 1)

            pe.wait_ge(khi_done, 4)
            pe.wait_ge(klo_done, 2)
            pe.wait_ge(vlo_done, 1)
            with pe.Fori(0, 4) as i:
                for u in range(2):
                    m, s = i * 2 + (ATT0 + u), i * 2 + u
                    pe.wait_ge(qc_done, s * 2 + 2)
                    for t in range(2):
                        for hh in range(2):
                            rows_h = slice(hh * HD, (hh + 1) * HD)
                            out = ps[:, 3 + hh, t * NM:(t + 1) * NM]
                            pe.matmul(out, q_st[:, u, hh, t, :], k_hh[:, hh, t, :], start=True, stop=False)
                            last = pe.matmul(out, q_st[rows_h, u, hh, t, :], k_lo[rows_h, t, :],
                                             start=False, stop=True)
                            if t == 1:
                                last.then_inc(sc_done, 1)
                    gemm(m, 0, u)
                    for b in range(2):
                        pe.wait_ge(p_done, s * 4 + (2 + 2 * b))
                        for n in range(4):
                            last = pe.transpose(ps[:, 5 + b, n * P:(n + 1) * P],
                                                probs[:, (4 * b + n) * P:(4 * b + n + 1) * P], ident[:, :])
                        last.then_inc(pTp_done, 1)
                    gemm(m, 1, u)
                    for h in range(NH):
                        if h % 2 == 0:
                            pe.wait_ge(pTlo_done, s * 2 + (h // 2 + 1))
                        for mt in range(MT):
                            pT = slice((2 * h + mt) * P, (2 * h + mt + 1) * P)
                            pe.matmul(ps[:, 7, h * 2 * HD:(h + 1) * 2 * HD], probsT_hi[:, pT], v_hl[:, mt, h, :],
                                      start=(mt == 0), stop=(mt == 1), skip_group_check=True)
                            last = pe.matmul(ps[:, 7, h * 2 * HD:h * 2 * HD + HD], probsT_lo[:, pT],
                                             v_hl[:, mt, h, 0:HD], start=False, stop=True,
                                             skip_group_check=True)
                    last.then_inc(pv_done, 1)
                    gemm(m, 2, u)
                    pe.wait_ge(attn_done, s + 1)
                    for t in range(2):
                        last = pe.transpose(ps[:, 7, t * P:(t + 1) * P],
                                            attn[:, t * P:(t + 1) * P], ident[:, :])
                    last.then_inc(attnT_done, 1)

            def gates(j, g):
                for gate in range(2):
                    n = (j * 3 + g) * 2 + gate
                    if n >= 3:
                        pe.wait_ge(gate_used, n - 2)
                    pairs = [(x, kin) for x, (kin, out) in enumerate(GATE_PAIRS) if out == j]
                    if n == 8:
                        pe.wait_ge(sp_exp, 1)
                    cols, bank = slice(g * GN, (g + 1) * GN), 3 + n % 3
                    x = GATE_PAIRS.index((j, j))
                    last = pe.matmul(ps[:, bank, 0:GN], gate_w[:, gate, x, :], mixT[:, 3 + j, cols],
                                     start=True, stop=True)
                    for x, kin in pairs:
                        if kin != j:
                            r, c = (slice(96, 128), slice(0, 32)) if kin < j else (slice(0, 32), slice(96, 128))
                            last = pe.matmul(ps[c, bank, 0:GN], gate_w[r, gate, x, c], mixT[r, 3 + kin, cols],
                                             start=False, stop=True, skip_group_check=True)
                    last.then_inc(gate_done, 1)

            def col0(c):
                return min(c * P, LASTC)

            pe.wait_ge(conv_done, 3)
            pe.wait_ge(gatew_in, 16)
            pe.wait_ge(p_done, 32)
            pe.wait_ge(pTlo_done, 16)

            def v_transpose(c):
                if c == 1:
                    pe.wait_ge(c_done, 8)
                if c >= 2:
                    pe.wait_ge(vt_used, c - 1)
                for j in range(3):
                    last = pe.transpose(ps[:, 6 + c % 2, j * P:(j + 1) * P],
                                        zT[:, 5 + j, col0(c):col0(c) + P], ident[:, :])
                last.then_inc(vt_done, 1)

            for g in range(NG):
                gemm(12, g, 0)
                v_transpose(3 * g)
                v_transpose(3 * g + 1)
                gates(0, g)
                v_transpose(3 * g + 2)

            def sample_scores(n):
                pe.wait_ge(c_in[n % 6], 16 * (n // 6 + 1))
                for mt in range(MT):
                    for t in range(2):
                        last = pe.matmul(ps[:, 5, mt * 32 + n * NH:mt * 32 + (n + 1) * NH],
                                         cache_ring[:, n % 6, t * NM + mt * P:t * NM + (mt + 1) * P],
                                         qb[:, t, n, :], start=(t == 0), stop=(t == 1))
                last.then_inc(cache_read, 1)

            def sample_values(n):
                part = NS + n
                pe.wait_ge(c_in[part % 6], 16 * (part // 6 + 1))
                for t in range(2):
                    at = (t * NS + n) * NH
                    for mt in range(MT):
                        last = pe.matmul(ps[:, 7, at:at + NH],
                                         cache_ring[:, part % 6, mt * NM + t * P:mt * NM + (t + 1) * P],
                                         pT_s[:, mt, n * NH:(n + 1) * NH], start=(mt == 0), stop=(mt == 1))
                last.then_inc(cache_read, 1)

            pe.wait_ge(qb_done, 4)
            for g in range(NG):
                def between(x):
                    if x in (2, 5):
                        sample_scores(3 * g - 1 + x // 3)
                gemm(13, g, 1, between if g else None)
                if g == 0:
                    pe.wait_ge(gate_used, 6)
                    sample_scores(0)
                sample_scores(3 * g + 1)
            def spatial(c):
                pe.wait_ge(vn_done, c // 4 + 1)
                pe.wait_ge(vt_used if c < 2 else mix_done, 9 if c < 2 else c - 1)
                for h in range(AH):
                    last = pe.matmul(ps[:, 6 + c % 2, h * AD:(h + 1) * AD], wsT[:, h, :],
                                     v_tok[:, c, h * AD:(h + 1) * AD], start=True, stop=True)
                last.then_inc(sp_done, 1)

            pe.wait_ge(w_masked, 1)
            for g in range(NG):
                gemm(14, g, 0)
                if g == 0:
                    pe.wait_ge(s1c_done, 1)
                    for mt in range(MT):
                        last = pe.matmul(ps[0:32, 5, mt * P:(mt + 1) * P], sT_s[:, mt * 32:(mt + 1) * 32],
                                         ident[:, :], start=True, stop=True)
                    last.then_inc(s2_done, 1)
                spatial(3 * g)
                spatial(3 * g + 1)
                gates(1, g)
                if g < 2:
                    spatial(3 * g + 2)
            for g in range(NG):
                gemm(15, g, 1)
                if g == 1:
                    pe.wait_ge(sp_norm, 1)
                    pe.wait_ge(gate_used, 12)
                    for mt in range(MT):
                        last = pe.matmul(ps[:, 5, mt * 32:(mt + 1) * 32], p_s[:, mt * P:(mt + 1) * P],
                                         ident[0:32, 0:32], start=True, stop=True)
                    last.then_inc(s3_done, 1)
                for c in range(3 * g, 3 * g + 3):
                    pe.wait_ge(mix_done, 9)
                    if c >= 3:
                        pe.wait_ge(a_done, c - 2)
                    elif c == 2:
                        pe.wait_ge(gate_used, 12)
                    for j in range(3):
                        last = pe.transpose(ps[:, MIX_BANKS[c % 3], j * P:(j + 1) * P],
                                            v_tok[:, c, j * P:(j + 1) * P], ident[:, :])
                    last.then_inc(mT_done, 1)
            pe.wait_ge(s3c_done, 1)
            for g in range(NG):
                gemm(16, g, 0)
                pe.wait_ge(a_done, 9)
                gates(2, g)
            pe.wait_ge(a_done, 9)
            for g, samples in enumerate(((0, 1), (2,), (3, 4), (5,), (6,), (7,))):
                gemm(17 + g // 3, g % 3, 1 - g // 3)
                for n in samples:
                    sample_values(n)

            def project(c, u, first=False):
                pe.wait_ge(o_done, c + 1)
                for x, k in enumerate(K_ORDER):
                    if first:
                        pe.wait_ge(wo_done, x + 1)
                    for n in range(2):
                        last = product(u, k, n, x)
                last.then_inc(y_done, 1)

            def product(u, k, n, x):
                ok, cols = slice(k * P, (k + 1) * P), slice(n * 512, (n + 1) * 512)
                for part, (o, w) in enumerate(((o_hi, wo_hi), (o_hi, wo_lo), (o_lo, wo_hi))):
                    last = pe.matmul(ps[:, 3 * u + n, :], o[:, u, ok], w[:, k, cols],
                                     start=(x == 0 and part == 0), stop=(x == KT - 1 and part == 2))
                return last

            pe.wait_ge(gate_used, 18)
            project(0, 1, first=True)
            pe.wait_ge(os_done, 1)
            for x, k in enumerate(K_ORDER):
                for n in range(2):
                    cols = slice(n * 512, (n + 1) * 512)
                    pe.matmul(ps[0:2 * NL, 6 + n, :], o_s[:, k, :], wo_hi[:, k, cols],
                              start=(x == 0), stop=(x == KT - 1), skip_group_check=True)
                    last = pe.matmul(ps[0:NL, 6 + n, :], o_s[:, k, 0:NL], wo_lo[:, k, cols],
                                     start=False, stop=(x == KT - 1), skip_group_check=True)
            last.then_inc(ys_done, 1)
            with pe.Fori(0, 3) as i:
                for v in range(2):
                    pe.wait_ge(y_used, i * 2 + (v + 1))
                    project(i * 2 + (v + 1), v)
            pe.wait_ge(y_used, 7)
            pe.wait_ge(o_done, 8)
            for n in range(2):
                for x, k in enumerate(K_ORDER):
                    last = product(0, k, n, x)
                last.then_inc(y_half, 1)

        @block.scalar
        def _(act):
            own = Tally(act, act_own)

            def split_w(m, slot, arrived):
                act.wait_ge(w_in[slot], arrived)
                if not isinstance(m, int) or m >= 2:
                    act.wait_ge(z_done, m * 3 + (-3))
                act.activation(w_hi[:, slot, :], w_stage[:, slot, :], ACT.Copy).then_inc(whi_done, 1)

            def split_tile(m):
                split_w(m, m % 2, 16 * (m // 2 + 1))

            act.wait_ge(lam_done, 1)
            act.activation(lt[:, 1, :], lt[:, 0, :], ACT.Exp, scale=-1.0).then_inc(elam_done, 1)
            act.wait_ge(wfirst_in, 16)
            act.activation(w_hi[:, 0, 0:WF], w_stage[:, 0, 0:WF], ACT.Copy).then_inc(wfirsthi_done, 1)
            act.wait_ge(par_in, 16)
            for k in range(KT):
                if k == 1:
                    act.wait_ge(w_in[0], 16)
                    act.activation(w_hi[:, 0, WF:DM], w_stage[:, 0, WF:DM], ACT.Copy).then_inc(whi_done, 1)
                if k == 2:
                    split_tile(1)
                act.wait_ge(xT_in[k], 16)
                act.activation(x_hi[:, k, :], mixT[:, k, :], ACT.Copy, scale=pc("g_pre", k)).then_inc(xhi_done, 1)
            for k in range(KT):
                act.wait_ge(xlo_done, k + 1)
                act.activation(mixT[:, k, :], mixT[:, k, :], ACT.Square).then_inc(xsq_done, 1)
                if k == 3:
                    split_tile(2)
            act.wait_ge(memn_in, 16)
            for mt in range(MT):
                own.link(act.activation(probsT[:, 0:DM], mem_nat[:, mt, :], ACT.Square, accum_out=ssq[:, mt:mt + 1]))
            act.wait_ge(xsum_done, KT - 1)
            for i in range(4):
                kk = slice(2 * i, 2 * i + 2)
                act.wait_ge(memg_done, i + 1)
                act.activation(memT_hi[:, kk, :], memT[:, kk, :], ACT.Copy).then_inc(mhi_done, 1)
                act.wait_ge(wm_in[i], 16)
                act.activation(w_mem_hi[:, kk, :], w_mem[:, kk, :], ACT.Copy).then_inc(mhi_done, 1)
            split_tile(3)
            act.wait_ge(ms_done, 4)
            act.activation(rstdB[:, :], rstdB[:, :], ACT.Sqrt).then_inc(root_done, 1)
            act.activation(rstd[:, :], ssq[:, :], ACT.Sqrt).then_inc(root_done, 1)
            split_tile(4)
            act.wait_ge(kvp_done, 1)
            act.wait_ge(rstdB_done, 2)
            for mt in range(MT):
                act.activation(kv[:, mt, :], ps[:, 3 + mt, :], ACT.Copy, scale=rstd[:, mt:mt + 1]).then_inc(kv_done, 1)
            act.wait_ge(kv_done, 2)
            act.activation(v_hl[:, :, :, 0:HD], kv[:, :, 256:512].rearrange("p m (h n) -> p m h n", h=NH),
                           ACT.Copy).then_inc(vhi_done, 1)

            def split_q(c0, slot):
                for hh in range(2):
                    r = slice(hh * HD, (hh + 1) * HD)
                    act.activation(q_st[r, slot, hh, :, :], zT[r, 0:2, bass.ds(c0, P)], ACT.Copy).then_inc(qhi_done, 1)

            act.wait_ge(q_done, 2)
            split_q(0, 0)
            act.wait_ge(z_used, 3 * (T_GC + 1))
            act.activation(sig_c[0], mixT[:, 6, :], ACT.Sigmoid).then_inc(gcsig_done, 1)
            act.wait_ge(kTp_done, 1)
            for src in range(2):
                for hh in range(2):
                    r, to = slice(hh * HD, (hh + 1) * HD), (hh + src) % 2
                    act.activation(k_hh[to * HD:(to + 1) * HD, hh, :, :],
                                   ps[r, 5, :].rearrange("p (t n) -> p t n", t=2), ACT.Copy).then_inc(khi_done, 1)
            act.wait_ge(z_used, 3 * (T_GC + 2))
            act.activation(sig_c[1], mixT[:, 7, :], ACT.Sigmoid).then_inc(gcsig_done, 1)

            def attention(s):
                act.wait_ge(negm_done, s + 1)
                for h in range(NH):
                    t, hh = h // 2, h % 2
                    n = hh * 2 + t
                    act.activation(probs[:, h * NM:(h + 1) * NM], ps[:, 3 + hh, t * NM:(t + 1) * NM],
                                   ACT.Exp, bias=negm[:, n:n + 1], scale=HD ** -0.5,
                                   accum_out=sums[:, h:h + 1]).then_inc(p_done, 1)
                for b in range(2):
                    act.wait_ge(pTp_done, s * 2 + (b + 1))
                    act.activation(probsT_hi[:, b * 512:(b + 1) * 512], ps[:, 5 + b, :],
                                   ACT.Copy).then_inc(pThi_done, 1)

            split_tile(ATT0 + 1)
            attention(0)
            with act.Fori(0, 3) as i:
                for v in range(2):
                    split_q(i * (2 * P) + (v + 1) * P, 1 - v)
                    split_w(i * 2 + (ATT0 + 2 + v), v, i * 16 + 64)
                    attention(i * 2 + (v + 1))
            split_q(7 * P, 1)
            split_tile(12)
            attention(7)

            def gate_sigmoids(j, g):
                for gate, (dst, bias) in enumerate(((s_r, "b_a"), (s_i, "b_x"))):
                    n = (j * 3 + g) * 2 + gate
                    act.wait_ge(gate_done, n + 1)
                    act.activation(dst[:, g * GN:(g + 1) * GN], ps[:, 3 + n % 3, 0:GN], ACT.Sigmoid,
                                   bias=pc(bias, j)).then_inc(gate_used, 1)

            def decay(j):
                act.wait_ge(gate_used, 6 * (j + 1))
                act.wait_ge(placed, 2 * j)
                act.activation(s_th, s_r, ACT.Tanh, scale=nsp[:, j:j + 1]).then_inc(decay_done, 1)
                act.activation(s_a2, s_r, ACT.Exp, scale=lt[:, 5, j:j + 1]).then_inc(decay_done, 1)
                act.wait_ge(decay_done, 3 * j + 2)
                act.activation(s_r, s_r, ACT.Exp, scale=nsp[:, j:j + 1]).then_inc(decay_done, 1)

            def place(j):
                act.wait_ge(scan_done, 2 * (j + 1))
                act.wait_ge(gate_done, 6 * min(j + 2, 3))
                act.wait_ge(ixc_done, j + 1)
                act.activation(mixT[:, 3 + j, :], s_th, ACT.Copy).then_inc(placed, 1)
                act.activation(h_last[:, j, :], s_th[:, NT - 1:TT], ACT.Copy).then_inc(placed, 1)

            def root_b(j):
                act.wait_ge(rest_done, j + 1)
                act.activation(s_th, s_th, ACT.Sqrt, scale=-1.0).then_inc(root_b_done, 1)

            split_tile(13)
            act.wait_ge(pv_done, NCH)
            for j in range(2):
                act.wait_ge(z_used, 3 * (T_GA + j + 1))
                act.activation(zT[:, 9 + j, :], mixT[:, j, :], ACT.Sigmoid).then_inc(gasig_done, 1)
            act.wait_ge(pTp_done, 16)
            act.wait_ge(qb_done, 4)
            act.wait_ge(conv_done, 3)
            act.wait_ge(conv_stored, 48)
            for g in range(NG):
                for c in range(3 * g, 3 * g + 3):
                    if c % 3 == 2:
                        gate_sigmoids(0, g)
                    act.wait_ge(vt_done, c + 1)
                    if c >= 4:
                        act.wait_ge(vsum_done, c - 3)
                    act.activation(v_sq[:, c % 4, :], ps[:, 6 + c % 2, 0:AW], ACT.Square).then_inc(vsq_done, 1)
                    act.activation(v_tok[:, c, :], ps[:, 6 + c % 2, 0:AW], ACT.Copy).then_inc(vt_used, 1)
            act.wait_ge(z_used, 3 * T_GB)
            act.wait_ge(pv_done, NCH)
            act.activation(s_th, mixT[:, 2, :], ACT.Sigmoid).then_inc(gasig_done, 1)
            split_tile(14)
            act.wait_ge(vms_done, 1)
            act.activation(rstdv[:, :], ssv[:, :], ACT.Sqrt).then_inc(vroot_done, 1)
            act.wait_ge(vsum_done, 9)
            act.wait_ge(ga_done, 3)
            act.wait_ge(nsp_done, 1)
            decay(0)
            root_b(0)
            act.wait_ge(cache_read, NS)
            act.activation(sT_s, ps[:, 5, 0:64], ACT.Copy).then_inc(s1c_done, 1)
            split_tile(15)
            act.wait_ge(scan_done, 2)
            gate_sigmoids(1, 0)
            act.wait_ge(snegm_done, 1)
            act.wait_ge(kv_stored, 16)
            act.activation(p_s, ps[0:32, 5, 0:NM], ACT.Exp, bias=sst[:, 1:2], scale=HD ** -0.5,
                           accum_out=sst[:, 2:3]).then_inc(sp_exp, 1)
            gate_sigmoids(1, 1)
            gate_sigmoids(1, 2)
            place(0)
            split_tile(16)
            decay(1)
            act.wait_ge(s3_done, 1)
            act.activation(small_T[:, 1, :], ps[:, 5, 0:64], ACT.Copy).then_inc(s3c_done, 1)
            root_b(1)
            split_tile(17)
            for g in range(NG):
                act.wait_ge(z_used, 3 * (T_GB + g + 1))
                act.wait_ge(gbm_done, g)
                act.activation(s_sig, zT[:, 8 + g, :], ACT.Sigmoid).then_inc(gbsig_done, 1)
                act.wait_ge(scan_done, 4)
                gate_sigmoids(2, g)
            place(1)
            split_tile(18)
            decay(2)
            root_b(2)
            place(2)

            def split_o(c0, slot):
                act.activation(o_hi[:, slot, :].rearrange("p (k n) -> p k n", k=KT),
                               mixT[:, :, bass.ds(c0, P)], ACT.Copy).then_inc(ohi_done, 1)

            def y_stats(c, u):
                act.wait_ge(y_done, c + 1)
                if not isinstance(c, int) or c > 0:
                    act.wait_ge(ysq_done, c)
                act.activation(probs[:, 0:DM].rearrange("p (a b) -> p a b", a=2), ps[:, 3 * u:3 * u + 2, :],
                               ACT.Square, accum_out=sy[:, u:u + 1]).then_inc(ysq_done, 1)
                act.wait_ge(yms_done, c + 1)
                act.activation(ry[:, u:u + 1], sy[:, u:u + 1], ACT.Sqrt).then_inc(yroot_done, 1)

            act.wait_ge(z_done, 3 * (N_TILES - 1))
            act.wait_ge(c_done, NCH)
            act.wait_ge(b_done, 3)
            act.wait_ge(z_used, 3 * (N_TILES - 1) + 1)
            split_o(0, 1)
            for n, k in enumerate(K_ORDER):
                act.wait_ge(wo_in[n], 16)
                if n < KT - 1:
                    act.wait_ge(x_free, n + 1)
                else:
                    act.wait_ge(z_done, 3 * N_TILES)
                act.activation(wo_hi[:, k, 0:DM], wo_source(n), ACT.Copy).then_inc(wohi_done, 1)
            act.wait_ge(z_used, 3 * N_TILES)
            act.wait_ge(cs_done, 3)
            act.wait_ge(y_used, 1)
            act.activation(o_s[:, :, 0:NL], mixT[:, :, TT - NL:TT], ACT.Copy).then_inc(oshi_done, 1)
            split_o(P, 0)
            y_stats(0, 1)
            act.wait_ge(ys_done, 1)
            act.activation(probsT[0:NL, 0:DM].rearrange("p (a b) -> p a b", a=2), ps[NL:2 * NL, 6:8, :],
                           ACT.Copy).then_inc(yslo_done, 1)
            act.wait_ge(ysum_done, 1)
            act.wait_ge(ysq_done, 1)
            act.activation(probs[0:NL, 0:DM].rearrange("p (a b) -> p a b", a=2), y_s, ACT.Square,
                           accum_out=sy[0:NL, 2:3]).then_inc(yssq_done, 1)
            act.wait_ge(ysms_done, 1)
            act.wait_ge(yssq_done, 1)
            act.activation(sy[0:NL, 3:4], sy[0:NL, 2:3], ACT.Sqrt).then_inc(ysroot_done, 1)
            with act.Fori(0, 3) as i:
                for v in range(2):
                    act.wait_ge(y_done, i * 2 + (v + 1))
                    act.wait_ge(o_done, i * 2 + (v + 1))
                    split_o(i * (2 * P) + (v + 2) * P, 1 - v)
                    y_stats(i * 2 + (v + 1), v)
            for n in range(2):
                act.wait_ge(y_half, n + 1)
                act.activation(probs[:, n * 512:(n + 1) * 512], ps[:, n, :], ACT.Square,
                               accum_out=sl[:, n:n + 1]).then_inc(ysq_half, 1)
            act.wait_ge(yms_done, 8)
            act.activation(ry[:, 0:1], sl[:, 0:1], ACT.Sqrt).then_inc(yroot_done, 1)

        @block.gpsimd
        def _(pool):
            def low_w(m, slot):
                pool.wait_ge(whi_done, m + 1)
                pool.tensor_tensor(w_lo[:, slot, :], w_stage[:, slot, :], w_hi[:, slot, :].bitcast(F),
                                   ALU.subtract).then_inc(wlo_done, 1)

            pool.memset(ident[:, :], 0.0).then_inc(const_set, 1)
            pool.wait_ge(const_set, 1)
            pool.affine_select(out=ident[:, :], in_=ident[:, :], compare_op=ALU.not_equal, fill=1.0, base=0,
                               pattern=[[-1, P]], channel_multiplier=1).then_inc(const_set, 1)
            pool.memset(qb[:, :, :, :], 0.0).then_inc(const_set, 1)
            pool.memset(ones[:, :], 1.0).then_inc(const_set, 1)
            pool.wait_ge(wlo_done, 2)
            low_w(2, 0)
            for i in range(4):
                kk = slice(2 * i, 2 * i + 2)
                pool.wait_ge(mhi_done, 2 * i + 2)
                pool.tensor_tensor(w_mem_lo[:, kk, :], w_mem[:, kk, :], w_mem_hi[:, kk, :].bitcast(F),
                                   ALU.subtract).then_inc(wmlo_done, 1)
            low_w(3, 1)
            pool.wait_ge(wsT_in, 16)
            pool.affine_select(out=wsT[:, :, :], in_=wsT[:, :, :], compare_op=ALU.is_ge, fill=0.0, base=0,
                               pattern=[[0, AH], [1, P]], channel_multiplier=-1).then_inc(w_masked, 1)
            low_w(4, 0)
            pool.wait_ge(q_done, 2)
            with pool.Fori(0, 4) as i:
                for u in range(2):
                    m, s = i * 2 + (ATT0 + u), i * 2 + u
                    pool.wait_ge(qhi_done, s * 2 + 2)
                    pool.wait_ge(wlo_done, m + 1)
                    for hh in range(2):
                        r, to = slice(hh * HD, (hh + 1) * HD), slice((1 - hh) * HD, (2 - hh) * HD)
                        pool.tensor_tensor(q_st[to, u, hh, :, :], zT[r, 0:2, bass.ds(i * (2 * P) + u * P, P)],
                                           q_st[r, u, hh, :, :].bitcast(F), ALU.subtract).then_inc(qc_done, 1)
                        pool.wait_ge(qc_done, s * 2 + (hh + 1))
                    low_w(m + 1, 1 - u)

            def keep_xc(j):
                pool.wait_ge(gate_used, 6 * (j + 1))
                pool.tensor_tensor(s_i, s_i, mixT[:, 3 + j, :], ALU.mult).then_inc(ixc_done, 1)

            low_w(13, 1)
            low_w(14, 0)
            keep_xc(0)
            pool.wait_ge(rows_in, 16)
            for q, (c0, n) in enumerate(((0, 4), (4, 4), (8, 1))):
                pool.wait_ge(vr_done, q + 1)
                pool.tensor_tensor(v_tok[:, c0:c0 + n, :], v_tok[:, c0:c0 + n, :],
                                   rows[:, 0:AW].unsqueeze(1).broadcast_to([P, n, AW]), ALU.mult).then_inc(vn_done, 1)
            low_w(15, 1)
            for j in range(3):
                pool.wait_ge(ga_done, j + 1)
                pool.tensor_tensor(mixT[:, j, :], mixT[:, j, :], rstdB[:, :], ALU.mult).then_inc(gar_done, 1)
            low_w(16, 0)
            keep_xc(1)
            low_w(17, 1)
            low_w(18, 0)
            keep_xc(2)

            def low_o(c0, slot):
                pool.tensor_tensor(o_lo[:, slot, :].rearrange("p (k n) -> p k n", k=KT),
                                   mixT[:, :, bass.ds(c0, P)],
                                   o_hi[:, slot, :].bitcast(F).rearrange("p (k n) -> p k n", k=KT),
                                   ALU.subtract).then_inc(o_done, 1)

            def add_x(c, u, arrived):
                pool.wait_ge(y_used, c + 2)
                pool.wait_ge(x_in[u], arrived)
                pool.tensor_tensor(y_out[:, u, :], y_out[:, u, :], x_ring[:, u, 0:DM], ALU.add).then_inc(y_ready, 1)

            pool.wait_ge(ohi_done, 1)
            low_o(0, 1)
            pool.wait_ge(oshi_done, 1)
            pool.tensor_tensor(o_s[:, :, NL:2 * NL], mixT[:, :, TT - NL:TT], o_s[:, :, 0:NL].bitcast(F),
                               ALU.subtract).then_inc(os_done, 1)
            pool.wait_ge(ohi_done, 2)
            low_o(P, 0)
            add_x(0, 1, 16)
            with pool.Fori(0, 3) as i:
                for v in range(2):
                    pool.wait_ge(ohi_done, i * 2 + (v + 3))
                    low_o(i * (2 * P) + (v + 2) * P, 1 - v)
                    add_x(i * 2 + (v + 1), v, i * 16 + 16 * (1 + v))

        @block.vector
        def _(dve):
            own = Tally(dve, dve_own)

            def evac(m, g, dst):
                dve.wait_ge(z_done, m * 3 + (g + 1))
                dve.tensor_tensor(dst, ps[:, g, 0:GN], rstdB[:, g * GN:(g + 1) * GN], ALU.mult).then_inc(z_used, 1)

            def raw(m, g, dst):
                dve.wait_ge(z_done, m * 3 + (g + 1))
                dve.tensor_copy(dst, ps[:, 3 * m + g, 0:GN]).then_inc(z_used, 1)

            def grp(g):
                return slice(g * GN, (g + 1) * GN)

            dve.wait_ge(par_in, 16)
            own.link(dve.tensor_scalar(lt[:, 2, :], pc("lam", 0, 3), -1.0, None, ALU.mult))
            dve.tensor_tensor(lt[:, 0, :], pc("lam", 0, 3), lt[:, 2, :], ALU.max).then_inc(lam_done, 1)

            def low_w(m, cols):
                return dve.tensor_tensor(w_lo[:, m, cols], w_stage[:, m, cols], w_hi[:, m, cols].bitcast(F),
                                         ALU.subtract)

            dve.wait_ge(wfirsthi_done, 1)
            low_w(0, slice(0, WF)).then_inc(wfirstlo_done, 1)
            for k in range(KT):
                if k in (1, 2):
                    dve.wait_ge(whi_done, k)
                    low_w(k - 1, slice(WF, DM) if k == 1 else slice(0, DM)).then_inc(wlo_done, 1)
                dve.wait_ge(xhi_done, k + 1)
                dve.scalar_tensor_tensor(x_lo[:, k, :], mixT[:, k, :], pc("g_pre", k), x_hi[:, k, :].bitcast(F),
                                         ALU.mult, ALU.subtract).then_inc(xlo_done, 1)
            for k in range(1, KT):
                dve.wait_ge(xsq_done, k + 1)
                dve.tensor_tensor(probs[:, :], mixT[:, 0, :] if k == 1 else probs[:, :], mixT[:, k, :],
                                  ALU.add).then_inc(xsum_done, 1)
                if k == 3:
                    for g in range(NG):
                        raw(0, g, zT[:, 0, grp(g)])
                dve.wait_ge(xsum_done, k)
            for g in range(NG):
                raw(1, g, zT[:, 1, grp(g)])
            for i in range(4):
                kk = slice(2 * i, 2 * i + 2)
                dve.wait_ge(memT_in[i], 16)
                dve.tensor_tensor(memT[:, kk, :], memT[:, kk, :],
                                  pc("g_mem", 2 * i, 2).unsqueeze(2).broadcast_to([P, 2, NM]), ALU.mult).then_inc(memg_done, 1)
                dve.wait_ge(mhi_done, 2 * i + 1)
                dve.tensor_tensor(memT_lo[:, kk, :], memT[:, kk, :], memT_hi[:, kk, :].bitcast(F),
                                  ALU.subtract).then_inc(mlo_done, 1)
            for g in range(NG):
                dve.wait_ge(rstdp_done, g + 1)
                dve.tensor_scalar(rstdB[:, grp(g)], ps[:, 5 + g, 0:GN], 1.0 / DM, EPS, ALU.mult, ALU.add).then_inc(ms_done, 1)
            dve.wait_ge(act_own, 2)
            dve.tensor_scalar(ssq[:, :], ssq[:, :], 1.0 / DM, EPS, ALU.mult, ALU.add).then_inc(ms_done, 1)
            for n, t in enumerate((rstdB, rstd)):
                dve.wait_ge(root_done, n + 1)
                dve.reciprocal(t[:, :], t[:, :]).then_inc(rstdB_done, 1)
            dve.wait_ge(rstdB_done, 2)
            for g in range(NG):
                evac(2, g, mixT[:, 6, grp(g)])
            for tile in (zT[:, 0, :], zT[:, 1, :]):
                dve.tensor_tensor(tile, tile, rstdB[:, :], ALU.mult).then_inc(q_done, 1)
            dve.wait_ge(elam_done, 1)
            own.link(dve.tensor_scalar(lt[:, 3, :], lt[:, 1, :], 2.0, None, ALU.add))
            own.link(dve.reciprocal(lt[:, 4, :], lt[:, 3, :]))
            own.link(dve.tensor_tensor(lt[:, 3, :], lt[:, 4, :], lt[:, 1, :], ALU.mult))
            own.link(dve.tensor_tensor(lt[:, 4, :], lt[:, 3, :], lt[:, 3, :], ALU.mult))
            own.link(dve.tensor_scalar(lt[:, 5, :], lt[:, 4, :], 1.0 / 17, None, ALU.mult))
            for n in range(15, 2, -2):
                own.link(dve.scalar_tensor_tensor(lt[:, 5, :], lt[:, 5, :], 1.0 / n, lt[:, 4, :], ALU.add, ALU.mult))
            own.link(dve.scalar_tensor_tensor(lt[:, 5, :], lt[:, 5, :], 1.0, lt[:, 3, :], ALU.add, ALU.mult))
            own.link(dve.tensor_scalar(lt[:, 2, :], lt[:, 2, :], 0.0, -LRU_C, ALU.max, ALU.mult))
            own.link(dve.scalar_tensor_tensor(nsp[:, :], lt[:, 5, :], -2.0 * LRU_C, lt[:, 2, :], ALU.mult, ALU.add))
            dve.tensor_scalar(lt[:, 5, :], nsp[:, :], 2.0, None, ALU.mult).then_inc(nsp_done, 1)
            dve.wait_ge(vhi_done, 1)
            dve.tensor_tensor(v_hl[:, :, :, HD:2 * HD], kv[:, :, 256:512].rearrange("p m (h n) -> p m h n", h=NH),
                              v_hl[:, :, :, 0:HD].bitcast(F), ALU.subtract).then_inc(vlo_done, 1)
            dve.wait_ge(khi_done, 4)
            for hh in range(2):
                r = slice(hh * HD, (hh + 1) * HD)
                dve.tensor_tensor(k_lo[r, :, :], ps[r, 5, :].rearrange("p (t n) -> p t n", t=2),
                                  k_hh[r, hh, :, :].bitcast(F), ALU.subtract).then_inc(klo_done, 1)

            def gate_c(j):
                dve.wait_ge(gcsig_done, j + 1)
                dve.tensor_tensor(mixT[:, 6 + j, :], mixT[:, 6 + j, :], sig_c[j], ALU.mult)

            gate_c(0)
            for g in range(NG):
                evac(3, g, mixT[:, 7, grp(g)])
            dve.wait_ge(const_set, 3)
            dve.wait_ge(q_done, 2)
            for t in range(2):
                for hh in range(2):
                    r = slice(hh * HD, (hh + 1) * HD)
                    dve.tensor_copy(qb[r, t, :, 2 * t + hh], zT[r, t, NT:TT]).then_inc(qb_done, 1)

            def attend(m, s, c0, dst, between=(None,) * 3):
                for hh in range(2):
                    dve.wait_ge(sc_done, s * 2 + (hh + 1))
                    own.mark(dve.tensor_reduce(mx[:, 2 * hh:2 * hh + 2],
                                               ps[:, 3 + hh, :].rearrange("p (t n) -> p t n", t=2), AX.X, ALU.max))
                own.wait()
                dve.tensor_scalar(negm[:, :], mx[:, :], -HD ** -0.5, None, ALU.mult).then_inc(negm_done, 1)
                if between[0]:
                    between[0]()
                evac(m, 0, dst(0))
                for b in range(2):
                    half = slice(b * 512, (b + 1) * 512)
                    dve.wait_ge(pThi_done, s * 2 + (b + 1))
                    dve.tensor_tensor(probsT_lo[:, half], ps[:, 5 + b, :], probsT_hi[:, half].bitcast(F),
                                      ALU.subtract).then_inc(pTlo_done, 1)
                dve.wait_ge(p_done, s * 4 + 4)
                own.link(dve.reciprocal(rsum[:, :], sums[:, :]))
                if between[1]:
                    between[1]()
                evac(m, 1, dst(1))
                dve.wait_ge(pv_done, s + 1)
                by_head = attn[:, :].rearrange("p (h n) -> p h n", h=NH)
                both = ps[:, 7, :].rearrange("p (h n) -> p h n", h=NH)
                own.link(dve.tensor_copy(by_head, both[:, :, HD:2 * HD]))
                own.link(dve.tensor_tensor(by_head, both[:, :, 0:HD], by_head, ALU.add))
                dve.tensor_tensor(by_head, by_head, rsum[:, :].unsqueeze(2).broadcast_to([P, NH, HD]), ALU.mult).then_inc(attn_done, 1)
                if between[2]:
                    between[2]()
                evac(m, 2, dst(2))
                dve.wait_ge(attnT_done, s + 1)
                cols = mixT[:, 6:8, bass.ds(c0, P)]
                dve.tensor_tensor(cols, ps[:, 7, 0:256].rearrange("p (t n) -> p t n", t=2), cols,
                                  ALU.mult).then_inc(c_done, 1)

            def convolve(j):
                xb, xc = zT[:, 2 + j, :], mixT[:, 3 + j, :]

                def tap(back):
                    w = pc("w_conv", 4 * j + 3 - back)
                    own.mark(dve.scalar_tensor_tensor(xc[:, back:NT], xb[:, 0:NT - back], w, xc[:, back:NT],
                                                      ALU.mult, ALU.add))
                    return dve.scalar_tensor_tensor(xc[:, NT:TT], pc("st_conv", 24 * j + 8 * (3 - back), 8), w,
                                                    xc[:, NT:TT], ALU.mult, ALU.add)

                def first():
                    dve.wait_ge(z_used, 3 * (T_XB + j + 1))
                    own.link(dve.tensor_scalar(xc, xb, pc("w_conv", 4 * j + 3), pc("b_conv", j), ALU.mult, ALU.add))
                    own.mark(tap(1))

                def second():
                    own.wait()
                    own.mark(tap(2))

                def third():
                    own.wait()
                    tap(3).then_inc(conv_done, 1)

                return first, second, third

            attend(ATT0, 0, 0, lambda g: zT[:, 2, grp(g)], (lambda: gate_c(1), None, None))
            base, per = own.k, 5
            with dve.Fori(0, 2) as i:
                own.base, own.k = i * per + base, 0
                attend(i + (ATT0 + 1), i + 1, i * P + P,
                       lambda g: zf[:, bass.ds(i * TT + (3 * TT + g * GN), GN)])
                assert own.k == per
            own.base, own.k = base + 2 * per, 0
            for m in (7, 8, 9):
                attend(m, m - ATT0, (m - ATT0) * P, lambda g: zT[:, m - 2, grp(g)], convolve(m - 7))
            for m in (10, 11):
                attend(m, m - ATT0, (m - ATT0) * P, lambda g: mixT[:, m - 10, grp(g)])

            def gate_a(j):
                dve.wait_ge(gasig_done, j + 1)
                dve.tensor_tensor(mixT[:, j, :], mixT[:, j, :], (zT[:, 9, :], zT[:, 10, :], s_th)[j],
                                  ALU.mult).then_inc(ga_done, 1)

            def v_sums(c):
                dve.wait_ge(vsq_done, c + 1)
                dve.tensor_reduce(ssv[:, 4 * c:4 * c + 4], v_sq[:, c % 4, :].rearrange("p (h n) -> p h n", h=AH),
                                  AX.X, ALU.add).then_inc(vsum_done, 1)

            def rest(j):
                dve.wait_ge(decay_done, 3 * (j + 1))
                dve.scalar_tensor_tensor(s_th, s_a2, 1.0, s_th, ALU.add, ALU.mult).then_inc(rest_done, 1)

            def scan(j):
                dve.wait_ge(root_b_done, j + 1)
                dve.wait_ge(ixc_done, j + 1)
                own.link(dve.tensor_tensor(s_i, s_i, s_th, ALU.mult))
                dve.tensor_tensor_scan(s_th[:, 0:NT], s_r[:, 0:NT], s_i[:, 0:NT], 0.0, ALU.mult, ALU.add).then_inc(scan_done, 1)
                own.link(dve.tensor_tensor(s_th[:, NT:TT], s_r[:, NT:TT], pc("st_h", 8 * j, 8), ALU.mult))
                dve.tensor_tensor(s_th[:, NT:TT], s_th[:, NT:TT], s_i[:, NT:TT], ALU.add).then_inc(scan_done, 1)

            for g in range(NG):
                evac(12, g, mixT[:, 2, grp(g)])
                if g < 2:
                    gate_a(g)
                for c in range(3 * g, 3 * g + 3):
                    v_sums(c)
            dve.wait_ge(vsum_done, 9)
            dve.tensor_scalar(ssv[:, :], ssv[:, :], 1.0 / AD, EPS, ALU.mult, ALU.add).then_inc(vms_done, 1)
            gate_a(2)
            dve.wait_ge(vroot_done, 1)
            own.link(dve.reciprocal(rstdv[:, :], rstdv[:, :]))
            for q, (c0, n) in enumerate(((0, 4), (4, 4), (8, 1))):
                vv = v_tok[:, c0:c0 + n, :].rearrange("p c (h n) -> p (c h) n", h=AH)
                dve.tensor_tensor(vv, vv, rstdv[:, 16 * q:16 * q + 4 * n].unsqueeze(2).broadcast_to([P, 4 * n, AD]),
                                  ALU.mult).then_inc(vr_done, 1)
            evac(13, 0, zT[:, 8, grp(0)])
            rest(0)
            evac(13, 1, zT[:, 8, grp(1)])
            scan(0)
            evac(13, 2, zT[:, 8, grp(2)])
            for g in range(NG):
                evac(14, g, zT[:, 9, grp(g)])
                if g == 0:
                    dve.wait_ge(s2_done, 1)
                    own.link(dve.tensor_reduce(sst[:, 0:1], ps[0:32, 5, 0:NM], AX.X, ALU.max))
                    dve.tensor_scalar(sst[:, 1:2], sst[:, 0:1], -HD ** -0.5, None, ALU.mult).then_inc(snegm_done, 1)
                if g == 2:
                    dve.wait_ge(sp_exp, 1)
                    own.link(dve.reciprocal(sst[:, 3:4], sst[:, 2:3]))
                    dve.tensor_scalar(p_s, p_s, sst[:, 3:4], None, ALU.mult).then_inc(sp_norm, 1)
                for c in range(3 * g, 3 * g + 3):
                    vc = v_tok[:, c, :].rearrange("p (h n) -> p h n", h=AH)
                    if c < NCH:
                        dve.wait_ge(sp_done, c + 1)
                        dve.tensor_tensor(vc, ps[:, 6 + c % 2, 0:AW].rearrange("p (h n) -> p h n", h=AH),
                                          pc("b_s", 0, 4).unsqueeze(2).broadcast_to([P, AH, AD]), ALU.add).then_inc(mix_done, 1)
                    else:
                        dve.wait_ge(vn_done, 3)
                        dve.wait_ge(vs_stored, 16)
                        own.link(dve.tensor_tensor(vc, vc, rows[:, AW:AW + 4].unsqueeze(2).broadcast_to([P, AH, AD]), ALU.mult))
                        dve.tensor_tensor(vc, vc, rows[:, AW + 4:AW + 8].unsqueeze(2).broadcast_to([P, AH, AD]),
                                          ALU.add).then_inc(mix_done, 1)
            dve.wait_ge(gar_done, 3)
            for g in range(NG):
                evac(15, g, zT[:, 10, grp(g)])
                for c in range(3 * g, 3 * g + 3):
                    dve.wait_ge(mT_done, c + 1)
                    n, a = (P, 0) if c < NCH else (NS, P - NS)
                    dve.tensor_tensor(mixT[:, 0:3, c * P:c * P + n],
                                      ps[:, MIX_BANKS[c % 3], 0:AW].rearrange("p (j n) -> p j n", j=3)[:, :, a:a + n],
                                      mixT[:, 0:3, c * P:c * P + n], ALU.mult).then_inc(a_done, 1)
            rest(1)
            scan(1)

            def times_u(m, g):
                out = mixT[:, m - T_U, grp(g)]
                dve.wait_ge(z_done, 3 * m + g + 1)
                dve.tensor_tensor(out, ps[:, g, 0:GN], out, ALU.mult).then_inc(z_used, 1)

            dve.wait_ge(a_done, 9)

            def close_b(j):
                dve.wait_ge(placed, 2 * (j + 1))
                dve.wait_ge(gbm_done, j + 1)
                dve.tensor_tensor(mixT[:, 3 + j, :], mixT[:, 3 + j, :], zT[:, 8 + j, :], ALU.mult).then_inc(b_done, 1)

            for g in range(NG):
                times_u(16, g)
                dve.wait_ge(gbsig_done, g + 1)
                dve.tensor_tensor(zT[:, 8 + g, :], zT[:, 8 + g, :], s_sig, ALU.mult).then_inc(gbm_done, 1)
            times_u(17, 0)
            close_b(0)
            rest(2)
            times_u(17, 1)
            close_b(1)
            times_u(17, 2)
            scan(2)
            close_b(2)
            def low_wo(n):
                k = K_ORDER[n]
                dve.wait_ge(wohi_done, n + 1)
                dve.tensor_tensor(wo_lo[:, k, 0:DM], wo_source(n), wo_hi[:, k, 0:DM].bitcast(F),
                                  ALU.subtract).then_inc(wo_done, 1)

            times_u(18, 0)
            times_u(18, 1)
            low_wo(0)
            low_wo(1)
            times_u(18, 2)
            dve.wait_ge(cache_read, 2 * NS)
            for t in range(2):
                for hh in range(2):
                    r = slice(hh * HD, (hh + 1) * HD)
                    got = ps[r, 7, t * 32:(t + 1) * 32].rearrange("p (n h) -> p n h", h=NH)[:, :, 2 * t + hh]
                    dve.tensor_tensor(mixT[r, 6 + t, NT:TT], got, mixT[r, 6 + t, NT:TT],
                                      ALU.mult).then_inc(cs_done if t + hh < 2 else y_used, 1)
            for n in range(2, KT):
                low_wo(n)
            dve.wait_ge(gpost_in, 16)

            def finish(c, u, stored):
                dve.wait_ge(ysq_done, c + 1)
                dve.tensor_scalar(sy[:, u:u + 1], sy[:, u:u + 1], 1.0 / DM, EPS, ALU.mult, ALU.add).then_inc(yms_done, 1)
                dve.wait_ge(yroot_done, c + 1)
                own.link(dve.reciprocal(ry[:, u:u + 1], ry[:, u:u + 1]))
                if stored is not None:
                    dve.wait_ge(y_stored[u], stored)
                dve.scalar_tensor_tensor(y_out[:, u, :].rearrange("p (a b) -> p a b", a=2), ps[:, 3 * u:3 * u + 2, :],
                                         ry[:, u:u + 1], g_post.rearrange("p (a b) -> p a b", a=2),
                                         ALU.mult, ALU.mult).then_inc(y_used, 1)

            finish(0, 1, None)
            dve.wait_ge(yslo_done, 1)
            dve.tensor_tensor(y_s, ps[0:NL, 6:8, :], probsT[0:NL, 0:DM].rearrange("p (a b) -> p a b", a=2),
                              ALU.add).then_inc(ysum_done, 1)
            dve.wait_ge(yssq_done, 1)
            dve.tensor_scalar(sy[0:NL, 2:3], sy[0:NL, 2:3], 1.0 / DM, EPS, ALU.mult, ALU.add).then_inc(ysms_done, 1)
            dve.wait_ge(ysroot_done, 1)
            own.link(dve.reciprocal(sy[0:NL, 3:4], sy[0:NL, 3:4]))
            own.link(dve.scalar_tensor_tensor(y_s, y_s, sy[0:NL, 3:4], g_post[0:NL].rearrange("p (a b) -> p a b", a=2),
                                              ALU.mult, ALU.mult))
            dve.wait_ge(xs_in, 16)
            dve.tensor_tensor(y_s, y_s, x_s.rearrange("p (a b) -> p a b", a=2), ALU.add).then_inc(ys_ready, 1)
            finish(1, 0, None)
            finish(2, 1, 16)
            base = own.base + own.k
            with dve.Fori(0, 2) as i:
                for v in range(2):
                    own.base, own.k = i * 2 + (base + v), 0
                    finish(i * 2 + (3 + v), v, i * 16 + (16 + 16 * v))
            own.base, own.k = base + 4, 0
            dve.wait_ge(y_stored[0], 16 * 3)
            dve.wait_ge(x_in[0], 16 * 4)
            halves = [slice(n * 512, (n + 1) * 512) for n in range(2)]
            for n in range(2):
                dve.wait_ge(ysq_half, n + 1)
                if n == 1:
                    own.link(dve.tensor_tensor(sl[:, 0:1], sl[:, 0:1], sl[:, 1:2], ALU.add))
                    dve.tensor_scalar(sl[:, 0:1], sl[:, 0:1], 1.0 / DM, EPS, ALU.mult, ALU.add).then_inc(yms_done, 1)
                dve.tensor_tensor(y_out[:, 0, halves[n]], ps[:, n, :], g_post[:, halves[n]], ALU.mult).then_inc(yg_half, 1)
            dve.wait_ge(yroot_done, 8)
            own.link(dve.reciprocal(ry[:, 0:1], ry[:, 0:1]))
            dve.wait_ge(yg_half, 2)
            for n in range(2):
                dve.scalar_tensor_tensor(y_out[:, 0, halves[n]], y_out[:, 0, halves[n]], ry[:, 0:1],
                                         x_ring[:, 0, halves[n]], ALU.mult, ALU.add).then_inc(y_last, 1)


_OUTS = {"o_y": [TT, DM], "o_kv": [P, MT, 512], "o_conv": [P, 3, 3 + NS], "o_st": [P, 72],
         "o_h": [P, 3, 1 + NS], "o_vs": [NS, AW]}


def kernel(**inputs):
    import concourse.bacc as bacc
    from concourse.bass_utils import run_bass_kernel_spmd

    a = {k: np.asarray(v) for k, v in inputs.items()}

    def tiles(w):
        return w.reshape(-1, P, w.shape[-1]).transpose(1, 0, 2)

    def per_part(v):
        return v.reshape(-1, P).T

    x_all = np.concatenate([a["x_prompt"][0], a["x_sample"][:, 0]], axis=0)
    w_in = a["w_in"][0]
    cuts = {"u": 0, "v": AW, "ga": 2 * AW, "xb": 3 * AW, "gb": 4 * AW, "q": 5 * AW, "gc": 5 * AW + 256}
    order = [("q", 2), ("gc", 2), ("xb", 3), ("v", 3), ("ga", 3), ("gb", 3), ("u", 3)]
    cols = np.concatenate([w_in[:, cuts[n]:cuts[n] + P * t] for n, t in order], axis=1)
    w_tiles = cols.reshape(KT, P, N_TILES, P).transpose(2, 1, 0, 3).reshape(N_TILES, P, DM)
    st = a["state_conv"][0].transpose(2, 1, 0).reshape(3, P, 3, NS).transpose(1, 0, 2, 3).reshape(P, 72)
    sh = a["state_h"][0].T.reshape(3, P, NS).transpose(1, 0, 2).reshape(P, 24)
    wc = a["w_conv"][0].T.reshape(3, P, 4).transpose(1, 0, 2).reshape(P, 12)
    par = np.concatenate([per_part(a["g_pre"][0]), per_part(a["g_mem"][0]), wc, per_part(a["b_conv"][0]),
                          per_part(a["b_a"][0]), per_part(a["b_x"][0]), per_part(a["lru_lambda"][0]),
                          st, sh, a["b_s"][0].T], axis=1)
    gate_w = np.zeros((P, 2, len(GATE_PAIRS), P), np.float32)
    for n, name in enumerate(("w_a", "w_x")):
        full = np.zeros((AW, AW), np.float32)
        for b in range(8):
            full[48 * b:48 * b + 48, 48 * b:48 * b + 48] = a[name][0, b]
        for x, (kin, out) in enumerate(GATE_PAIRS):
            gate_w[:, n, x] = full[kin * P:(kin + 1) * P, out * P:(out + 1) * P]
    arrays = {
        "par": par,
        "memT": tiles(a["mem_prompt"][0].T),
        "w_mem": tiles(np.concatenate([a["w_mk"][0], a["w_mv"][0]], axis=1)),
        "w_tiles": w_tiles,
        "xT": tiles(x_all.T),
        "mem_nat": tiles(a["mem_prompt"][0]),
        "x_all": x_all,
        "rows": np.concatenate([a["g_v"][0], a["w_s"][0, :, 0, 0], a["b_s"][0, :, 0]]),
        "wsT": a["w_s"][0].transpose(2, 0, 1),
        "gate_w": gate_w,
        "kcT": a["cache_mem_k"][0].reshape(NS, NM, 2, P).transpose(0, 3, 2, 1).reshape(NS, P, 512),
        "vc": a["cache_mem_v"][0].reshape(NS, MT, P, 256).transpose(0, 2, 1, 3).reshape(NS, P, 512),
        "w_out": a["w_out"][0].reshape(KT, P, DM),
        "g_post": a["g_post"][0],
    }
    nc = bacc.Bacc("TRN2", target_bir_lowering=False, num_devices=1)
    d, feed = {}, {}
    for name, v in arrays.items():
        v = np.ascontiguousarray(v)
        feed["in_" + name] = v
        d[name] = nc.dram_tensor("in_" + name, list(v.shape), F, kind="ExternalInput").ap()
    for name, shape in _OUTS.items():
        d[name] = nc.dram_tensor(name, shape, F, kind="ExternalOutput").ap()
    build(nc, d)
    r = run_bass_kernel_spmd(nc, [feed], core_ids=[0]).results[0]
    y, kvo = r["o_y"], r["o_kv"].transpose(1, 0, 2).reshape(NM, 512)
    cv = r["o_conv"].transpose(1, 0, 2).reshape(AW, 3 + NS)
    stp = r["o_st"].reshape(P, 3, 3, NS).transpose(3, 2, 1, 0).reshape(NS, 3, AW)
    hh = r["o_h"].transpose(1, 0, 2).reshape(AW, 1 + NS)
    new_conv_s = np.concatenate([stp[:, 1:], cv[:, 3:].T[:, None]], axis=1)
    return (y[:NT][None], y[NT:][:, None],
            kvo[:, :256].reshape(1, 1, NM, NH, HD), kvo[:, 256:].reshape(1, 1, NM, NH, HD),
            np.ascontiguousarray(cv[:, :3].T)[None, None], np.ascontiguousarray(hh[:, 0])[None, None],
            new_conv_s[None], np.ascontiguousarray(hh[:, 1:].T)[None], r["o_vs"][None, :, None])
```
